# Optimizing a Trainium2 kernel written in Bass

```python
import jax, jax.numpy as jnp
from jax import lax
import numpy as np
import math

D_MODEL = 1024
BATCH = 1
SEQ = 512
DEPTH = 1

D_MIX = D_MODEL
C_CONV = D_MIX // 2
C_POOL = D_MIX - C_CONV
CONV_HEADS = 8
CONV_WIDTH = 31
POOL_WINDOWS = (2, 4, 8, 16)
N_POOL_GROUPS = len(POOL_WINDOWS)
POOL_GROUP = C_POOL // N_POOL_GROUPS
D_IN = 2 * C_CONV + C_POOL
D_FF = ((8 * D_MODEL // 3 + 255) // 256) * 256
RMS_EPS = 1e-6
LN_EPS = 1e-5


def rmsnorm(x, g):
    xf = x.astype(jnp.float32)
    y = xf * lax.rsqrt(jnp.mean(xf * xf, axis=-1, keepdims=True) + RMS_EPS)
    return (y * g.astype(jnp.float32)).astype(x.dtype)

def layernorm(x, g, b):
    xf = x.astype(jnp.float32)
    mu = jnp.mean(xf, axis=-1, keepdims=True)
    var = jnp.mean(jnp.square(xf - mu), axis=-1, keepdims=True)
    y = (xf - mu) * lax.rsqrt(var + LN_EPS)
    return (y * g.astype(jnp.float32) + b.astype(jnp.float32)).astype(x.dtype)

def conformer_conv_group(a, gate, w_dw, b_dw, ln_g, ln_b):
    u = a * jax.nn.sigmoid(gate)
    k = w_dw.astype(u.dtype)[:, None, :]
    v = lax.conv_general_dilated(
        u, k, window_strides=(1,), padding=[(CONV_WIDTH - 1, 0)],
        dimension_numbers=("NWC", "WIO", "NWC"),
        feature_group_count=C_CONV) + b_dw.astype(u.dtype)
    v = layernorm(v, ln_g, ln_b)
    return jax.nn.silu(v)

def multiscale_pool_group(p, w_pool, s_pool):
    seq = p.shape[1]
    pos = jnp.arange(seq)
    outs = []
    for i, w in enumerate(POOL_WINDOWS):
        seg = p[..., i * POOL_GROUP:(i + 1) * POOL_GROUP].astype(jnp.float32)
        cs = jnp.cumsum(seg, axis=1)
        lag = jnp.pad(cs, ((0, 0), (w, 0), (0, 0)))[:, :seq]
        cnt = jnp.minimum(pos + 1, w).astype(jnp.float32)[None, :, None]
        y = ((cs - lag) / cnt - seg).astype(p.dtype)
        outs.append(jnp.einsum("bsg,gh->bsh", y, w_pool[i]))
    return jnp.concatenate(outs, axis=-1) * s_pool

def swiglu(x, w_gate, w_up, w_down):
    return (jax.nn.silu(x @ w_gate) * (x @ w_up)) @ w_down

def first_inputs(seed: int = 0) -> dict:
    key = jax.random.key(seed)
    ks = jax.random.split(key, 20)
    f = jnp.float32
    n = lambda k, s, sc: jax.random.normal(k, s, f) * sc
    return {
        "x": jax.random.normal(ks[0], (BATCH, SEQ, D_MODEL), f),
        "g_mix": 1.0 + n(ks[1], (DEPTH, D_MODEL), 0.05),
        "w_in": n(ks[2], (DEPTH, D_MODEL, D_IN), D_MODEL ** -0.5),
        "b_in": n(ks[3], (DEPTH, D_IN), 0.02),
        "w_dw": n(ks[4], (DEPTH, CONV_WIDTH, C_CONV), CONV_WIDTH ** -0.5),
        "b_dw": n(ks[5], (DEPTH, C_CONV), 0.02),
        "ln_g": 1.0 + n(ks[6], (DEPTH, C_CONV), 0.05),
        "ln_b": n(ks[7], (DEPTH, C_CONV), 0.02),
        "w_pool": n(ks[8], (DEPTH, N_POOL_GROUPS, POOL_GROUP, POOL_GROUP), POOL_GROUP ** -0.5),
        "s_pool": 1.0 + n(ks[9], (DEPTH, C_POOL), 0.1),
        "w_out": n(ks[10], (DEPTH, D_MIX, D_MODEL), D_MIX ** -0.5),
        "g_ffn": 1.0 + n(ks[11], (DEPTH, D_MODEL), 0.05),
        "w_gate": n(ks[12], (DEPTH, D_MODEL, D_FF), D_MODEL ** -0.5),
        "w_up": n(ks[13], (DEPTH, D_MODEL, D_FF), D_MODEL ** -0.5),
        "w_down": n(ks[14], (DEPTH, D_FF, D_MODEL), D_FF ** -0.5),
        "g_final": 1.0 + n(ks[15], (D_MODEL,), 0.05),
    }

def first_block(x, g_mix, w_in, b_in, w_dw, b_dw, ln_g, ln_b, w_pool, s_pool,
              w_out, g_ffn, w_gate, w_up, w_down, g_final):
    h = x
    for l in range(DEPTH):
        xn = rmsnorm(h, g_mix[l])
        z = xn @ w_in[l] + b_in[l]
        a = z[..., :C_CONV]
        gate = z[..., C_CONV:2 * C_CONV]
        p = z[..., 2 * C_CONV:]
        y_conv = conformer_conv_group(a, gate, w_dw[l], b_dw[l], ln_g[l], ln_b[l])
        y_pool = multiscale_pool_group(p, w_pool[l], s_pool[l])
        y = jnp.concatenate([y_conv, y_pool], axis=-1)
        h = h + y @ w_out[l]
        h = h + swiglu(rmsnorm(h, g_ffn[l]), w_gate[l], w_up[l], w_down[l])
    return rmsnorm(h, g_final)


DEPTH_2 = 2

CHUNK = 64
Q_BLOCK = 128
N_A_LAYERS = DEPTH_2 // 2
N_B_LAYERS = DEPTH_2 - N_A_LAYERS
HEAD_DIM = 64
FOX_HEADS = D_MODEL // HEAD_DIM
DIFF_HEADS = D_MODEL // (2 * HEAD_DIM)
DIFF_V_DIM = 2 * HEAD_DIM
D_FF_2 = 2816
CONV_WIDTH_2 = 3
ROPE_THETA = 10000.0
RMS_EPS_2 = 1e-5
DN_ALPHA = (2 * DEPTH_2) ** 0.25
DN_BETA = (8 * DEPTH_2) ** -0.25


def _layer_norm(x, g, b):
    xf = x.astype(jnp.float32)
    mu = jnp.mean(xf, axis=-1, keepdims=True)
    var = jnp.mean(jnp.square(xf - mu), axis=-1, keepdims=True)
    y = (xf - mu) * lax.rsqrt(var + LN_EPS)
    return (y * g.astype(jnp.float32) + b.astype(jnp.float32)).astype(x.dtype)

def _rope_tables(seq_len):
    inv_freq = 1.0 / (ROPE_THETA ** (jnp.arange(0, HEAD_DIM, 2, dtype=jnp.float32) / HEAD_DIM))
    ang = jnp.arange(seq_len, dtype=jnp.float32)[:, None] * inv_freq[None, :]
    return jnp.cos(ang), jnp.sin(ang)

def _apply_rope(t, cos, sin):
    half = t.shape[-1] // 2
    t1, t2 = t[..., :half], t[..., half:]
    c = cos.astype(t.dtype)
    s = sin.astype(t.dtype)
    return jnp.concatenate([t1 * c - t2 * s, t2 * c + t1 * s], axis=-1)

def _heads(t, n_heads, d):
    b, s, _ = t.shape
    return t.reshape(b, s, n_heads, d).transpose(0, 2, 1, 3)

def _merge_blocks(o):
    nb, b, h, qb, dv = o.shape
    return o.transpose(1, 0, 3, 2, 4).reshape(b, nb * qb, h * dv)

def _fox_attention(x, w_in, b_f, w_out):
    b, s, d = x.shape
    proj = x @ w_in
    q = _heads(proj[..., :d], FOX_HEADS, HEAD_DIM)
    k = _heads(proj[..., d:2 * d], FOX_HEADS, HEAD_DIM)
    v = _heads(proj[..., 2 * d:3 * d], FOX_HEADS, HEAD_DIM)
    f_logit = proj[..., 3 * d:].astype(jnp.float32) + b_f.astype(jnp.float32)
    c = jnp.cumsum(jax.nn.log_sigmoid(f_logit), axis=1).transpose(0, 2, 1)
    scale = HEAD_DIM ** -0.5
    kpos = jnp.arange(s)

    def block(i):
        start = i * Q_BLOCK
        qb = lax.dynamic_slice_in_dim(q, start, Q_BLOCK, axis=2)
        cb = lax.dynamic_slice_in_dim(c, start, Q_BLOCK, axis=2)
        logits = jnp.einsum('bhqd,bhkd->bhqk', qb, k).astype(jnp.float32) * scale
        logits = logits + cb[..., :, None] - c[..., None, :]
        qpos = start + jnp.arange(Q_BLOCK)
        mask = kpos[None, :] <= qpos[:, None]
        p = jax.nn.softmax(jnp.where(mask, logits, -jnp.inf), axis=-1).astype(v.dtype)
        return jnp.einsum('bhqk,bhkd->bhqd', p, v)

    o = lax.map(block, jnp.arange(s // Q_BLOCK))
    return _merge_blocks(o) @ w_out

def _shared_kv(x, w_kv, cos, sin):
    b, s, _ = x.shape
    kw = 2 * DIFF_HEADS * HEAD_DIM
    proj = x @ w_kv
    k = proj[..., :kw].reshape(b, s, 2, DIFF_HEADS, HEAD_DIM).transpose(2, 0, 3, 1, 4)
    k1 = _apply_rope(k[0], cos, sin)
    k2 = _apply_rope(k[1], cos, sin)
    v = _heads(proj[..., kw:], DIFF_HEADS, DIFF_V_DIM)
    return k1, k2, v

def _diff_attention(x, k1, k2, v, w_q, lam_p, subln_g, w_out, lambda_init, cos, sin):
    b, s, _ = x.shape
    qp = (x @ w_q).reshape(b, s, 2, DIFF_HEADS, HEAD_DIM).transpose(2, 0, 3, 1, 4)
    q1 = _apply_rope(qp[0], cos, sin)
    q2 = _apply_rope(qp[1], cos, sin)
    lp = lam_p.astype(jnp.float32)
    lam = jnp.exp(jnp.sum(lp[0] * lp[1])) - jnp.exp(jnp.sum(lp[2] * lp[3])) + lambda_init
    scale = HEAD_DIM ** -0.5
    kpos = jnp.arange(s)

    def block(i):
        start = i * Q_BLOCK
        qb1 = lax.dynamic_slice_in_dim(q1, start, Q_BLOCK, axis=2)
        qb2 = lax.dynamic_slice_in_dim(q2, start, Q_BLOCK, axis=2)
        qpos = start + jnp.arange(Q_BLOCK)
        mask = kpos[None, :] < ((qpos // CHUNK) + 1)[:, None] * CHUNK
        s1 = jnp.einsum('bhqd,bhkd->bhqk', qb1, k1).astype(jnp.float32) * scale
        s2 = jnp.einsum('bhqd,bhkd->bhqk', qb2, k2).astype(jnp.float32) * scale
        p1 = jax.nn.softmax(jnp.where(mask, s1, -jnp.inf), axis=-1)
        p2 = jax.nn.softmax(jnp.where(mask, s2, -jnp.inf), axis=-1)
        a = (p1 - lam * p2).astype(v.dtype)
        return jnp.einsum('bhqk,bhkd->bhqd', a, v)

    o = lax.map(block, jnp.arange(s // Q_BLOCK)).astype(jnp.float32)
    o = o * lax.rsqrt(jnp.mean(jnp.square(o), axis=-1, keepdims=True) + RMS_EPS_2)
    o = (o * subln_g.astype(jnp.float32) * (1.0 - lambda_init)).astype(x.dtype)
    return _merge_blocks(o) @ w_out

def _conv_ffn(x, w_in, conv_w, conv_b, w_out):
    s = x.shape[1]
    u = x @ w_in
    up = jnp.pad(u, ((0, 0), (CONV_WIDTH_2 - 1, 0), (0, 0)))
    u = sum(conv_w[j] * up[:, j:j + s] for j in range(CONV_WIDTH_2)) + conv_b
    g, val = u[..., :D_FF_2], u[..., D_FF_2:]
    return (jax.nn.silu(g) * val) @ w_out

def second_inputs(seed: int = 0) -> dict:
    key = jax.random.key(seed)
    ks = jax.random.split(key, 20)
    d = D_MODEL
    f32 = jnp.float32
    nrm = lambda k, shape, sc: jax.random.normal(k, shape, f32) * sc
    return {
        'x': jax.random.normal(ks[0], (BATCH, SEQ, d), f32),
        'a_w_in': nrm(ks[1], (N_A_LAYERS, d, 3 * d + FOX_HEADS), d ** -0.5),
        'a_b_f': jax.random.uniform(ks[2], (N_A_LAYERS, FOX_HEADS), f32, 1.0, 6.0),
        'a_w_out': nrm(ks[3], (N_A_LAYERS, d, d), DN_BETA * d ** -0.5),
        'kv_w': nrm(ks[4], (d, 2 * DIFF_HEADS * HEAD_DIM + DIFF_HEADS * DIFF_V_DIM), d ** -0.5),
        'b_w_q': nrm(ks[5], (N_B_LAYERS, d, 2 * DIFF_HEADS * HEAD_DIM), d ** -0.5),
        'b_lambda': nrm(ks[6], (N_B_LAYERS, 4, HEAD_DIM), 0.1),
        'b_subln_g': 1.0 + nrm(ks[7], (N_B_LAYERS, DIFF_V_DIM), 0.02),
        'b_w_out': nrm(ks[8], (N_B_LAYERS, DIFF_HEADS * DIFF_V_DIM, d), DN_BETA * d ** -0.5),
        'ffn_w_in': nrm(ks[9], (DEPTH_2, d, 2 * D_FF_2), d ** -0.5),
        'ffn_conv_w': nrm(ks[10], (DEPTH_2, CONV_WIDTH_2, 2 * D_FF_2), CONV_WIDTH_2 ** -0.5),
        'ffn_conv_b': nrm(ks[11], (DEPTH_2, 2 * D_FF_2), 0.02),
        'ffn_w_out': nrm(ks[12], (DEPTH_2, D_FF_2, d), DN_BETA * D_FF_2 ** -0.5),
        'ln_attn_g': 1.0 + nrm(ks[13], (DEPTH_2, d), 0.02),
        'ln_attn_b': nrm(ks[14], (DEPTH_2, d), 0.02),
        'ln_ffn_g': 1.0 + nrm(ks[15], (DEPTH_2, d), 0.02),
        'ln_ffn_b': nrm(ks[16], (DEPTH_2, d), 0.02),
    }

def second_block(x, a_w_in, a_b_f, a_w_out, kv_w, b_w_q, b_lambda, b_subln_g, b_w_out,
              ffn_w_in, ffn_conv_w, ffn_conv_b, ffn_w_out,
              ln_attn_g, ln_attn_b, ln_ffn_g, ln_ffn_b):
    cos, sin = _rope_tables(x.shape[1])
    k1 = k2 = v = None
    for layer in range(DEPTH_2):
        if layer < N_A_LAYERS:
            h = _fox_attention(x, a_w_in[layer], a_b_f[layer], a_w_out[layer])
        else:
            j = layer - N_A_LAYERS
            lambda_init = 0.8 - 0.6 * math.exp(-0.3 * layer)
            h = _diff_attention(x, k1, k2, v, b_w_q[j], b_lambda[j], b_subln_g[j], b_w_out[j],
                                lambda_init, cos, sin)
        x = _layer_norm(DN_ALPHA * x + h, ln_attn_g[layer], ln_attn_b[layer])
        f = _conv_ffn(x, ffn_w_in[layer], ffn_conv_w[layer], ffn_conv_b[layer], ffn_w_out[layer])
        x = _layer_norm(DN_ALPHA * x + f, ln_ffn_g[layer], ln_ffn_b[layer])
        if layer == N_A_LAYERS - 1:
            k1, k2, v = _shared_kv(x, kv_w, cos, sin)
    return x


def setup_inputs(seed=0):
    out = dict(first_inputs(seed))
    for name, value in second_inputs(seed + 1).items():
        if name != "x":
            out[name + "_2"] = value
    return out


def reference(
    x, g_mix, w_in, b_in, w_dw, b_dw, ln_g, ln_b, w_pool, s_pool, w_out, g_ffn, w_gate, w_up,
    w_down, g_final, a_w_in_2, a_b_f_2, a_w_out_2, kv_w_2, b_w_q_2, b_lambda_2, b_subln_g_2,
    b_w_out_2, ffn_w_in_2, ffn_conv_w_2, ffn_conv_b_2, ffn_w_out_2, ln_attn_g_2, ln_attn_b_2,
    ln_ffn_g_2, ln_ffn_b_2,
):
    x = first_block(
        x, g_mix, w_in, b_in, w_dw, b_dw, ln_g, ln_b, w_pool, s_pool, w_out, g_ffn, w_gate,
        w_up, w_down, g_final,
    )
    return second_block(
        x, a_w_in_2, a_b_f_2, a_w_out_2, kv_w_2, b_w_q_2, b_lambda_2, b_subln_g_2, b_w_out_2,
        ffn_w_in_2, ffn_conv_w_2, ffn_conv_b_2, ffn_w_out_2, ln_attn_g_2, ln_attn_b_2,
        ln_ffn_g_2, ln_ffn_b_2,
    )


_drawn_inputs = setup_inputs


def setup_inputs(seed=0):
    import zlib

    import numpy as np

    out = dict(_drawn_inputs(seed))
    spreads = {}
    factors = {'b_in': 5.846, 'ln_b': 5.491, 'b_subln_g_2': 8.0, 'ffn_conv_b_2': 6.331}
    for name, (base, spread) in spreads.items():
        noise = np.random.default_rng([zlib.crc32(name.encode()), seed]).standard_normal(out[name].shape)
        drawn = base * np.exp(spread * noise) if base else spread * noise
        out[name] = __import__('jax').numpy.asarray(drawn.astype(out[name].dtype))
    for name, factor in factors.items():
        out[name] = (out[name] * factor).astype(out[name].dtype)
    return out
```

```python
from contextlib import ExitStack, contextmanager

import numpy as np
import concourse.bass as bass
from concourse import mybir

P = 128
S = 512
D = 1024
DT = D // P
QT = S // P
C_CONV = 512
CT = C_CONV // P
TAPS = 31
WINDOWS = (2, 4, 8, 16)
PAD = 16
D_FF = 2816
FT = D_FF // P
FF_TAPS = 3
HEAD = 64
FOX_HEADS = D // HEAD
DIFF_HEADS = D // (2 * HEAD)
CHUNK = 64
RMS_EPS, LN_EPS, SUB_EPS = 1e-6, 1e-5, 1e-5
ALPHA = 4.0 ** 0.25
LAMBDA_INIT = 0.8 - 0.6 * float(np.exp(-0.3))
MASKED = -1.0e30
DOWN = (6, 6, 5, 5)
assert sum(DOWN) == FT

F32 = mybir.dt.float32
F32R = mybir.dt.float32r
BF16 = mybir.dt.bfloat16
ALU = mybir.AluOpType
ACT = mybir.ActivationFunctionType
AX_X = mybir.AxisListType.X

OPEN = 1
RAW = 4
SPLIT = 2

STAGES = {}
_item, _turn = 0, DT
for _name, _n, _t in (("in", 12, 12), ("out", 8, 8), ("gu0", 2 * FT, 2 * FT), ("down0", 8 * len(DOWN), 8),
                      ("qkv1", 24, 24), ("out1", 8, 8), ("gu1", 2 * FT, 2 * FT), ("down1", 8 * len(DOWN), 8),
                      ("qkv2", 24, 24), ("subln", 0, DIFF_HEADS), ("out2", 8, 8),
                      ("gu2", 2 * FT, 2 * FT), ("down2", 8 * len(DOWN), 8), ("back", 0, 8)):
    STAGES[_name] = (_item, _turn)
    _item, _turn = _item + _n, _turn + _t
ITEMS = _item

ROWS0 = {}
_row = 0
for _name, _n in (("g_mix", 8), ("b_in", 12), ("b_dw", 4), ("ln_g", 4), ("ln_b", 4), ("s_pool", 4),
                  ("g_ffn", 8), ("g_final", 8), ("ln_attn_g_2", 16), ("ln_attn_b_2", 16),
                  ("ln_ffn_g_2", 16), ("ln_ffn_b_2", 16), ("b_subln_g_2", 1)):
    ROWS0[_name] = (_row, _n)
    _row += _n
ROWS_OF = [_row, TAPS * CT, 2 * 44, 2 * 44, 2 * 44, 2 * 44]


class Nth:

    def __init__(self, base, it=0, per=0):
        if isinstance(it, int):
            base, it, per = base + it * per, 0, 0
        self.base, self.it, self.per = base, it, per

    def __add__(self, k):
        return Nth(self.base + k, self.it, self.per)

    def n(self, k=0):
        return self.base + k if isinstance(self.it, int) else self.it * self.per + (self.base + k)

    def slot(self, size):
        assert self.per % size == 0
        return self.base % size

    def round(self, size, k=0):
        if isinstance(self.it, int):
            return self.base // size + k
        assert self.per % size == 0
        return self.it * (self.per // size) + (self.base // size + k)


class Chain:

    def __init__(self, eng, sem):
        self.eng, self.sem, self.count, self.it, self.per = eng, sem, 0, None, 0

    def did(self, ins):
        ins.then_inc(self.sem, 1)
        self.count += 1

    def sync(self):
        if self.it is None:
            self.eng.wait_ge(self.sem, self.count)
        else:
            self.eng.wait_ge(self.sem, self.it * self.per + self.count)

    def link(self, ins):
        self.did(ins)
        self.sync()

    @contextmanager
    def loop(self, times, per):
        start = self.count
        with self.eng.Fori(0, times) as it:
            self.it, self.per = it, per
            yield it
            assert self.count - start == per, (self.count - start, per)
        self.count, self.it = start + per * times, None


def two_blocks(nc, A, out):
    ctx = ExitStack()
    with ctx:
        def sb(name, shape, dt=F32, stack=None):
            return (stack or ctx).enter_context(nc.sbuf_tensor(name, shape, dt))

        def pb(name, dt=F32):
            return ctx.enter_context(nc.psum_tensor(name, [P, 512], dt))

        def sem(name):
            return ctx.enter_context(nc.semaphore(name))

        def sems(name, n):
            return [sem(f"{name}{i}") for i in range(n)]

        xres = sb("xres", [P, DT, S])
        XH = sb("XH", [P, DT, S], F32R)
        XL = sb("XL", [P, DT, S], F32R)
        raw = sb("raw", [P, RAW, DT, P])
        WH = sb("WH", [P, SPLIT, DT, P], F32R)
        WL = sb("WL", [P, SPLIT, DT, P], F32R)
        par = sb("par", [P, 6 * P])
        ident = sb("ident", [P, P])
        ones = sb("ones", [P, P])
        identb = sb("identb", [P, P], BF16)
        masks = sb("masks", [P, 2, P], BF16)
        work = sb("work", [P, 6, S])
        small = sb("small", [P, 96])
        tmp = [work[:, 0, :], work[:, 1, :]]
        ssum, ssq, rstd, mean = (work[:, i, :] for i in (2, 3, 4, 5))

        first = ExitStack()
        xin = sb("xin", [P, QT, D], stack=first)
        prow = sb("prow", [P, 6, P], stack=first)
        upad = sb("upad", [P, CT, TAPS - 1 + S], stack=first)
        sig = sb("sig", [P, 2, S], stack=first)
        vconv = sb("vconv", [P, CT, S], stack=first)
        ppad = sb("ppad", [P, CT, PAD + S], stack=first)
        psums = sb("psums", [P, 2, PAD + S], stack=first)
        ypool = sb("ypool", [P, CT, S], stack=first)
        wpool = sb("wpool", [P, CT, P], stack=first)
        mixp = sb("mixp", [P, 2, S], stack=first)
        cnts = sb("cnts", [P, PAD], stack=first)
        icnt = sb("icnt", [P, PAD], stack=first)
        first.close()
        ffn = ExitStack()
        HH = sb("HH", [P, FT, S], F32R, stack=ffn)
        HL = sb("HL", [P, FT, S], F32R, stack=ffn)
        act_g = sb("act_g", [P, 2, S], stack=ffn)
        hid = sb("hid", [P, 2, S], stack=ffn)
        ffn.close()
        att = ExitStack()
        QKV = sb("QKV", [P, 3 * DT, S], stack=att)
        QKH = sb("QKH", [P, 2, 2, S], F32R, stack=att)
        QKL = sb("QKL", [P, 2, 2, S], F32R, stack=att)
        VH = sb("VH", [P, 2, S], F32R, stack=att)
        VL = sb("VL", [P, 2, S], F32R, stack=att)
        PTH = sb("PTH", [P, 2, QT, S], F32R, stack=att)
        PTL = sb("PTL", [P, 2, QT, S], F32R, stack=att)
        only1 = ExitStack()
        Cm = sb("Cm", [P, 2, S], F32R, stack=only1)
        wf = sb("wf", [P, DT, FOX_HEADS], stack=only1)
        hot = sb("hot", [P, FOX_HEADS // 2], stack=only1)
        onesr = sb("onesr", [P, P], F32R, stack=only1)
        only1.close()
        rope = sb("rope", [P, 2, S], stack=att)
        lamr = sb("lamr", [1, 4 * HEAD], stack=att)
        att.close()
        pmap = work
        CC = work[:, 2, :]
        lam_row = [small[0:1, 40:42], small[0:1, 42:44], small[0:1, 44:45]]

        bank = [pb("bank0"), pb("bank1")]
        sc = [pb("score0"), pb("score1")]
        tb = [pb("turned0"), pb("turned1")]
        ob = [pb("attended0"), pb("attended1")]

        x_in = sem("x_in")
        par_in = sem("par_in")
        small_in = sem("small_in")
        wf_in = sem("wf_in")
        rope_in = sem("rope_in")
        w_landed = sems("w_landed", RAW)
        w_hi = sem("w_hi")
        w_lo = sem("w_lo")
        item_done = sem("item_done")
        bank_read = sems("bank_read", 2)
        consts = sem("consts")
        turned_x = sem("turned_x")
        turned_par = sem("turned_par")
        par_ok = sem("par_ok")
        dv = sem("dv")
        av = sem("av")
        gv = sem("gv")
        sum_tiles = sem("sum_tiles")
        stats_done = sem("stats_done")
        var_ready = sem("var_ready")
        rstd_ready = sem("rstd_ready")
        xn_ready = sem("xn_ready")
        x_hi = sem("x_hi")
        x_lo = sem("x_lo")
        cv_sum = sem("cv_sum")
        cv_stats, cv_var, cv_rstd = sem("cv_stats"), sem("cv_var"), sem("cv_rstd")
        cv_n, cv_hi, cv_lo = sem("cv_n"), sem("cv_hi"), sem("cv_lo")
        ypool_ready, pool_mm = sem("ypool_ready"), sem("pool_mm")
        pool_out, pool_hi, pool_lo = sem("pool_out"), sem("pool_hi"), sem("pool_lo")
        h_hi = sem("h_hi")
        h_lo = sems("h_lo", 2)
        g_act = sem("g_act")
        ff_lin = sems("ff_lin", 2)
        gate_done = sem("gate_done")
        gate_a, gate_b = sem("gate_a"), sem("gate_b")
        cc_zero = sem("cc_zero")
        hid_ready = sems("hid_ready", 2)
        roped = sems("roped", 2)
        rot_ready = sem("rot_ready")
        cc_ready = sem("cc_ready")
        st_h = sem("st_h")
        st_l = sem("st_l")
        cm_ready = sem("cm_ready")
        v_turned = sems("v_turned", 2)
        v_out = sems("v_out", 2)
        s_done = sems("s_done", 2)
        mx = sems("mx", 2)
        ex = sems("ex", 2)
        pn = sems("pn", 2)
        t_done = sems("t_done", 2)
        pt_h, pt_l = sems("pt_h", 2), sems("pt_l", 2)
        o_done = [sems(f"o_done{i}", 2) for i in range(2)]
        o_hi = sem("o_hi")
        o_read = sems("o_read", 2)
        lam_a, lam_b, lam_c, lam_d = (sem(f"lam_{x}") for x in "abcd")
        sub_sq, sub_var, sub_rs, sub_n, sub_hi, sub_lo = (
            sem(x) for x in ("sub_sq", "sub_var", "sub_rs", "sub_n", "sub_hi", "sub_lo"))
        y_turned = sem("y_turned")
        y_out = sem("y_out")

        slots = [*h_lo, *hid_ready, *o_done[0], *o_done[1], *ex, *t_done, *pt_l, *o_read, *v_turned, *v_out,
                 *roped, sub_lo]

        def pcol(name, t):
            return par[:, ROWS0[name][0] + t:ROWS0[name][0] + t + 1]

        def tap(j, c):
            return par[:, P + j * CT + c:P + j * CT + c + 1]

        def ff_par(layer, what, n):
            return par[:, bass.ds(n + ((2 + 2 * layer + what // 2) * P + (what % 2) * 44), 1)]

        def cols(w):
            return w.rearrange("(k p) n -> p k n", p=P)

        w_in, w_out0 = cols(A["w_in"][0]), cols(A["w_out"][0])
        w_gate, w_up = cols(A["w_gate"][0]), cols(A["w_up"][0])
        a_in, a_out = cols(A["a_w_in_2"][0]), cols(A["a_w_out_2"][0])
        kv_w, b_q, b_out = cols(A["kv_w_2"]), cols(A["b_w_q_2"][0]), cols(A["b_w_out_2"][0])
        ff_in = [cols(A["ffn_w_in_2"][i]) for i in range(2)]
        downs = [cols(A["w_down"][0])] + [cols(A["ffn_w_out_2"][i]) for i in range(2)]

        def qkv_there(eng, following):
            for b in range(2):
                eng.wait_ge(bank_read[b], STAGES[following][1] // 2)
                eng.wait_ge(v_out[b], DT // 2 * (1 if following == "out1" else 2) + OPEN)

        block = ctx.enter_context(nc.Block())

        @block.sync
        def _(sp):
            def load(g, src, kt=DT):
                if not (isinstance(g.it, int) and g.base < RAW):
                    sp.wait_ge(w_lo, g.n(1 - RAW))
                sp.dma_start(raw[:, g.slot(RAW), 0:kt, :], src).then_inc(w_landed[g.slot(RAW)], 16)

            def stage(name, times, per, source):
                with sp.Fori(0, times) as it:
                    for j in range(per):
                        load(Nth(STAGES[name][0] + j, it, per), *source(it, j))

            xv = A["x"][0].rearrange("(q p) d -> p q d", p=P)
            for q in range(QT):
                sp.dma_start(xin[:, q, :], xv[:, q, :]).then_inc(x_in, 16)
            for n in range(12):
                c = CT + n // 2 if n < 8 and n % 2 == 0 else n // 2 if n < 8 else n
                load(Nth(n), w_in[:, :, c * P:(c + 1) * P])
                if n == 3:
                    sp.dma_start(wpool[:, :, :], A["w_pool"][0].rearrange("i g h -> g i h")).then_inc(small_in, 16)

            def tiles(w, first=0):
                def source(it, j):
                    return (w[:, :, bass.ds(it * 4 * P + (first + j) * P, P)],)
                return source

            def pairs(wa, wb, first_b=0):
                def source(it, j):
                    return ((wa, wb)[j % 2][:, :, bass.ds(it * 2 * P + (j // 2 + (first_b if j % 2 else 0)) * P, P)],)
                return source

            def down(w):
                def source(it, j):
                    k0, kt = sum(DOWN[:j % 4]), DOWN[j % 4]
                    return (w[:, k0:k0 + kt, bass.ds(it * 2 * P + j // 4 * P, P)], kt)
                return source

            stage("out", 2, 4, tiles(w_out0))
            stage("gu0", FT // 2, 4, pairs(w_gate, w_up))
            stage("down0", DT // 2, 8, down(downs[0]))
            sp.wait_ge(item_done, STAGES["qkv1"][0])
            sp.dma_start(wf[:, :, :], a_in[:, :, 3 * D:3 * D + FOX_HEADS]).then_inc(wf_in, 16)
            sp.dma_start(small[0:FOX_HEADS, 48:49], A["a_b_f_2"].rearrange("o h -> h o")).then_inc(wf_in, 16)
            stage("qkv1", 6, 4, tiles(a_in))
            stage("out1", 2, 4, tiles(a_out))
            stage("gu1", FT // 2, 4, pairs(ff_in[0], ff_in[0], FT))
            stage("down1", DT // 2, 8, down(downs[1]))
            sp.wait_ge(item_done, STAGES["qkv2"][0])
            sp.dma_start(rope[:, :, :], A["rope"].rearrange("a p s -> p a s")).then_inc(rope_in, 16)
            sp.dma_start(lamr[:, :], A["b_lambda_2"].rearrange("o a d -> o (a d)")).then_inc(rope_in, 16)
            for which, source in enumerate((tiles(b_q), tiles(kv_w), tiles(kv_w, DT))):
                with sp.Fori(0, 2) as it:
                    for j in range(4):
                        load(Nth(STAGES["qkv2"][0] + which * DT + j, it, 4), *source(it, j))
            stage("out2", 2, 4, tiles(b_out))
            stage("gu2", FT // 2, 4, pairs(ff_in[1], ff_in[1], FT))
            stage("down2", DT // 2, 8, down(downs[2]))
            ov = out[0].rearrange("(q p) d -> p q d", p=P)
            for q in range(QT):
                for b in range(2):
                    sp.wait_ge(bank_read[b], STAGES["back"][1] // 2 + q + 1)
                sp.dma_start(ov[:, q, :], QKV[:, 2 * q:2 * q + 2, :].rearrange("p a s -> p (a s)")).then_inc(y_out, 16)
            sp.wait_ge(y_out, 16 * QT)

        @block.gpsimd
        def _(pool):
            own = Chain(pool, gv)

            def low(g):
                pool.wait_ge(w_hi, g.n(1))
                s = g.slot(SPLIT)
                pool.tensor_tensor(WL[:, s, :, :], raw[:, g.slot(RAW), :, :], WH[:, s, :, :].bitcast(F32),
                                   ALU.subtract).then_inc(w_lo, 1)

            pool.memset(ident[:, :], 0.0).then_inc(consts, 1)
            pool.memset(ones[:, :], 1.0).then_inc(consts, 1)
            pool.wait_ge(consts, 1)
            pool.affine_select(out=ident[:, :], in_=ident[:, :], compare_op=ALU.not_equal, fill=1.0,
                               base=0, pattern=[[-1, P]], channel_multiplier=1).then_inc(consts, 1)
            for c in range(CT):
                pool.memset(ppad[:, c, 0:PAD], 0.0).then_inc(consts, 1)
                pool.memset(upad[:, c, 0:TAPS - 1], 0.0).then_inc(consts, 1)
            for c in range(2):
                pool.memset(psums[:, c, 0:PAD], 0.0).then_inc(consts, 1)
            for c in range(PAD):
                pool.memset(cnts[:, c:c + 1], float(c + 1)).then_inc(consts, 1)
            pool.memset(masks[:, :, :], 0.0).then_inc(consts, 1)
            done = 3 + 2 * CT + 2 + PAD + 1
            pool.wait_ge(consts, done)
            pool.affine_select(out=masks[:, 0, :], in_=masks[:, 0, :], compare_op=ALU.is_ge, fill=MASKED,
                               base=0, pattern=[[-1, P]], channel_multiplier=1).then_inc(consts, 1)
            pool.memset(masks[0:CHUNK, 1, CHUNK:P], MASKED).then_inc(consts, 1)
            pool.tensor_copy(identb[:, :], ident[:, :]).then_inc(consts, 1)
            for n, q in enumerate(slots):
                pool.memset(small[:, 64 + n:65 + n], 0.0).then_inc(q, OPEN)

            def lows_of_x(m, src):
                for t in range(DT):
                    pool.wait_ge(x_hi, DT * m + t + 1)
                    pool.tensor_tensor(XL[:, t, :], src(t), XH[:, t, :].bitcast(F32),
                                       ALU.subtract).then_inc(x_lo, 1)

            low(Nth(0))
            lows_of_x(0, lambda t: tmp[t % 2])
            for n in range(12):
                low(Nth(n + 1))
            pool.wait_ge(cv_n, 1)
            for i, w in enumerate(WINDOWS):
                pool.wait_ge(bank_read[i % 2], (DT + 8 + i) // 2 + 1)
                src, d, side = ppad[:, i, :], 1, 0
                while d < w:
                    dst = psums[:, side, :]
                    own.link(pool.tensor_tensor(dst[:, PAD:], src[:, PAD:], src[:, PAD - d:PAD + S - d], ALU.add))
                    src, d, side = dst, 2 * d, 1 - side
                own.did(pool.tensor_tensor(ypool[:, i, 0:w], src[:, PAD:PAD + w], icnt[:, 0:w], ALU.mult))
                own.link(pool.tensor_scalar(ypool[:, i, w:], src[:, PAD + w:], 1.0 / w, None, ALU.mult))
                pool.tensor_tensor(ypool[:, i, :], ypool[:, i, :], ppad[:, i, PAD:], ALU.subtract).then_inc(ypool_ready, 1)
            for i in range(CT):
                pool.wait_ge(pool_hi, i + 1)
                pool.tensor_tensor(XL[:, CT + i, :], mixp[:, i % 2, :], XH[:, CT + i, :].bitcast(F32),
                                   ALU.subtract).then_inc(pool_lo, 1)
            for c in range(CT):
                pool.wait_ge(cv_hi, c + 1)
                pool.tensor_tensor(XL[:, c, :], vconv[:, c, :], XH[:, c, :].bitcast(F32),
                                   ALU.subtract).then_inc(cv_lo, 1)

            def lows(name, times, per):
                with pool.Fori(0, times) as it:
                    for j in range(per):
                        low(Nth(STAGES[name][0] + j + 1, it, per))

            def lows_of_hidden(name, layer):
                with pool.Fori(0, FT // 2) as it:
                    for j in range(2):
                        low(Nth(STAGES[name][0] + 2 * j + 1, it, 4))
                        low(Nth(STAGES[name][0] + 2 * j + 2, it, 4))
                        h = Nth(FT * layer + j, it, 2)
                        pool.wait_ge(h_hi, h.n(1))
                        pool.tensor_tensor(HL[:, bass.ds(it * 2 + j, 1), :], hid[:, j:j + 1, :],
                                           HH[:, bass.ds(it * 2 + j, 1), :].bitcast(F32), ALU.subtract).then_inc(h_lo[j], 1)

            lows("out", 2, 4)
            lows_of_x(1, lambda t: tmp[t % 2])
            lows_of_hidden("gu0", 0)
            lows("down0", DT // 2, 8)
            lows_of_x(2, lambda t: xres[:, t, :])
            pool.memset(CC, 0.0).then_inc(cc_zero, 1)
            lows("qkv1", 6, 4)
            qkv_there(pool, "out1")

            def stage_lo(tile, low_, high_):
                pool.tensor_tensor(low_, QKV[:, tile, :], high_.bitcast(F32), ALU.subtract).then_inc(st_l, 1)

            with pool.Fori(0, FOX_HEADS // 4) as it:
                for s in range(2):
                    pool.wait_ge(o_done[s][1], Nth(0, it, 1).n() + OPEN)
                    for k in range(3):
                        pool.wait_ge(st_h, Nth(3 * s + k, it, 6).n(1))
                        stage_lo(bass.ds(it * 2 + (s + DT * k), 1), *((QKL[:, s, k:k + 1, :], QKH[:, s, k:k + 1, :]) if k < 2
                                 else (VL[:, s:s + 1, :], VH[:, s:s + 1, :])))
            lows("out1", 2, 4)
            lows_of_x(3, lambda t: xres[:, t, :])
            lows_of_hidden("gu1", 1)
            lows("down1", DT // 2, 8)
            lows_of_x(4, lambda t: xres[:, t, :])
            lows("qkv2", 6, 4)
            for q in roped:
                pool.wait_ge(q, DT + OPEN)
            with pool.Fori(0, DIFF_HEADS // 2) as it:
                for c in range(2):
                    for k in range(2):
                        pool.wait_ge(st_h, Nth(3 * FOX_HEADS // 2 + 2 * c + k, it, 6).n(1))
                        stage_lo(bass.ds(it + (4 * c + DT * k), 1), QKL[:, c, k:k + 1, :], QKH[:, c, k:k + 1, :])
                for e in range(2):
                    pool.wait_ge(st_h, Nth(3 * FOX_HEADS // 2 + 4 + e, it, 6).n(1))
                    stage_lo(bass.ds(it * 2 + (e + 2 * DT), 1), VL[:, e:e + 1, :], VH[:, e:e + 1, :])
                for e in range(2):
                    pool.wait_ge(sub_hi, Nth(e, it, 2).n(1))
                    pool.tensor_tensor(XL[:, bass.ds(it * 2 + e, 1), :], work[:, 4:5, :],
                                       XH[:, bass.ds(it * 2 + e, 1), :].bitcast(F32), ALU.subtract).then_inc(sub_lo, 1)
            lows("out2", 2, 4)
            lows_of_x(5, lambda t: xres[:, t, :])
            lows_of_hidden("gu2", 2)
            lows("down2", DT // 2 - 1, 8)
            for j in range(7):
                low(Nth(STAGES["down2"][0] + 8 * (DT // 2 - 1) + j + 1))

        @block.tensor
        def _(pe):
            def product(out_, wh, wl, xh, xl, start, stop):
                pe.matmul(out_, wh, xl, start=start, stop=False)
                pe.matmul(out_, wh, xh, start=False, stop=False)
                return pe.matmul(out_, wl, xh, start=False, stop=stop)

            def item(g, b, hi, lo, k0, kt, start, stop):
                pe.wait_ge(w_lo, g.n(1))
                s = g.slot(SPLIT)
                for k in range(kt):
                    mm = product(bank[b][:, :], WH[:, s, k, :], WL[:, s, k, :], hi[:, k0 + k, :], lo[:, k0 + k, :],
                                 start and k == 0, stop and k == kt - 1)
                mm.then_inc(item_done, 1)

            def bank_free(u):
                pe.wait_ge(bank_read[u.slot(2)], u.round(2))

            def stage(name, times, per=4):
                with pe.Fori(0, times) as it:
                    for j in range(per):
                        u = Nth(STAGES[name][1] + j, it, per)
                        bank_free(u)
                        item(Nth(STAGES[name][0] + j, it, per), u.slot(2), XH, XL, 0, DT, True, True)

            def down(name, layer):
                for q in h_lo:
                    pe.wait_ge(q, (layer + 1) * FT // 2 + OPEN)
                with pe.Fori(0, DT // 2) as it:
                    for j in range(8):
                        u = Nth(STAGES[name][1] + j // 4, it, 2)
                        if j % 4 == 0:
                            bank_free(u)
                        item(Nth(STAGES[name][0] + j, it, 8), u.slot(2), HH, HL, sum(DOWN[:j % 4]), DOWN[j % 4],
                             j % 4 == 0, j % 4 == 3)

            def stage_v(name, before):
                with pe.Fori(0, 2) as it:
                    for j in range(5):
                        if j < 4:
                            n = Nth(2 * DT + j, it, 4)
                            u = n + STAGES[name][1]
                            bank_free(u)
                            item(n + STAGES[name][0], u.slot(2), XH, XL, 0, DT, True, True)
                        for t in {1: [0], 2: [1], 3: [2], 4: [3]}.get(j, []):
                            b, n = t % 2, Nth(2 * DT + t, it, 4)
                            pe.wait_ge(bank_read[b], (n + STAGES[name][1]).round(2, 1))
                            pe.wait_ge(v_out[b], Nth(before + t, it, 4).round(2) + OPEN)
                            for q in range(QT):
                                mm = pe.transpose(tb[b][:, q * P:(q + 1) * P], tmp[b][:, q * P:(q + 1) * P], ident[:, :])
                            mm.then_inc(v_turned[b], 1)

            def stats(m, centred):
                pe.wait_ge(sum_tiles, DT * (m + 1))
                mm = pe.matmul(sc[0][:, :], ones[:, :], ssq, start=True, stop=True)
                if centred:
                    mm = pe.matmul(sc[1][:, :], ones[:, :], ssum, start=True, stop=True)
                mm.then_inc(stats_done, 1)

            pe.wait_ge(consts, 3)
            pe.wait_ge(x_in, 16 * QT)
            for t in range(DT):
                if t >= 2:
                    pe.wait_ge(bank_read[t % 2], t // 2)
                for q in range(QT):
                    mm = pe.transpose(bank[t % 2][:, q * P:(q + 1) * P], xin[:, q, t * P:(t + 1) * P], ident[:, :])
                mm.then_inc(turned_x, 1)
            pe.wait_ge(par_in, 16 * PAR_LOADS)
            for i, n in enumerate(ROWS_OF):
                mm = pe.transpose(tb[i // 4][:, i % 4 * P:i % 4 * P + n], prow[0:n, i, :], ident[0:n, 0:n])
            mm.then_inc(turned_par, 1)
            stats(0, False)
            pe.wait_ge(x_lo, DT)
            for n in range(12):
                u = Nth(STAGES["in"][1] + n)
                bank_free(u)
                item(Nth(n), u.slot(2), XH, XL, 0, DT, True, True)
            pe.wait_ge(small_in, 16)
            pe.wait_ge(par_ok, 2)
            for i in range(CT):
                pe.wait_ge(ypool_ready, i + 1)
                if i >= 2:
                    pe.wait_ge(pool_out, i - 1)
                pe.matmul(tb[i % 2][:, :], wpool[:, i, :], ypool[:, i, :], start=True, stop=True).then_inc(pool_mm, 1)
            pe.wait_ge(cv_sum, CT)
            pe.matmul(sc[0][:, :], ones[:, :], ssq, start=True, stop=True)
            pe.matmul(sc[1][:, :], ones[:, :], ssum, start=True, stop=True).then_inc(cv_stats, 1)
            pe.wait_ge(pool_lo, CT)
            pe.wait_ge(cv_lo, CT)
            stage("out", 2)
            stats(1, False)
            pe.wait_ge(x_lo, 2 * DT)
            stage("gu0", FT // 2)
            down("down0", 0)
            stats(2, False)
            pe.wait_ge(x_lo, 3 * DT)
            pe.wait_ge(wf_in, 32)
            for k in range(DT):
                mm = pe.matmul(sc[0][0:FOX_HEADS, :], wf[:, k, :], xres[:, k, :], start=(k == 0), stop=(k == DT - 1))
            mm.then_inc(gate_done, 1)
            stage("qkv1", 4)
            stage_v("qkv1", 0)

            def turn_map(b, used, src, i):
                pe.wait_ge(pn[b], used.n(1))
                pe.wait_ge(pt_l[b], used.n() + OPEN)
                for j in range(i + 1):
                    mm = pe.transpose(tb[b][:, j * P:(j + 1) * P], src[:, j * P:(j + 1) * P], ident[:, :])
                mm.then_inc(t_done[b], 1)

            def attend(v, e, o_turn, done):
                pe.wait_ge(o_read[e], o_turn + OPEN)
                for j in range(QT):
                    mm = product(ob[e][:, j * P:], VH[:, v, j * P:(j + 1) * P], VL[:, v, j * P:(j + 1) * P], PTH[:, e, j, j * P:],
                                 PTL[:, e, j, j * P:], j == 0, j == QT - 1)
                mm.then_inc(done, 1)

            def score(b, used, slot, e, i, mask, bias):
                n = (i + 1) * P
                rows = slice(HEAD * e, HEAD * e + HEAD)
                q, k = slice(i * P, n), slice(0, n)
                pe.wait_ge(ex[b], used.n() + OPEN)
                pe.matmul(sc[b][:, k], QKH[rows, slot, 0, q], QKL[rows, slot, 1, k], start=True, stop=False)
                pe.matmul(sc[b][:, k], QKH[rows, slot, 0, q], QKH[rows, slot, 1, k], start=False, stop=False)
                pe.matmul(sc[b][:, k], QKL[rows, slot, 0, q], QKH[rows, slot, 1, k], start=False, stop=False)
                if bias:
                    pe.matmul(sc[b][:, k], onesr[rows, :], Cm[rows, slot, k], start=False, stop=False)
                pe.matmul(sc[b][:, i * P:n], identb[:, :], masks[:, mask, :], start=False, stop=True).then_inc(s_done[b], 1)

            qkv_there(pe, "out1")
            pe.wait_ge(consts, CONSTS)
            pe.wait_ge(cc_ready, 5)
            with pe.Fori(0, FOX_HEADS // 4) as it:
                steps = [(s, e, i) for s in range(2) for e in range(2) for i in range(QT)]

                def used_of(s, e, i):
                    return Nth(2 * (2 * s + e) + i // 2, it, 8)
                for n in range(len(steps) + 2):
                    if n < len(steps):
                        s, e, i = steps[n]
                        if e == 0 and i == 0:
                            pe.wait_ge(st_l, Nth(3 * s, it, 6).n(3))
                            pe.wait_ge(cm_ready, Nth(s, it, 2).n(1))
                        score(i % 2, used_of(s, e, i), s, e, i, 0, True)
                    if 1 <= n <= len(steps):
                        s, e, i = steps[n - 1]
                        turn_map(i % 2, used_of(s, e, i), pmap[:, i % 2, :], i)
                    if n >= 2 and steps[n - 2][2] == QT - 1:
                        s, e, _ = steps[n - 2]
                        for b in range(2):
                            pe.wait_ge(pt_l[b], Nth(2 * (2 * s + e), it, 8).n(2) + OPEN)
                        attend(s, e, Nth(s, it, 2).n(), o_done[s][e])
            pe.wait_ge(o_read[0], FOX_HEADS // 2 + OPEN)
            pe.wait_ge(o_read[1], FOX_HEADS // 2 + OPEN)
            stage("out1", 2)
            stats(3, True)
            pe.wait_ge(x_lo, 4 * DT)
            stage("gu1", FT // 2)
            down("down1", 1)
            stats(4, True)
            pe.wait_ge(x_lo, 5 * DT)
            stage("qkv2", 4)
            stage_v("qkv2", DT)
            pe.wait_ge(lam_a, 1)
            pe.matmul(sc[0][:, 0:1], ones[0:1, :], lam_row[2], start=True, stop=True).then_inc(lam_b, 1)

            qkv_there(pe, "subln")
            for q in roped:
                pe.wait_ge(q, DT + OPEN)
            pe.wait_ge(lam_d, 1)
            with pe.Fori(0, DIFF_HEADS // 2) as it:
                pe.wait_ge(st_l, Nth(3 * FOX_HEADS // 2, it, 6).n(6))
                steps = [(e, i) for e in range(2) for i in range(QT)]
                for n in range(len(steps) + 2):
                    if n < len(steps):
                        e, i = steps[n]
                        for c in range(2):
                            score(c, Nth(2 * FOX_HEADS + n, it, 8), c, e, i, 1, False)
                    if 1 <= n <= len(steps):
                        e, i = steps[n - 1]
                        turn_map(i % 2, Nth(2 * FOX_HEADS + (n - 1) // 2, it, 4), pmap[:, 2 * (i % 2), :], i)
                    if n >= 2 and steps[n - 2][1] == QT - 1:
                        e, _ = steps[n - 2]
                        for b in range(2):
                            pe.wait_ge(pt_l[b], Nth(2 * FOX_HEADS + 2 * e, it, 4).n(2) + OPEN)
                        attend(e, e, Nth(FOX_HEADS // 2, it, 1).n(), o_done[0][e])
                        u = Nth(STAGES["subln"][1] + e, it, 2)
                        bank_free(u)
                        pe.wait_ge(sub_sq, Nth(e, it, 2).n(1))
                        pe.matmul(bank[e][:, :], ones[:, :], work[:, 5, :], start=True, stop=True).then_inc(sub_var, 1)
            pe.wait_ge(sub_lo, DIFF_HEADS + OPEN)
            stage("out2", 2)
            stats(5, True)
            pe.wait_ge(x_lo, 6 * DT)
            stage("gu2", FT // 2)
            down("down2", 2)
            stats(6, True)
            pe.wait_ge(x_hi, 7 * DT)
            for n in range(2 * QT):
                u = Nth(STAGES["back"][1] + n)
                bank_free(u)
                for k in range(4):
                    mm = pe.transpose(bank[u.slot(2)][:, k * P:(k + 1) * P],
                                      xres[:, n % 2 * 4 + k, n // 2 * P:(n // 2 + 1) * P], ident[:, :])
                mm.then_inc(y_turned, 1)

        @block.scalar
        def _(act):
            own = Chain(act, av)

            def rows(i, r, src):
                n = src.shape[0]
                act.dma_start(prow[r:r + n, i, :], src).then_inc(par_in, 16)

            for name, (r, n) in ROWS0.items():
                src = A[name]
                if len(src.shape) == 1:
                    src = src.rearrange("(t p) -> t p", p=P)
                else:
                    src = src.rearrange("l (t p) -> (l t) p", p=P)
                rows(0, r, src)
            rows(1, 0, A["w_dw"][0].rearrange("j (c p) -> (j c) p", p=P))
            for layer in range(2):
                taps = A["ffn_conv_w_2"][layer].rearrange("j (c p) -> j c p", p=P)
                rows(2 + 2 * layer, 0, taps[0])
                rows(2 + 2 * layer, 44, taps[1])
                rows(3 + 2 * layer, 0, taps[2])
                rows(3 + 2 * layer, 44, A["ffn_conv_b_2"][layer].rearrange("(c p) -> c p", p=P))

            def high(g):
                act.wait_ge(w_landed[g.slot(RAW)], g.round(RAW, 1) * 16)
                if not (isinstance(g.it, int) and g.base < SPLIT):
                    act.wait_ge(item_done, g.n(1 - SPLIT))
                act.activation(WH[:, g.slot(SPLIT), :, :], raw[:, g.slot(RAW), :, :], ACT.Copy).then_inc(w_hi, 1)

            def root(m):
                act.wait_ge(var_ready, m + 1)
                act.activation(rstd, work[:, 1, :], ACT.Sqrt).then_inc(rstd_ready, 1)

            def norm_rms(m, src):
                root(m)
                for t in range(DT):
                    act.wait_ge(xn_ready, DT * m + t + 1)
                    act.activation(XH[:, t, :], src(t), ACT.Copy).then_inc(x_hi, 1)

            def norm_ln(m, g, b, split=True):
                root(m)
                for t in range(DT):
                    act.wait_ge(xn_ready, DT * m + t + 1)
                    y = act.activation(xres[:, t, :], tmp[t % 2], ACT.Identity, bias=b(t), scale=g(t))
                    if split:
                        own.link(y)
                        act.activation(XH[:, t, :], xres[:, t, :], ACT.Copy).then_inc(x_hi, 1)
                    else:
                        y.then_inc(x_hi, 1)

            def highs(name, times, per):
                with act.Fori(0, times) as it:
                    for j in range(per):
                        high(Nth(STAGES[name][0] + j + 1, it, per))

            high(Nth(0))
            norm_rms(0, lambda t: tmp[t % 2])
            act.wait_ge(par_ok, 2)
            for n in range(12):
                high(Nth(n + 1))
                u = Nth(STAGES["in"][1] + n)
                if n < 8 and n % 2 == 0:
                    c = n // 2
                    act.wait_ge(item_done, n + 1)
                    if c >= 2:
                        act.wait_ge(bank_read[1], (DT + 2 * (c - 2) + 1) // 2 + 1)
                    act.activation(sig[:, c % 2, :], bank[0][:, :], ACT.Sigmoid, bias=pcol("b_in", CT + c)).then_inc(bank_read[0], 1)
                elif n >= 8:
                    act.wait_ge(item_done, n + 1)
                    act.wait_ge(consts, CONSTS)
                    act.activation(ppad[:, n - 8, PAD:], bank[u.slot(2)][:, :], ACT.Identity,
                                   bias=pcol("b_in", n)).then_inc(bank_read[u.slot(2)], 1)
            for i in range(CT):
                act.wait_ge(pool_mm, i + 1)
                if i >= 2:
                    act.wait_ge(pool_lo, i - 1)
                act.activation(mixp[:, i % 2, :], tb[i % 2][:, :], ACT.Copy, scale=pcol("s_pool", i)).then_inc(pool_out, 1)
                act.wait_ge(pool_out, i + 1)
                act.activation(XH[:, CT + i, :], mixp[:, i % 2, :], ACT.Copy).then_inc(pool_hi, 1)
            act.wait_ge(cv_var, 1)
            act.activation(rstd, work[:, 1, :], ACT.Sqrt).then_inc(cv_rstd, 1)
            for c in range(CT):
                act.wait_ge(cv_n, 2 + c)
                own.link(act.activation(vconv[:, c, :], vconv[:, c, :], ACT.Silu, bias=pcol("ln_b", c), scale=pcol("ln_g", c)))
                act.activation(XH[:, c, :], vconv[:, c, :], ACT.Copy).then_inc(cv_hi, 1)
            highs("out", 2, 4)
            norm_rms(1, lambda t: tmp[t % 2])

            def hidden_hi(it, j, layer, name):
                act.wait_ge(bank_read[1], Nth(STAGES[name][1] + 2 * j + 1, it, 4).round(2, 1))
                act.activation(HH[:, bass.ds(it * 2 + j, 1), :], hid[:, j:j + 1, :], ACT.Copy).then_inc(h_hi, 1)

            with act.Fori(0, FT // 2) as it:
                for j in range(2):
                    g = Nth(STAGES["gu0"][0] + 2 * j, it, 4)
                    high(g + 1)
                    act.wait_ge(item_done, g.n(1))
                    act.wait_ge(bank_read[1], Nth(STAGES["gu0"][1] + 2 * j + 1, it, 4).round(2, -1))
                    act.activation(act_g[:, j, :], bank[0][:, :], ACT.Silu).then_inc(bank_read[0], 1)
                    high(g + 2)
                    hidden_hi(it, j, 0, "gu0")
            highs("down0", DT // 2, 8)
            norm_rms(2, lambda t: xres[:, t, :])
            act.wait_ge(gate_a, 1)
            act.activation(tmp[1][0:FOX_HEADS, :], tmp[1][0:FOX_HEADS, :], ACT.Exp).then_inc(gate_b, 1)
            act.wait_ge(gate_b, 1)
            act.activation(tmp[1][0:FOX_HEADS, :], tmp[1][0:FOX_HEADS, :], ACT.Ln, bias=1.0).then_inc(gate_b, 1)

            def values_out(name, before):
                with act.Fori(0, 2) as it:
                    for j in range(4):
                        n = Nth(2 * DT + j, it, 4)
                        g, u = n + STAGES[name][0], n + STAGES[name][1]
                        high(g + 1)
                        act.wait_ge(item_done, g.n(1))
                        act.wait_ge(v_turned[j % 2], Nth(before + j, it, 4).round(2) + OPEN)
                        act.activation(tmp[j % 2], bank[j % 2][:, :], ACT.Copy).then_inc(bank_read[j % 2], 1)

            for part in range(2):
                with act.Fori(0, 2) as it:
                    for j in range(4):
                        n = Nth(8 * part + j, it, 4)
                        g, u = n + STAGES["qkv1"][0], n + STAGES["qkv1"][1]
                        high(g + 1)
                        act.wait_ge(item_done, g.n(1))
                        act.activation(QKV[:, bass.ds(it * 4 + (8 * part + j), 1), :], bank[u.slot(2)][:, :].rearrange("p (a s) -> p a s", a=1), ACT.Copy,
                                       scale=(HEAD ** -0.5 if part == 0 else 1.0)).then_inc(bank_read[u.slot(2)], 1)
            act.wait_ge(cc_ready, 4)
            values_out("qkv1", 0)
            qkv_there(act, "out1")

            def stage_hi(tile, dst):
                act.activation(dst, QKV[:, tile, :], ACT.Copy).then_inc(st_h, 1)

            def exps(b, used, dst, i):
                act.wait_ge(mx[b], used.n(1))
                act.activation(dst[:, 0:(i + 1) * P], sc[b][:, 0:(i + 1) * P], ACT.Exp, bias=small[:, b:b + 1],
                               accum_out=small[:, 2 + b:3 + b]).then_inc(ex[b], 1)

            def map_hi(b, used, e, i):
                act.wait_ge(t_done[b], used.n(1) + OPEN)
                act.activation(PTH[:, e, 0:i + 1, i * P:(i + 1) * P],
                               tb[b][:, 0:(i + 1) * P].rearrange("p (j q) -> p j q", q=P), ACT.Copy).then_inc(pt_h[b], 1)

            with act.Fori(0, FOX_HEADS // 4) as it:
                steps = [(s, e, i) for s in range(2) for e in range(2) for i in range(QT)]

                def used_of(s, e, i):
                    return Nth(2 * (2 * s + e) + i // 2, it, 8)
                for n in range(len(steps) + 2):
                    if n < len(steps):
                        s, e, i = steps[n]
                        if e == 0 and i == 0:
                            act.wait_ge(o_done[s][1], Nth(0, it, 1).n() + OPEN)
                            for k in range(2):
                                stage_hi(bass.ds(it * 2 + (s + DT * k), 1), QKH[:, s, k:k + 1, :])
                            stage_hi(bass.ds(it * 2 + (s + 2 * DT), 1), VH[:, s:s + 1, :])
                        act.wait_ge(t_done[i % 2], used_of(s, e, i).n() + OPEN)
                        exps(i % 2, used_of(s, e, i), pmap[:, i % 2, :], i)
                    if 1 <= n <= len(steps):
                        s, e, i = steps[n - 1]
                        if i == 0:
                            act.wait_ge(o_done[1 - s][e], Nth(s, it, 1).n() + OPEN)
                        map_hi(i % 2, used_of(s, e, i), e, i)
                    if n >= 2 and steps[n - 2][2] == QT - 1:
                        s, e, _ = steps[n - 2]
                        r = slice(HEAD * e, HEAD * e + HEAD)
                        act.wait_ge(o_done[s][e], Nth(0, it, 1).n(1) + OPEN)
                        act.activation(XH[r, bass.ds(it * 2 + s, 1), :], ob[e][r, :].rearrange("p (a s) -> p a s", a=1), ACT.Copy).then_inc(o_hi, 1)
            highs("out1", 2, 4)
            norm_ln(3, lambda t: pcol("ln_attn_g_2", t), lambda t: pcol("ln_attn_b_2", t))

            def conv_hidden(name, layer):
                with act.Fori(0, FT // 2) as it:
                    for j in range(2):
                        g = Nth(STAGES[name][0] + 2 * j, it, 4)
                        for side, dst in ((0, act_g), (1, hid)):
                            high(g + side + 1)
                            act.wait_ge(item_done, g.n(1 + side))
                            if side == 0:
                                act.wait_ge(hid_ready[j], Nth(FT * (layer - 1) + j, it, 2).round(2) + OPEN)
                            else:
                                act.wait_ge(h_lo[j], Nth(FT * layer + j, it, 2).round(2) + OPEN)
                            n = it * 2 + (j + FT * side)
                            act.activation(dst[:, j, :], bank[side][:, :], ACT.Identity, bias=ff_par(layer - 1, 3, n),
                                           scale=ff_par(layer - 1, 2, n)).then_inc(ff_lin[side], 1)
                        act.wait_ge(bank_read[0], Nth(STAGES[name][1] + 2 * j, it, 4).round(2, 1))
                        act.activation(act_g[:, j, :], act_g[:, j, :], ACT.Silu).then_inc(g_act, 1)
                        act.wait_ge(hid_ready[j], Nth(FT * (layer - 1) + j, it, 2).round(2, 1) + OPEN)
                        act.activation(HH[:, bass.ds(it * 2 + j, 1), :], hid[:, j:j + 1, :], ACT.Copy).then_inc(h_hi, 1)

            conv_hidden("gu1", 1)
            highs("down1", DT // 2, 8)
            norm_ln(4, lambda t: pcol("ln_ffn_g_2", t), lambda t: pcol("ln_ffn_b_2", t))
            for part in range(2):
                with act.Fori(0, 2) as it:
                    for j in range(4):
                        n = Nth(8 * part + j, it, 4)
                        g, u = n + STAGES["qkv2"][0], n + STAGES["qkv2"][1]
                        high(g + 1)
                        act.wait_ge(item_done, g.n(1))
                        src = bank[u.slot(2)]
                        act.wait_ge(roped[j % 2], n.round(2) + OPEN)
                        for r in range(4):
                            o = r + 1 - 2 * (r % 2)
                            act.activation(tmp[j % 2][32 * r:32 * r + 32, :], src[32 * o:32 * o + 32, :], ACT.Copy).then_inc(rot_ready, 1)
            for q in roped:
                act.wait_ge(q, DT + OPEN)
            values_out("qkv2", DT)
            qkv_there(act, "subln")
            act.wait_ge(lam_c, 1)
            act.activation(lam_row[1], lam_row[0], ACT.Exp).then_inc(lam_c, 1)

            with act.Fori(0, DIFF_HEADS // 2) as it:
                act.wait_ge(o_done[0][1], Nth(FOX_HEADS // 4, it, 1).n() + OPEN)
                for c in range(2):
                    for k in range(2):
                        stage_hi(bass.ds(it + (4 * c + DT * k), 1), QKH[:, c, k:k + 1, :])
                for e in range(2):
                    stage_hi(bass.ds(it * 2 + (e + 2 * DT), 1), VH[:, e:e + 1, :])
                steps = [(e, i) for e in range(2) for i in range(QT)]
                for n in range(len(steps) + 2):
                    if n < len(steps):
                        e, i = steps[n]
                        t = Nth(2 * FOX_HEADS + n // 2, it, 4)
                        act.wait_ge(t_done[i % 2], t.n() + OPEN)
                        for c in range(2):
                            used = Nth(2 * FOX_HEADS + n, it, 8)
                            act.wait_ge(mx[c], used.n(1))
                            act.activation(pmap[:, 2 * (i % 2) + c, 0:(i + 1) * P], sc[c][:, 0:(i + 1) * P], ACT.Exp,
                                           bias=small[:, 4 + 2 * (i % 2) + c:5 + 2 * (i % 2) + c],
                                           accum_out=small[:, 8 + 2 * (i % 2) + c:9 + 2 * (i % 2) + c]).then_inc(ex[c], 1)
                    if 1 <= n <= len(steps):
                        e, i = steps[n - 1]
                        if i == 0:
                            act.wait_ge(o_done[0][e], Nth(FOX_HEADS // 4, it, 1).n() + OPEN)
                        map_hi(i % 2, Nth(2 * FOX_HEADS + (n - 1) // 2, it, 4), e, i)
                    if n >= 2 and steps[n - 2][1] == QT - 1:
                        e, _ = steps[n - 2]
                        m = Nth(e, it, 2)
                        act.wait_ge(o_done[0][e], Nth(FOX_HEADS // 4, it, 1).n(1) + OPEN)
                        act.wait_ge(sub_lo, m.n() + OPEN)
                        act.activation(work[:, 4, :], ob[e][:, :], ACT.Copy).then_inc(o_read[e], 1)
                        act.wait_ge(o_read[e], Nth(FOX_HEADS // 2, it, 1).n(1) + OPEN)
                        act.activation(work[:, 5, :], work[:, 4, :], ACT.Square).then_inc(sub_sq, 1)
                        act.wait_ge(sub_var, m.n(1))
                        own_u = Nth(STAGES["subln"][1] + e, it, 2)
                        act.activation(work[:, 5, :], bank[e][:, :], ACT.Ln, bias=small[:, 46:47], scale=1.0 / P).then_inc(bank_read[e], 1)
                        act.wait_ge(bank_read[e], own_u.round(2, 1))
                        act.activation(work[:, 5, :], work[:, 5, :], ACT.Exp, scale=-0.5).then_inc(sub_rs, 1)
                        act.wait_ge(sub_n, m.n(1))
                        act.activation(XH[:, bass.ds(it * 2 + e, 1), :], work[:, 4:5, :], ACT.Copy).then_inc(sub_hi, 1)
            highs("out2", 2, 4)
            norm_ln(5, lambda t: pcol("ln_attn_g_2", DT + t), lambda t: pcol("ln_attn_b_2", DT + t))
            conv_hidden("gu2", 2)
            highs("down2", DT // 2 - 1, 8)
            for j in range(7):
                high(Nth(STAGES["down2"][0] + 8 * (DT // 2 - 1) + j + 1))
            norm_ln(6, lambda t: pcol("ln_ffn_g_2", DT + t), lambda t: pcol("ln_ffn_b_2", DT + t), split=False)

        @block.vector
        def _(dve):
            own = Chain(dve, dv)

            def add_squares(x, count):
                own.link(dve.tensor_tensor(tmp[0], x, x, ALU.mult))
                dve.tensor_tensor(ssq, ssq, tmp[0], ALU.add).then_inc(*count)

            def clear_sums():
                own.did(dve.memset(ssum, 0.0))
                own.link(dve.memset(ssq, 0.0))

            clear_sums()
            for t in range(DT):
                dve.wait_ge(turned_x, t + 1)
                dve.tensor_copy(xres[:, t, :], bank[t % 2][:, :]).then_inc(bank_read[t % 2], 1)
                dve.wait_ge(bank_read[t % 2], t // 2 + 1)
                if t:
                    dve.wait_ge(sum_tiles, t)
                add_squares(xres[:, t, :], (sum_tiles, 1))
            dve.wait_ge(turned_par, 1)
            for i, n in enumerate(ROWS_OF):
                own.did(dve.tensor_copy(par[:, i * P:i * P + n], tb[i // 4][:, i % 4 * P:i % 4 * P + n]))
            own.sync()
            dve.memset(small[:, 46:47], SUB_EPS).then_inc(par_ok, 1)
            dve.tensor_scalar(small[:, 47:48], pcol("b_subln_g_2", 0), 1.0 - LAMBDA_INIT, None, ALU.mult).then_inc(par_ok, 1)

            def moments(centred, var, width, eps):
                if centred:
                    own.link(dve.tensor_scalar(mean, sc[1][:, :], 1.0 / width, None, ALU.mult))
                    own.link(dve.tensor_tensor(tmp[0], mean, mean, ALU.mult))
                    own.link(dve.scalar_tensor_tensor(out=tmp[1], in0=sc[0][:, :], scalar=1.0 / width, in1=tmp[0],
                                                      op0=ALU.mult, op1=ALU.subtract))
                    own.link(dve.tensor_scalar(tmp[1], tmp[1], 0.0, eps, ALU.max, ALU.add))
                else:
                    own.link(dve.tensor_scalar(tmp[1], sc[0][:, :], 1.0 / width, eps, ALU.mult, ALU.add))
                dve.reciprocal(tmp[1], tmp[1]).then_inc(var, 1)
                clear_sums()

            def norm(m, scale, centred, in_place):
                dve.wait_ge(stats_done, m + 1)
                moments(centred, var_ready, D, LN_EPS if centred else RMS_EPS)
                dve.wait_ge(rstd_ready, m + 1)
                if centred:
                    own.link(dve.tensor_tensor(mean, mean, rstd, ALU.mult))
                for t in range(DT):
                    if t >= 2 and not in_place:
                        if m == 6:
                            dve.wait_ge(x_hi, DT * m + t - 1)
                        else:
                            dve.wait_ge(x_lo, DT * m + t - 1)
                    if centred:
                        own.link(dve.tensor_tensor(tmp[t % 2], xres[:, t, :], rstd, ALU.mult))
                        dve.tensor_tensor(tmp[t % 2], tmp[t % 2], mean, ALU.subtract).then_inc(xn_ready, 1)
                    else:
                        dst = xres[:, t, :] if in_place else tmp[t % 2]
                        dve.scalar_tensor_tensor(out=dst, in0=xres[:, t, :], scalar=pcol(scale, t), in1=rstd,
                                                 op0=ALU.mult, op1=ALU.mult).then_inc(xn_ready, 1)

            norm(0, "g_mix", False, False)
            dve.wait_ge(consts, CONSTS)
            dve.reciprocal(icnt[:, :], cnts[:, :]).then_inc(cv_n, 1)
            for c in range(CT):
                n = 2 * c + 1
                dve.wait_ge(item_done, n + 1)
                dve.wait_ge(bank_read[0], (DT + 2 * c) // 2 + 1)
                dve.scalar_tensor_tensor(out=upad[:, c, TAPS - 1:], in0=bank[1][:, :], scalar=pcol("b_in", c),
                                         in1=sig[:, c % 2, :], op0=ALU.add, op1=ALU.mult).then_inc(bank_read[1], 1)
                dve.wait_ge(bank_read[1], (DT + 2 * c + 1) // 2 + 1)
                own.link(dve.tensor_scalar(vconv[:, c, :], upad[:, c, 0:S], tap(0, c), pcol("b_dw", c), ALU.mult, ALU.add))
                for j in range(1, TAPS):
                    own.link(dve.scalar_tensor_tensor(out=vconv[:, c, :], in0=upad[:, c, j:j + S], scalar=tap(j, c),
                                                      in1=vconv[:, c, :], op0=ALU.mult, op1=ALU.add))
                if c:
                    dve.wait_ge(cv_sum, c)
                own.did(dve.tensor_tensor(ssum, ssum, vconv[:, c, :], ALU.add))
                add_squares(vconv[:, c, :], (cv_sum, 1))
            dve.wait_ge(cv_stats, 1)
            moments(True, cv_var, C_CONV, LN_EPS)
            dve.wait_ge(cv_rstd, 1)
            own.link(dve.tensor_tensor(mean, mean, rstd, ALU.mult))
            for c in range(CT):
                own.link(dve.tensor_tensor(vconv[:, c, :], vconv[:, c, :], rstd, ALU.mult))
                dve.tensor_tensor(vconv[:, c, :], vconv[:, c, :], mean, ALU.subtract).then_inc(cv_n, 1)

            def residual(name, m, items_of_tile, factor, centred):
                per = (2 if centred else 1) * 2
                with own.loop(DT // 2, per) as it:
                    for j in range(2):
                        last = Nth(STAGES[name][0] + (j + 1) * items_of_tile - 1, it, 2 * items_of_tile)
                        u = Nth(STAGES[name][1] + j, it, 2)
                        r = xres[:, bass.ds(it * 2 + j, 1), :]
                        dve.wait_ge(item_done, last.n(1))
                        dve.scalar_tensor_tensor(out=r, in0=r, scalar=factor, in1=bank[j][:, :].rearrange("p (a s) -> p a s", a=1),
                                                 op0=ALU.mult, op1=ALU.add).then_inc(bank_read[j], 1)
                        dve.wait_ge(bank_read[j], u.round(2, 1))
                        dve.wait_ge(sum_tiles, Nth(DT * m + j, it, 2).n())
                        if centred:
                            own.did(dve.tensor_tensor(work[:, 2:3, :], work[:, 2:3, :], r, ALU.add))
                        own.link(dve.tensor_tensor(work[:, 0:1, :], r, r, ALU.mult))
                        dve.tensor_tensor(ssq, ssq, tmp[0], ALU.add).then_inc(sum_tiles, 1)

            residual("out", 1, 1, 1.0, False)
            norm(1, "g_ffn", False, False)
            with dve.Fori(0, FT // 2) as it:
                for j in range(2):
                    g, u = Nth(STAGES["gu0"][0] + 2 * j + 1, it, 4), Nth(STAGES["gu0"][1] + 2 * j, it, 4)
                    dve.wait_ge(item_done, g.n(1))
                    dve.wait_ge(bank_read[0], u.round(2, 1))
                    dve.wait_ge(h_lo[j], Nth(j, it, 2).round(2) + OPEN)
                    dve.tensor_tensor(hid[:, j, :], bank[1][:, :], act_g[:, j, :], ALU.mult).then_inc(bank_read[1], 1)
            residual("down0", 2, len(DOWN), 1.0, False)
            norm(2, "g_final", False, True)
            dve.wait_ge(gate_done, 1)
            z, e = tmp[0][0:FOX_HEADS, :], tmp[1][0:FOX_HEADS, :]
            own.link(dve.tensor_scalar(z, sc[0][0:FOX_HEADS, :], small[0:FOX_HEADS, 48:49], None, ALU.add))
            dve.scalar_tensor_tensor(out=e, in0=z, scalar=-1.0, in1=z, op0=ALU.mult, op1=ALU.min).then_inc(gate_a, 1)
            own.link(dve.tensor_scalar(z, z, 0.0, None, ALU.min))
            dve.wait_ge(gate_b, 2)
            own.link(dve.tensor_tensor(e, e, z, ALU.subtract))
            own.link(dve.memset(rstd[0:FOX_HEADS, :], 1.0))
            own.link(dve.tensor_tensor_scan(z, rstd[0:FOX_HEADS, :], e, 0.0, ALU.mult, ALU.add))
            dve.wait_ge(cc_zero, 1)
            for e in range(2):
                h, at = slice(64 * e, 64 * e + 64), 65 * e
                own.did(dve.tensor_tensor(hot[h, :], ident[h, at:at + FOX_HEADS:2],
                                          ident[h, at + 32:at + 32 + FOX_HEADS:2], ALU.add))
            high_c = PTH[0:FOX_HEADS, 0, 0, :]
            own.link(dve.tensor_copy(high_c, z))
            for r in range(0, P, 64):
                dve.tensor_copy(CC[r:r + FOX_HEADS, :], high_c.bitcast(F32)).then_inc(cc_ready, 1)
                dve.tensor_tensor(CC[r + 32:r + 32 + FOX_HEADS, :], z, high_c.bitcast(F32), ALU.subtract).then_inc(cc_ready, 1)
            dve.tensor_copy(onesr[:, :], ones[:, :]).then_inc(cc_ready, 1)
            dve.wait_ge(cc_ready, 5)

            def values_back(before):
                with dve.Fori(0, 2) as it:
                    for j in range(4):
                        dve.wait_ge(v_turned[j % 2], Nth(before + j, it, 4).round(2, 1) + OPEN)
                        dve.tensor_copy(QKV[:, bass.ds(it * 4 + (2 * DT + j), 1), :],
                                        tb[j % 2][:, :].rearrange("p (a s) -> p a s", a=1)).then_inc(v_out[j % 2], 1)

            values_back(0)

            def row_max(b, used, i, col):
                dve.wait_ge(s_done[b], used.n(1))
                dve.tensor_reduce(small[:, col:col + 1], sc[b][:, 0:(i + 1) * P], AX_X, ALU.max, negate=True).then_inc(mx[b], 1)

            def map_lo(b, used, e, i):
                dve.wait_ge(pt_h[b], used.n(1))
                dst = PTL[:, e, 0:i + 1, i * P:(i + 1) * P]
                dve.tensor_tensor(dst, tb[b][:, 0:(i + 1) * P].rearrange("p (j q) -> p j q", q=P),
                                  PTH[:, e, 0:i + 1, i * P:(i + 1) * P].bitcast(F32), ALU.subtract).then_inc(pt_l[b], 1)

            with own.loop(FOX_HEADS // 4, 4 * QT) as it:
                steps = [(s, e, i) for s in range(2) for e in range(2) for i in range(QT)]

                def used_of(s, e, i):
                    return Nth(2 * (2 * s + e) + i // 2, it, 8)
                for n in range(len(steps) + 3):
                    if n < len(steps):
                        s, e, i = steps[n]
                        if e == 0 and i == 0:
                            dve.wait_ge(o_done[s][1], Nth(0, it, 1).n() + OPEN)
                            dve.tensor_scalar(Cm[:, s, :], CC, hot[:, bass.ds(it * 2 + s, 1)], None, ALU.mult).then_inc(cm_ready, 1)
                        row_max(i % 2, used_of(s, e, i), i, i % 2)
                    if 1 <= n <= len(steps):
                        s, e, i = steps[n - 1]
                        b = i % 2
                        dve.wait_ge(ex[b], used_of(s, e, i).n(1) + OPEN)
                        own.link(dve.reciprocal(small[:, 12 + b:13 + b], small[:, 2 + b:3 + b]))
                        dve.tensor_scalar(pmap[:, b, 0:(i + 1) * P], pmap[:, b, 0:(i + 1) * P], small[:, 12 + b:13 + b],
                                          None, ALU.mult).then_inc(pn[b], 1)
                    if 2 <= n <= len(steps) + 1:
                        s, e, i = steps[n - 2]
                        map_lo(i % 2, used_of(s, e, i), e, i)
                    if n >= 3 and steps[n - 3][2] == QT - 1:
                        s, e, _ = steps[n - 3]
                        r = slice(HEAD * e, HEAD * e + HEAD)
                        dve.wait_ge(o_hi, Nth(2 * s + e, it, 4).n(1))
                        dve.tensor_tensor(XL[r, bass.ds(it * 2 + s, 1), :], ob[e][r, :].rearrange("p (a s) -> p a s", a=1),
                                          XH[r, bass.ds(it * 2 + s, 1), :].bitcast(F32), ALU.subtract).then_inc(o_read[e], 1)
            clear_sums()
            residual("out1", 3, 1, ALPHA, True)
            norm(3, None, True, False)

            def conv_hidden(name, layer):
                with own.loop(FT // 2, 4) as it:
                    for j in range(2):
                        for side, dst in ((0, act_g), (1, hid)):
                            n = it * 2 + (j + FT * side)
                            h = Nth(FT * (layer - 1) + j, it, 2)
                            dve.wait_ge(ff_lin[side], h.n(1))
                            own.link(dve.scalar_tensor_tensor(
                                out=dst[:, j, 1:], in0=bank[side][:, 0:S - 1], scalar=ff_par(layer - 1, 1, n),
                                in1=dst[:, j, 1:], op0=ALU.mult, op1=ALU.add))
                            dve.scalar_tensor_tensor(
                                out=dst[:, j, 2:], in0=bank[side][:, 0:S - 2], scalar=ff_par(layer - 1, 0, n),
                                in1=dst[:, j, 2:], op0=ALU.mult, op1=ALU.add).then_inc(bank_read[side], 1)
                        dve.wait_ge(bank_read[1], Nth(STAGES[name][1] + 2 * j + 1, it, 4).round(2, 1))
                        dve.wait_ge(g_act, h.n(1))
                        dve.tensor_tensor(hid[:, j, :], hid[:, j, :], act_g[:, j, :], ALU.mult).then_inc(hid_ready[j], 1)

            conv_hidden("gu1", 1)
            residual("down1", 4, len(DOWN), ALPHA, True)
            norm(4, None, True, False)
            dve.wait_ge(rope_in, 32)
            for part in range(2):
                scale = HEAD ** -0.5 if part == 0 else 1.0
                with own.loop(2, 4) as it:
                    for j in range(4):
                        n = Nth(8 * part + j, it, 4)
                        u = n + STAGES["qkv2"][1]
                        t = QKV[:, bass.ds(it * 4 + (8 * part + j), 1), :]
                        dve.wait_ge(rot_ready, it * 16 + 4 * (8 * part + j + 1))
                        dve.scalar_tensor_tensor(out=t, in0=bank[j % 2][:, :].rearrange("p (a s) -> p a s", a=1), scalar=scale,
                                                 in1=rope[:, 0:1, :], op0=ALU.mult, op1=ALU.mult).then_inc(bank_read[j % 2], 1)
                        own.link(dve.scalar_tensor_tensor(out=tmp[j % 2], in0=tmp[j % 2], scalar=scale, in1=rope[:, 1, :],
                                                          op0=ALU.mult, op1=ALU.mult))
                        dve.wait_ge(bank_read[j % 2], u.round(2, 1))
                        dve.tensor_tensor(t, t, work[:, j % 2:j % 2 + 1, :], ALU.add).then_inc(roped[j % 2], 1)
            values_back(DT)
            for k in range(2):
                own.link(dve.tensor_tensor(lamr[:, 2 * k * HEAD:(2 * k + 1) * HEAD], lamr[:, 2 * k * HEAD:(2 * k + 1) * HEAD],
                                           lamr[:, (2 * k + 1) * HEAD:(2 * k + 2) * HEAD], ALU.mult))
                ins = dve.tensor_reduce(lam_row[0][:, k:k + 1], lamr[:, 2 * k * HEAD:(2 * k + 1) * HEAD], AX_X, ALU.add)
                if k == 0:
                    own.link(ins)
                else:
                    ins.then_inc(lam_c, 1)
            dve.wait_ge(lam_c, 2)
            own.link(dve.tensor_tensor(lam_row[2], lam_row[1][:, 0:1], lam_row[1][:, 1:2], ALU.subtract))
            dve.tensor_scalar(lam_row[2], lam_row[2], LAMBDA_INIT, None, ALU.add).then_inc(lam_a, 1)
            dve.wait_ge(lam_b, 1)
            dve.tensor_copy(small[:, 49:50], sc[0][:, 0:1]).then_inc(lam_d, 1)
            dve.wait_ge(lam_d, 1)

            with own.loop(DIFF_HEADS // 2, 2 * QT * 4 + 0) as it:
                steps = [(e, i) for e in range(2) for i in range(QT)]
                for n in range(len(steps) + 3):
                    if n < len(steps):
                        e, i = steps[n]
                        for c in range(2):
                            row_max(c, Nth(2 * FOX_HEADS + n, it, 8), i, 4 + 2 * (i % 2) + c)
                    if 1 <= n <= len(steps):
                        e, i = steps[n - 1]
                        b, k = i % 2, (i + 1) * P
                        r = 12 + 2 * b
                        for c in range(2):
                            dve.wait_ge(ex[c], Nth(2 * FOX_HEADS + n - 1, it, 8).n(1) + OPEN)
                            own.did(dve.reciprocal(small[:, r + c:r + c + 1], small[:, 8 + 2 * b + c:9 + 2 * b + c]))
                        own.sync()
                        own.link(dve.tensor_tensor(small[:, r + 1:r + 2], small[:, r + 1:r + 2], small[:, 49:50], ALU.mult))
                        own.link(dve.tensor_scalar(pmap[:, 2 * b + 1, 0:k], pmap[:, 2 * b + 1, 0:k], small[:, r + 1:r + 2], None, ALU.mult))
                        dve.scalar_tensor_tensor(out=pmap[:, 2 * b, 0:k], in0=pmap[:, 2 * b, 0:k], scalar=small[:, r:r + 1],
                                                 in1=pmap[:, 2 * b + 1, 0:k], op0=ALU.mult, op1=ALU.subtract).then_inc(pn[b], 1)
                    if 2 <= n <= len(steps) + 1:
                        e, i = steps[n - 2]
                        map_lo(i % 2, Nth(2 * FOX_HEADS + (n - 2) // 2, it, 4), e, i)
                    if n >= 3 and steps[n - 3][1] == QT - 1:
                        e, _ = steps[n - 3]
                        dve.wait_ge(sub_rs, Nth(e, it, 2).n(1))
                        dve.scalar_tensor_tensor(out=work[:, 4, :], in0=work[:, 4, :], scalar=small[:, 47:48], in1=work[:, 5, :],
                                                 op0=ALU.mult, op1=ALU.mult).then_inc(sub_n, 1)
            clear_sums()
            residual("out2", 5, 1, ALPHA, True)
            norm(5, None, True, False)
            conv_hidden("gu2", 2)
            residual("down2", 6, len(DOWN), ALPHA, True)
            norm(6, None, True, False)
            for n in range(2 * QT):
                u = Nth(STAGES["back"][1] + n)
                dve.wait_ge(y_turned, n + 1)
                dve.tensor_copy(QKV[:, n, :], bank[u.slot(2)][:, :]).then_inc(bank_read[u.slot(2)], 1)


PAR_LOADS = len(ROWS0) + 1 + 8
CONSTS = 3 + 2 * CT + 2 + PAD + 1 + 3


def rope_tables():
    inv = (1.0 / (np.float32(10000.0) ** (np.arange(0, HEAD, 2, dtype=np.float32) / np.float32(HEAD)))).astype(np.float32)
    ang = (np.arange(S, dtype=np.float32)[None, :] * inv[:, None]).astype(np.float32)
    cos, sin = np.cos(ang).astype(np.float32), np.sin(ang).astype(np.float32)
    return np.stack([np.concatenate([cos, cos, cos, cos]), np.concatenate([-sin, sin, -sin, sin])])


NAMES = ["x", "g_mix", "w_in", "b_in", "w_dw", "b_dw", "ln_g", "ln_b", "w_pool", "s_pool", "w_out", "g_ffn",
         "w_gate", "w_up", "w_down", "g_final", "a_w_in_2", "a_b_f_2", "a_w_out_2", "kv_w_2", "b_w_q_2",
         "b_lambda_2", "b_subln_g_2", "b_w_out_2", "ffn_w_in_2", "ffn_conv_w_2", "ffn_conv_b_2",
         "ffn_w_out_2", "ln_attn_g_2", "ln_attn_b_2", "ln_ffn_g_2", "ln_ffn_b_2"]


def kernel(**inputs):
    import concourse.bacc as bacc
    from concourse.bass_utils import run_bass_kernel_spmd

    nc = bacc.Bacc("TRN2", target_bir_lowering=False, num_devices=1)
    arrays = {name: np.ascontiguousarray(inputs[name]) for name in NAMES}
    arrays["rope"] = rope_tables()
    dram = {name: nc.dram_tensor(f"in_{name}", a.shape, mybir.dt.from_np(a.dtype), kind="ExternalInput").ap()
            for name, a in arrays.items()}
    out = nc.dram_tensor("y", (1, S, D), F32, kind="ExternalOutput").ap()
    two_blocks(nc, dram, out)
    r = run_bass_kernel_spmd(nc, [{f"in_{name}": a for name, a in arrays.items()}], core_ids=[0])
    return r.results[0]["y"]
```

```python
from contextlib import ExitStack, contextmanager

import numpy as np
import concourse.bass as bass
from concourse import mybir

P = 128
S = 512
D = 1024
DT = D // P
QT = S // P
C_CONV = 512
CT = C_CONV // P
TAPS = 31
WINDOWS = (2, 4, 8, 16)
PAD = 16
D_FF = 2816
FT = D_FF // P
FF_TAPS = 3
HEAD = 64
FOX_HEADS = D // HEAD
DIFF_HEADS = D // (2 * HEAD)
CHUNK = 64
RMS_EPS, LN_EPS, SUB_EPS = 1e-6, 1e-5, 1e-5
ALPHA = 4.0 ** 0.25
LAMBDA_INIT = 0.8 - 0.6 * float(np.exp(-0.3))
MASKED = -1.0e30
UNITS = DT
UNIT = (8, 8, 4, 4)
LN_EXP_SET = 6
DOWN = (6, 6, 5, 5)
assert sum(DOWN) == FT

F32 = mybir.dt.float32
F32R = mybir.dt.float32r
BF16 = mybir.dt.bfloat16
ALU = mybir.AluOpType
ACT = mybir.ActivationFunctionType
AX_X = mybir.AxisListType.X

OPEN = 1
RAW = 4
SPLIT = 2

STAGES = {}
_item, _turn = 0, DT
for _name, _n, _t in (("in", 12, 12), ("out", 8, 8), ("gu0", 2 * FT, 2 * FT), ("down0", 8 * len(DOWN), 8),
                      ("qkv1", 4 * UNITS, 4 * UNITS), ("out1", 8, 8), ("gu1", 2 * FT, 2 * FT),
                      ("down1", 8 * len(DOWN), 8), ("qkv2", 4 * UNITS, 4 * UNITS), ("out2", 8, 8),
                      ("gu2", 2 * FT, 2 * FT), ("down2", 8 * len(DOWN), 8), ("back", 0, 8)):
    STAGES[_name] = (_item, _turn)
    _item, _turn = _item + _n, _turn + _t
ITEMS = _item
IN_ORDER = [("gate", 0), ("value", 0), ("pool", 0), ("pool", 1), ("gate", 1), ("value", 1),
            ("gate", 3), ("value", 3), ("gate", 2), ("value", 2), ("pool", 2), ("pool", 3)]
PE_TILE = 3
DIAG_CHUNK = 8
SIZES = {"down0": 2 * DOWN, "down1": 2 * DOWN, "down2": 2 * DOWN}

ROWS0 = {}
_row = 0
for _name, _n in (("g_mix", 8), ("b_in", 12), ("b_dw", 4), ("ln_g", 4), ("ln_b", 4), ("s_pool", 4),
                  ("g_ffn", 8), ("g_final", 8), ("ln_attn_g_2", 16), ("ln_attn_b_2", 16),
                  ("ln_ffn_g_2", 16), ("ln_ffn_b_2", 16), ("b_subln_g_2", 1)):
    ROWS0[_name] = (_row, _n)
    _row += _n
ROWS_OF = [_row, TAPS * CT, 2 * 44, 2 * 44, 2 * 44, 2 * 44]


class Nth:

    def __init__(self, base, it=0, per=0):
        if isinstance(it, int):
            base, it, per = base + it * per, 0, 0
        self.base, self.it, self.per = base, it, per

    def __add__(self, k):
        return Nth(self.base + k, self.it, self.per)

    def times(self, m, k=0):
        return Nth(self.base * m + k, self.it, self.per * m)

    def n(self, k=0):
        return self.base + k if isinstance(self.it, int) else self.it * self.per + (self.base + k)

    def slot(self, size):
        assert self.per % size == 0
        return self.base % size

    def round(self, size, k=0):
        if isinstance(self.it, int):
            return self.base // size + k
        assert self.per % size == 0
        return self.it * (self.per // size) + (self.base // size + k)


class Chain:

    def __init__(self, eng, sem):
        self.eng, self.sem, self.count, self.it, self.per = eng, sem, 0, None, 0

    def did(self, ins):
        ins.then_inc(self.sem, 1)
        self.count += 1

    def sync(self):
        if self.it is None:
            self.eng.wait_ge(self.sem, self.count)
        else:
            self.eng.wait_ge(self.sem, self.it * self.per + self.count)

    def link(self, ins):
        self.did(ins)
        self.sync()

    @contextmanager
    def loop(self, times, per):
        start = self.count
        with self.eng.Fori(0, times) as it:
            self.it, self.per = it, per
            yield it
            assert self.count - start == per, (self.count - start, per)
        self.count, self.it = start + per * times, None


def two_blocks(nc, A, out):
    ctx = ExitStack()
    with ctx:
        def sb(name, shape, dt=F32, stack=None):
            return (stack or ctx).enter_context(nc.sbuf_tensor(name, shape, dt))

        def pb(name, dt=F32):
            return ctx.enter_context(nc.psum_tensor(name, [P, 512], dt))

        def sem(name):
            return ctx.enter_context(nc.semaphore(name))

        def sems(name, n):
            return [sem(f"{name}{i}") for i in range(n)]

        xres = sb("xres", [P, DT, S])
        XH = sb("XH", [P, DT, S], F32R)
        XL = sb("XL", [P, DT, S], F32R)
        raw = sb("raw", [P, RAW, DT, P])
        WH = sb("WH", [P, SPLIT, DT, P], F32R)
        WL = sb("WL", [P, SPLIT, DT, P], F32R)
        par = sb("par", [P, 6 * P])
        ident = sb("ident", [P, P])
        ones = sb("ones", [P, P])
        identb = sb("identb", [P, P], BF16)
        masks = sb("masks", [P, 2, P], BF16)
        work = sb("work", [P, 6, S])
        small = sb("small", [P, 96])
        tmp = [work[:, 0, :], work[:, 1, :]]
        ssum, ssq, rstd, mean = (work[:, i, :] for i in (2, 3, 4, 5))

        first = ExitStack()
        xin = sb("xin", [P, QT, D], stack=first)
        prow = sb("prow", [P, 6, P], stack=first)
        upad = sb("upad", [P, CT, TAPS - 1 + S], stack=first)
        sig = sb("sig", [P, 2, S], stack=first)
        vconv = sb("vconv", [P, CT, S], stack=first)
        ppad = sb("ppad", [P, CT, PAD + S], stack=first)
        psums = sb("psums", [P, 2, PAD + S], stack=first)
        ypool = sb("ypool", [P, CT, S], stack=first)
        wpool = sb("wpool", [P, CT, P], stack=first)
        mixp = sb("mixp", [P, 2, S], stack=first)
        tap_h = sb("tap_h", [P, TAPS], F32R, stack=first)
        tap_l = sb("tap_l", [P, TAPS], stack=first)
        dg_h = sb("dg_h", [P, TAPS, P], F32R, stack=first)
        dg_l = sb("dg_l", [P, TAPS, P], F32R, stack=first)
        u_h = sb("u_h", [P, TAPS - 1 + S], F32R, stack=first)
        u_l = sb("u_l", [P, TAPS - 1 + S], F32R, stack=first)
        cnts = sb("cnts", [P, PAD], stack=first)
        icnt = sb("icnt", [P, PAD], stack=first)
        first.close()
        ffn = ExitStack()
        HH = sb("HH", [P, FT, S], F32R, stack=ffn)
        HL = sb("HL", [P, FT, S], F32R, stack=ffn)
        act_g = sb("act_g", [P, 2, S], stack=ffn)
        hid = sb("hid", [P, 2, S], stack=ffn)
        ffn.close()
        att = ExitStack()
        QKH = sb("QKH", [P, 2, 2, S], F32R, stack=att)
        QKL = sb("QKL", [P, 2, 2, S], F32R, stack=att)
        VH = sb("VH", [P, 2, S], F32R, stack=att)
        VL = sb("VL", [P, 2, S], F32R, stack=att)
        PTH = sb("PTH", [P, 2, QT, S], F32R, stack=att)
        PTL = sb("PTL", [P, 2, QT, S], F32R, stack=att)
        OH = sb("OH", [P, DT, S], F32R, stack=att)
        OL = sb("OL", [P, DT, S], F32R, stack=att)
        pmap = sb("pmap", [P, 4, S], stack=att)
        Cm = sb("Cm", [P, 2, S], F32R, stack=att)
        wf = sb("wf", [P, DT, FOX_HEADS], stack=att)
        hot = sb("hot", [P, FOX_HEADS // 2], stack=att)
        onesr = sb("onesr", [P, P], F32R, stack=att)
        rope = sb("rope", [P, 2, S], stack=att)
        lamr = sb("lamr", [1, 4 * HEAD], stack=att)
        att.close()
        vt = work[:, 0, :]
        rot = work[:, 1, :]
        qk = work[:, 2, :]
        osb = work[:, 3, :]
        osq = work[:, 4, :]
        CC = work[:, 5, :]
        back = ExitStack()
        yout = sb("yout", [P, 2 * QT, S], stack=back)
        back.close()
        lam_row = [small[0:1, 40:42], small[0:1, 42:44], small[0:1, 44:45]]

        bank = [pb("bank0"), pb("bank1")]
        sc = [pb("score0"), pb("score1")]
        tb = [pb("turned0"), pb("turned1")]
        ob = [pb("attended0"), pb("attended1")]

        x_in = sem("x_in")
        rows0_in = sem("rows0_in")
        par_in = sem("par_in")
        small_in = sem("small_in")
        wf_in = sem("wf_in")
        rope_in = sem("rope_in")
        w_landed = sems("w_landed", RAW)
        first_map = sem("first_map")
        w_hi = sem("w_hi")
        w_lo = sem("w_lo")
        item_done = sem("item_done")
        bank_read = sems("bank_read", 2)
        consts = sem("consts")
        turned_x = sem("turned_x")
        turned_par = sem("turned_par")
        par_ok = sem("par_ok")
        dv = sem("dv")
        av = sem("av")
        gv = sem("gv")
        sum_tiles = sem("sum_tiles")
        stats_done = sem("stats_done")
        var_ready = sem("var_ready")
        rstd_ready = sem("rstd_ready")
        xn_ready = sem("xn_ready")
        x_hi = sem("x_hi")
        x_lo = sem("x_lo")
        cv_sum = sem("cv_sum")
        cv_stats, cv_var, cv_rstd = sem("cv_stats"), sem("cv_var"), sem("cv_rstd")
        cv_n, cv_hi, cv_lo = sem("cv_n"), sem("cv_hi"), sem("cv_lo")
        squared = sem("squared")
        taps_split = sem("taps_split")
        diag_h, diag_l = sem("diag_h"), sem("diag_l")
        u_hi, u_lo = sem("u_hi"), sem("u_lo")
        pe_conv = sem("pe_conv")
        pe_conv_out = sem("pe_conv_out")
        ypool_ready, pool_mm = sem("ypool_ready"), sem("pool_mm")
        pool_out, pool_hi, pool_lo = sem("pool_out"), sem("pool_hi"), sem("pool_lo")
        h_hi = sem("h_hi")
        h_lo = sems("h_lo", 2)
        g_act = sem("g_act")
        ff_lin = sems("ff_lin", 2)
        gate_done = sem("gate_done")
        gate_a, gate_b = sem("gate_a"), sem("gate_b")
        cc_zero = sem("cc_zero")
        hid_ready = sems("hid_ready", 2)
        roped = sem("roped")
        rot_ready = sem("rot_ready")
        cc_ready = sem("cc_ready")
        cm_ready = sem("cm_ready")
        v_turned = sem("v_turned")
        v_hi = sem("v_hi")
        qk_hi = sem("qk_hi")
        qk_lo = sem("qk_lo")
        s_done = sems("s_done", 2)
        mx = sems("mx", 2)
        ex = sems("ex", 2)
        pn = sems("pn", 2)
        t_done = sems("t_done", 2)
        pt_h, pt_l = sems("pt_h", 2), sems("pt_l", 2)
        o_done = sems("o_done", 2)
        o_hi = sem("o_hi")
        o_read = sems("o_read", 2)
        lam_a, lam_b, lam_c, lam_d = (sem(f"lam_{x}") for x in "abcd")
        sub_sq, sub_var, sub_ln, sub_rs, sub_n, sub_hi, sub_lo = (
            sem(x) for x in ("sub_sq", "sub_var", "sub_ln", "sub_rs", "sub_n", "sub_hi", "sub_lo"))
        y_turned = sem("y_turned")
        y_out = sem("y_out")

        slots = [*h_lo, *hid_ready, *ex, *pt_l, *o_read, qk_lo, sub_lo]

        def pcol(name, t):
            return par[:, ROWS0[name][0] + t:ROWS0[name][0] + t + 1]

        def tap(j, c):
            return par[:, P + j * CT + c:P + j * CT + c + 1]

        def in_item(kind, c):
            return IN_ORDER.index((kind, c))

        def turned_rows(i):
            return ob[1][:, 0:ROWS_OF[0]] if i == 0 else tb[i // 4][:, i % 4 * P:i % 4 * P + ROWS_OF[i]]

        def ff_par(layer, what, n):
            return par[:, bass.ds(n + ((2 + 2 * layer + what // 2) * P + (what % 2) * 44), 1)]

        def cols(w):
            return w.rearrange("(k p) n -> p k n", p=P)

        w_in, w_out0 = cols(A["w_in"][0]), cols(A["w_out"][0])
        w_gate, w_up = cols(A["w_gate"][0]), cols(A["w_up"][0])
        a_in, a_out = cols(A["a_w_in_2"][0]), cols(A["a_w_out_2"][0])
        kv_w, b_q, b_out = cols(A["kv_w_2"]), cols(A["b_w_q_2"][0]), cols(A["b_w_out_2"][0])
        ff_in = [cols(A["ffn_w_in_2"][i]) for i in range(2)]
        downs = [cols(A["w_down"][0])] + [cols(A["ffn_w_out_2"][i]) for i in range(2)]

        def loop_with_sizes(name, per):
            own_sizes = SIZES.get(name, (DT,) * per)
            return [own_sizes[j + 2] if j + 2 < per else max(own_sizes[j + 2 - per], DT) for j in range(per)]

        def at(u):
            return bass.ds(u.n(), 1)

        def weave_units(Fori, part):
            part(Nth(0), None)
            part(Nth(1), Nth(0))
            with Fori(0, (UNITS - 2) // 2) as it:
                for j in range(2):
                    part(Nth(2 + j, it, 2), Nth(1 + j, it, 2))
            part(None, Nth(UNITS - 1))

        block = ctx.enter_context(nc.Block())

        @block.sync
        def _(sp):
            def load(g, src, kt=DT):
                if not (isinstance(g.it, int) and g.base < RAW):
                    sp.wait_ge(w_lo, g.n(1 - RAW))
                sp.dma_start(raw[:, g.slot(RAW), 0:kt, 0:src.shape[2]], src).then_inc(w_landed[g.slot(RAW)], 16)

            def stage(name, times, per, source):
                with sp.Fori(0, times) as it:
                    for j in range(per):
                        load(Nth(STAGES[name][0] + j, it, per), *source(it, j))

            xv = A["x"][0].rearrange("(q p) d -> p q d", p=P)
            for q in range(QT):
                sp.dma_start(xin[:, q, :], xv[:, q, :]).then_inc(x_in, 16)
            def load_in(n):
                kind, c = IN_ORDER[n]
                c += {"gate": CT, "value": 0, "pool": 2 * CT}[kind]
                load(Nth(n), w_in[:, :, c * P:(c + 1) * P])

            def rows(i, r, src, signal):
                n = src.shape[0]
                sp.dma_start(prow[r:r + n, i, :], src).then_inc(signal, 16)

            load_in(0)
            load_in(1)
            for name, (r, n) in ROWS0.items():
                src = A[name]
                if len(src.shape) == 1:
                    src = src.rearrange("(t p) -> t p", p=P)
                else:
                    src = src.rearrange("l (t p) -> (l t) p", p=P)
                rows(0, r, src, rows0_in)
            load_in(2)
            load_in(3)
            rows(1, 0, A["w_dw"][0].rearrange("j (c p) -> (j c) p", p=P), par_in)
            for layer in range(2):
                taps = A["ffn_conv_w_2"][layer].rearrange("j (c p) -> j c p", p=P)
                rows(2 + 2 * layer, 0, taps[0], par_in)
                rows(2 + 2 * layer, 44, taps[1], par_in)
                rows(3 + 2 * layer, 0, taps[2], par_in)
                rows(3 + 2 * layer, 44, A["ffn_conv_b_2"][layer].rearrange("(c p) -> c p", p=P), par_in)
            sp.dma_start(wpool[:, :, :], A["w_pool"][0].rearrange("i g h -> g i h")).then_inc(small_in, 16)
            for n in range(4, 12):
                load_in(n)

            def tiles(w, first=0):
                def source(it, j):
                    return (w[:, :, bass.ds(it * 4 * P + (first + j) * P, P)],)
                return source

            def pairs(wa, wb, first_b=0):
                def source(it, j):
                    return ((wa, wb)[j % 2][:, :, bass.ds(it * 2 * P + (j // 2 + (first_b if j % 2 else 0)) * P, P)],)
                return source

            def down(w):
                def source(it, j):
                    k0, kt = sum(DOWN[:j % 4]), DOWN[j % 4]
                    return (w[:, k0:k0 + kt, bass.ds(it * 2 * P + j // 4 * P, P)], kt)
                return source

            stage("out", 2, 4, tiles(w_out0))
            stage("gu0", FT // 2, 4, pairs(w_gate, w_up))
            stage("down0", DT // 2, 8, down(downs[0]))
            sp.wait_ge(item_done, STAGES["qkv1"][0])
            sp.dma_start(wf[:, :, :], a_in[:, :, 3 * D:3 * D + FOX_HEADS]).then_inc(wf_in, 16)
            sp.dma_start(small[0:FOX_HEADS, 48:49], A["a_b_f_2"].rearrange("o h -> h o")).then_inc(wf_in, 16)
            def units(name, wq, wk, wv):
                with sp.Fori(0, UNITS) as it:
                    for j in range(4):
                        g = Nth(STAGES[name][0] + j, it, 4)
                        if j < 2 and name == "qkv2":
                            src = (wq, wk)[j]
                            sp.wait_ge(w_lo, g.n(1 - RAW))
                            sp.dma_start(raw[:, g.slot(RAW), :, 0:HEAD],
                                         src[:, :, bass.ds(it * HEAD, HEAD)]).then_inc(first_map, 16)
                            sp.wait_ge(first_map, it * 32 + 16 * (j + 1))
                            sp.dma_start(raw[:, g.slot(RAW), :, HEAD:P],
                                         src[:, :, bass.ds(it * HEAD + D // 2, HEAD)]).then_inc(w_landed[g.slot(RAW)], 16)
                        elif j < 2:
                            load(g, (wq, wk)[j][:, :, bass.ds(it * P, P)])
                        else:
                            load(g, wv[:, 4 * (j - 2):4 * (j - 1), bass.ds(it * P, P)], 4)

            units("qkv1", a_in[:, :, 0:D], a_in[:, :, D:2 * D], a_in[:, :, 2 * D:3 * D])
            stage("out1", 2, 4, tiles(a_out))
            stage("gu1", FT // 2, 4, pairs(ff_in[0], ff_in[0], FT))
            stage("down1", DT // 2, 8, down(downs[1]))
            sp.wait_ge(item_done, STAGES["qkv2"][0])
            sp.dma_start(rope[:, :, :], A["rope"].rearrange("a p s -> p a s")).then_inc(rope_in, 16)
            sp.dma_start(lamr[:, :], A["b_lambda_2"].rearrange("o a d -> o (a d)")).then_inc(rope_in, 16)
            units("qkv2", b_q, kv_w[:, :, 0:D], kv_w[:, :, D:2 * D])
            stage("out2", 2, 4, tiles(b_out))
            stage("gu2", FT // 2, 4, pairs(ff_in[1], ff_in[1], FT))
            stage("down2", DT // 2, 8, down(downs[2]))
            ov = out[0].rearrange("(q p) d -> p q d", p=P)
            for q in range(QT):
                for b in range(2):
                    sp.wait_ge(bank_read[b], STAGES["back"][1] // 2 + q + 1)
                sp.dma_start(ov[:, q, :], yout[:, 2 * q:2 * q + 2, :].rearrange("p a s -> p (a s)")).then_inc(y_out, 16)
            sp.wait_ge(y_out, 16 * QT)

        @block.gpsimd
        def _(pool):
            own = Chain(pool, gv)

            def low(g, kt=DT):
                pool.wait_ge(w_hi, g.n(1))
                s = g.slot(SPLIT)
                pool.tensor_tensor(WL[:, s, 0:kt, :], raw[:, g.slot(RAW), 0:kt, :], WH[:, s, 0:kt, :].bitcast(F32),
                                   ALU.subtract).then_inc(w_lo, 1)

            pool.memset(ident[:, :], 0.0).then_inc(consts, 1)
            pool.memset(ones[:, :], 1.0).then_inc(consts, 1)
            pool.wait_ge(consts, 1)
            pool.affine_select(out=ident[:, :], in_=ident[:, :], compare_op=ALU.not_equal, fill=1.0,
                               base=0, pattern=[[-1, P]], channel_multiplier=1).then_inc(consts, 1)
            for c in range(CT):
                pool.memset(ppad[:, c, 0:PAD], 0.0).then_inc(consts, 1)
                pool.memset(upad[:, c, 0:TAPS - 1], 0.0).then_inc(consts, 1)
            for c in range(2):
                pool.memset(psums[:, c, 0:PAD], 0.0).then_inc(consts, 1)
            for c in range(PAD):
                pool.memset(cnts[:, c:c + 1], float(c + 1)).then_inc(consts, 1)
            pool.memset(masks[:, :, :], 0.0).then_inc(consts, 1)
            done = 3 + 2 * CT + 2 + PAD + 1
            pool.wait_ge(consts, done)
            pool.affine_select(out=masks[:, 0, :], in_=masks[:, 0, :], compare_op=ALU.is_ge, fill=MASKED,
                               base=0, pattern=[[-1, P]], channel_multiplier=1).then_inc(consts, 1)
            pool.memset(masks[0:CHUNK, 1, CHUNK:P], MASKED).then_inc(consts, 1)
            pool.tensor_copy(identb[:, :], ident[:, :]).then_inc(consts, 1)
            for n, q in enumerate(slots):
                pool.memset(small[:, 64 + n:65 + n], 0.0).then_inc(q, OPEN)

            def lows_of_x(m, src):
                for t in range(DT):
                    pool.wait_ge(x_hi, DT * m + t + 1)
                    pool.tensor_tensor(XL[:, t, :], src(t), XH[:, t, :].bitcast(F32),
                                       ALU.subtract).then_inc(x_lo, 1)

            low(Nth(0))
            low(Nth(1))
            lows_of_x(0, lambda t: tmp[t % 2])

            def pooled(i):
                w = WINDOWS[i]
                n = in_item("pool", i)
                pool.wait_ge(bank_read[n % 2], (DT + n) // 2 + 1)
                src, d, side = ppad[:, i, :], 1, 0
                while d < w:
                    dst = psums[:, side, :]
                    own.link(pool.tensor_tensor(dst[:, PAD:], src[:, PAD:], src[:, PAD - d:PAD + S - d], ALU.add))
                    src, d, side = dst, 2 * d, 1 - side
                own.did(pool.tensor_tensor(ypool[:, i, 0:w], src[:, PAD:PAD + w], icnt[:, 0:w], ALU.mult))
                own.link(pool.tensor_scalar(ypool[:, i, w:], src[:, PAD + w:], 1.0 / w, None, ALU.mult))
                pool.tensor_tensor(ypool[:, i, :], ypool[:, i, :], ppad[:, i, PAD:], ALU.subtract).then_inc(ypool_ready, 1)

            for n in range(12):
                low(Nth(n + 2))
                if n == 2:
                    pool.wait_ge(taps_split, 2)
                    for a in range(0, TAPS, DIAG_CHUNK):
                        k = min(DIAG_CHUNK, TAPS - a)
                        pool.tensor_tensor(dg_l[:, a:a + k, :], ident[:, :].unsqueeze(1).broadcast_to([P, k, P]),
                                           tap_l[:, a:a + k].unsqueeze(2).broadcast_to([P, k, P]), ALU.mult).then_inc(diag_l, 1)
                    pool.wait_ge(cv_n, 1)
                if n == 5:
                    pooled(0)
                if n == 7:
                    pooled(1)
                if n == 10:
                    pool.wait_ge(u_hi, 1)
                    pool.tensor_tensor(u_l[:, :], upad[:, PE_TILE, :], u_h[:, :].bitcast(F32), ALU.subtract).then_inc(u_lo, 1)
            pooled(2)
            pooled(3)
            for i in range(CT):
                pool.wait_ge(pool_hi, i + 1)
                pool.tensor_tensor(XL[:, CT + i, :], mixp[:, i % 2, :], XH[:, CT + i, :].bitcast(F32),
                                   ALU.subtract).then_inc(pool_lo, 1)
            for c in range(CT):
                pool.wait_ge(cv_hi, c + 1)
                pool.tensor_tensor(XL[:, c, :], vconv[:, c, :], XH[:, c, :].bitcast(F32),
                                   ALU.subtract).then_inc(cv_lo, 1)

            def lows(name, times, per):
                with pool.Fori(0, times) as it:
                    for j, kt in enumerate(loop_with_sizes(name, per)):
                        low(Nth(STAGES[name][0] + j + 2, it, per), kt)

            def lows_of_hidden(name, layer):
                with pool.Fori(0, FT // 2) as it:
                    for j in range(2):
                        low(Nth(STAGES[name][0] + 2 * j + 2, it, 4))
                        low(Nth(STAGES[name][0] + 2 * j + 3, it, 4))
                        h = Nth(FT * layer + j, it, 2)
                        pool.wait_ge(h_hi, h.n(1))
                        pool.tensor_tensor(HL[:, bass.ds(it * 2 + j, 1), :], hid[:, j:j + 1, :],
                                           HH[:, bass.ds(it * 2 + j, 1), :].bitcast(F32), ALU.subtract).then_inc(h_lo[j], 1)

            lows("out", 2, 4)
            lows_of_x(1, lambda t: tmp[t % 2])
            lows_of_hidden("gu0", 0)
            lows("down0", DT // 2, 8)
            lows_of_x(2, lambda t: xres[:, t, :])
            pool.memset(CC[:, :], 0.0).then_inc(cc_zero, 1)

            with pool.Fori(0, UNITS) as it:
                for j in range(4):
                    low(Nth(STAGES["qkv1"][0] + j + 2, it, 4), (UNIT[2:] + UNIT[:2])[j])
            lows("out1", 2, 4)
            lows_of_x(3, lambda t: xres[:, t, :])
            lows_of_hidden("gu1", 1)
            lows("down1", DT // 2, 8)
            lows_of_x(4, lambda t: xres[:, t, :])

            def sub_low(u):
                pool.wait_ge(sub_hi, u.n(1))
                pool.tensor_tensor(OL[:, at(u), :], osb[:, :].rearrange("p (a s) -> p a s", a=1),
                                   OH[:, at(u), :].bitcast(F32), ALU.subtract).then_inc(sub_lo, 1)

            def unit_lows(iu, au):
                for j in range(4):
                    if iu is not None:
                        low(iu.times(4, STAGES["qkv2"][0] + j + 2), (UNIT[2:] + UNIT[:2])[j])
                    if j == 0 and au is not None and not (isinstance(au.it, int) and au.base == 0):
                        sub_low(au + -1)
                    if j < 2 and iu is not None:
                        pool.wait_ge(qk_hi, iu.times(2, 2 * UNITS + j).n(1))
                        pool.tensor_tensor(QKL[:, iu.slot(2), j, :], qk[:, :], QKH[:, iu.slot(2), j, :].bitcast(F32),
                                           ALU.subtract).then_inc(qk_lo, 1)

            weave_units(pool.Fori, unit_lows)
            sub_low(Nth(UNITS - 1))
            lows("out2", 2, 4)
            lows_of_x(5, lambda t: xres[:, t, :])
            lows_of_hidden("gu2", 2)
            lows("down2", DT // 2 - 1, 8)
            for j, kt in enumerate(loop_with_sizes("down2", 8)[:6]):
                low(Nth(STAGES["down2"][0] + 8 * (DT // 2 - 1) + j + 2), kt)

        @block.tensor
        def _(pe):
            def product(out_, wh, wl, xh, xl, start, stop):
                pe.matmul(out_, wh, xl, start=start, stop=False)
                pe.matmul(out_, wh, xh, start=False, stop=False)
                return pe.matmul(out_, wl, xh, start=False, stop=stop)

            def step(g, b, hi, lo, k0, k, kt, start, stop):
                if k == 0:
                    pe.wait_ge(w_lo, g.n(1))
                s = g.slot(SPLIT)
                mm = product(bank[b][:, :], WH[:, s, k, :], WL[:, s, k, :], hi[:, k0 + k, :], lo[:, k0 + k, :],
                             start and k == 0, stop and k == kt - 1)
                if k == kt - 1:
                    mm.then_inc(item_done, 1)

            def item(g, b, hi, lo, k0, kt, start, stop):
                for k in range(kt):
                    step(g, b, hi, lo, k0, k, kt, start, stop)

            def bank_free(u):
                pe.wait_ge(bank_read[u.slot(2)], u.round(2))

            def two_items(name, ready, order=tuple(range(DT))):
                g, u = STAGES[name]
                for k in order:
                    ready(k)
                    for j in range(2):
                        if k == order[0]:
                            bank_free(Nth(u + j))
                            pe.wait_ge(w_lo, g + j + 1)
                        s = (g + j) % SPLIT
                        mm = product(bank[(u + j) % 2][:, :], WH[:, s, k, :], WL[:, s, k, :], XH[:, k, :], XL[:, k, :],
                                     k == order[0], k == order[-1])
                        if k == order[-1]:
                            mm.then_inc(item_done, 1)

            def whole(name, j, it=0, per=4, x=(XH, XL)):
                u = Nth(STAGES[name][1] + j, it, per)
                bank_free(u)
                item(Nth(STAGES[name][0] + j, it, per), u.slot(2), *x, 0, DT, True, True)

            def stage(name, times, ready=None, x=(XH, XL), order=tuple(range(DT))):
                if ready:
                    two_items(name, ready, order)
                for j in range(2, 4):
                    whole(name, j, x=x)
                with pe.Fori(1, times) as it:
                    for j in range(4):
                        whole(name, j, it, x=x)

            def normed(m):
                return lambda k: pe.wait_ge(x_lo, DT * m + k + 1)

            def down(name, layer):
                for q in h_lo:
                    pe.wait_ge(q, (layer + 1) * FT // 2 + OPEN)
                with pe.Fori(0, DT // 2) as it:
                    for j in range(8):
                        u = Nth(STAGES[name][1] + j // 4, it, 2)
                        if j % 4 == 0:
                            bank_free(u)
                        item(Nth(STAGES[name][0] + j, it, 8), u.slot(2), HH, HL, sum(DOWN[:j % 4]), DOWN[j % 4],
                             j % 4 == 0, j % 4 == 3)

            def stats(m, centred):
                pe.wait_ge(sum_tiles, DT * (m + 1))
                mm = pe.matmul(sc[0][:, :], ones[:, :], ssq, start=True, stop=True)
                if centred:
                    mm = pe.matmul(sc[1][:, :], ones[:, :], ssum, start=True, stop=True)
                mm.then_inc(stats_done, 1)

            pe.wait_ge(consts, 3)
            pe.wait_ge(x_in, 16 * QT)
            for t in range(DT):
                if t >= 2:
                    pe.wait_ge(bank_read[t % 2], t // 2)
                for q in range(QT):
                    mm = pe.transpose(bank[t % 2][:, q * P:(q + 1) * P], xin[:, q, t * P:(t + 1) * P], ident[:, :])
                mm.then_inc(turned_x, 1)
            def turn_rows(i):
                n = ROWS_OF[i]
                return pe.transpose(turned_rows(i), prow[0:n, i, :], ident[0:n, 0:n])

            pe.wait_ge(rows0_in, 16 * len(ROWS0))
            turn_rows(0).then_inc(turned_par, 1)
            stats(0, False)
            pe.wait_ge(par_in, 16 * TAP_LOADS)
            for i in range(1, len(ROWS_OF)):
                mm = turn_rows(i)
            mm.then_inc(turned_par, 1)
            two_items("in", normed(0))
            for n in range(2, 12):
                whole("in", n)
            pe.wait_ge(u_lo, 1)
            pe.wait_ge(diag_h, TAPS)
            pe.wait_ge(diag_l, -(-TAPS // DIAG_CHUNK))
            for j in range(TAPS):
                mm = product(ob[0][:, :], dg_h[:, j, :], dg_l[:, j, :], u_h[:, j:j + S], u_l[:, j:j + S], j == 0, j == TAPS - 1)
            mm.then_inc(pe_conv, 1)
            pe.wait_ge(small_in, 16)
            pe.wait_ge(par_ok, 1)
            for i in range(CT):
                pe.wait_ge(ypool_ready, i + 1)
                if i >= 2:
                    pe.wait_ge(pool_out, i - 1)
                pe.matmul(tb[i % 2][:, :], wpool[:, i, :], ypool[:, i, :], start=True, stop=True).then_inc(pool_mm, 1)
            pe.wait_ge(cv_sum, CT)
            pe.matmul(sc[0][:, :], ones[:, :], ssq, start=True, stop=True)
            pe.matmul(sc[1][:, :], ones[:, :], ssum, start=True, stop=True).then_inc(cv_stats, 1)
            pe.wait_ge(pool_lo, CT)
            stage("out", 2, lambda k: pe.wait_ge(cv_lo, k + 1) if k < CT else None,
                  order=(*range(CT, DT), *range(CT)))
            stats(1, False)
            stage("gu0", FT // 2, normed(1))
            down("down0", 0)
            stats(2, False)
            pe.wait_ge(wf_in, 32)
            for k in range(DT):
                pe.wait_ge(xn_ready, 2 * DT + k + 1)
                mm = pe.matmul(sc[0][0:FOX_HEADS, :], wf[:, k, :], xres[:, k, :], start=(k == 0), stop=(k == DT - 1))
            mm.then_inc(gate_done, 1)

            def unit_steps(name, u, ready=None):
                turn0 = STAGES[name][1]
                item0 = STAGES[name][0]
                for tile in range(3):
                    for k in range(DT):
                        part, kk = (tile, k) if tile < 2 else (2 + k // 4, k % 4)
                        if k == 0:
                            bank_free(u.times(4, turn0 + tile))
                        step(u.times(4, item0 + part), tile % 2, XH, XL, k - kk, kk, UNIT[part],
                             part < 3, part != 2)
                        yield

            def unit_steps_fed(name, m):
                two_items(name, normed(m))
                turn0, item0 = STAGES[name][1], STAGES[name][0]
                bank_free(Nth(turn0 + 2))
                for k in range(DT):
                    step(Nth(item0 + 2 + k // 4), 0, XH, XL, k - k % 4, k % 4, 4, k < 4, k >= 4)

            def turn_v(name, layer, u):
                pe.wait_ge(bank_read[0], u.times(4, STAGES[name][1] + 2).round(2, 1))
                bank_free(u.times(4, STAGES[name][1] + 3))
                for q in range(QT):
                    mm = pe.transpose(bank[1][:, q * P:(q + 1) * P], vt[:, q * P:(q + 1) * P], ident[:, :])
                mm.then_inc(v_turned, 1)

            def score(n, used, slot, rows, side, i, mask, bias):
                c = n % 2
                q, k = slice(i * P, (i + 1) * P), slice(0, (i + 1) * P)
                pe.wait_ge(ex[c], used.n() + OPEN)
                pe.matmul(sc[c][:, k], QKH[rows, slot, 0, q], QKL[rows, slot, 1, k], start=True, stop=False)
                pe.matmul(sc[c][:, k], QKH[rows, slot, 0, q], QKH[rows, slot, 1, k], start=False, stop=False)
                pe.matmul(sc[c][:, k], QKL[rows, slot, 0, q], QKH[rows, slot, 1, k], start=False, stop=False)
                if bias:
                    pe.matmul(sc[c][:, k], onesr[rows, :], Cm[rows, slot, k], start=False, stop=False)
                pe.matmul(sc[c][:, q], identb[:, :], masks[:, mask, :], start=False, stop=True).then_inc(s_done[c], 1)

            def turn_map(b, used, src, i):
                pe.wait_ge(pn[b], used.n(1))
                pe.wait_ge(pt_l[b], used.n() + OPEN)
                for j in range(i + 1):
                    mm = pe.transpose(tb[b][:, j * P:(j + 1) * P], src[:, j * P:(j + 1) * P], ident[:, :])
                mm.then_inc(t_done[b], 1)

            def attend(e, slot, turn):
                pe.wait_ge(o_read[e], turn.n() + OPEN)
                for j in range(QT):
                    mm = product(ob[e][:, j * P:], VH[:, slot, j * P:(j + 1) * P], VL[:, slot, j * P:(j + 1) * P],
                                 PTH[:, e, j, j * P:], PTL[:, e, j, j * P:], j == 0, j == QT - 1)
                mm.then_inc(o_done[e], 1)

            def weave(steps, slot_work, skip=0):
                for sl in range(12):
                    slot_work(sl)
                    if sl >= skip:
                        for _ in range(2):
                            next(steps, None)
                for _ in steps:
                    pass

            def out_steps(name, ready, ks):
                g, u = STAGES[name]
                for k in ks:
                    ready(k)
                    for j in range(2):
                        if k == 0:
                            bank_free(Nth(u + j))
                        step(Nth(g + j), (u + j) % 2, OH, OL, 0, k, DT, True, True)
                        yield

            def fox_slot(u):
                slot = u.slot(2)

                def work_of(sl):
                    if sl == 1:
                        turn_v("qkv1", 0, u)
                    if sl < 8:
                        if sl == 0:
                            pe.wait_ge(cm_ready, u.n(1))
                            pe.wait_ge(bank_read[0], u.times(4, STAGES["qkv1"][1]).round(2, 1))
                            pe.wait_ge(bank_read[1], u.times(4, STAGES["qkv1"][1] + 1).round(2, 1))
                        rows = slice(HEAD * (sl % 2), HEAD * (sl % 2) + HEAD)
                        score(sl, u.times(4, sl // 2), slot, rows, sl % 2, sl // 2, 0, True)
                    if 2 <= sl < 10:
                        n = sl - 2
                        turn_map(n % 2, u.times(4, n // 2), pmap[:, n % 4, :], n // 2)
                    if sl >= 10:
                        e = sl - 10
                        pe.wait_ge(pt_l[e], u.times(4, 4).n() + OPEN)
                        pe.wait_ge(bank_read[1], u.times(4, STAGES["qkv1"][1] + 3).round(2, 1))
                        attend(e, slot, u)
                return work_of

            def fox_part(iu, au):
                if au is None:
                    unit_steps_fed("qkv1", 2)
                elif iu is None:
                    def ready(k):
                        for e in range(2):
                            pe.wait_ge(o_read[e], k + 1 + OPEN)
                    weave(out_steps("out1", ready, range(DT - 1)), fox_slot(au), skip=3)
                    for _ in out_steps("out1", ready, [DT - 1]):
                        pass
                else:
                    weave(unit_steps("qkv1", iu), fox_slot(au))

            pe.wait_ge(consts, CONSTS)
            weave_units(pe.Fori, fox_part)
            stage("out1", 2, x=(OH, OL))
            stats(3, True)
            stage("gu1", FT // 2, normed(3))
            down("down1", 1)
            stats(4, True)

            def diff_slot(u):
                slot = u.slot(2)
                first = 4 * UNITS

                def work_of(sl):
                    if sl == 1:
                        turn_v("qkv2", 1, u)
                    if sl == 2 and not (isinstance(u.it, int) and u.base == 0):
                        mean_square(u + -1)
                    if sl < 8:
                        if sl == 0:
                            pe.wait_ge(qk_lo, u.times(2, 2).n() + OPEN)
                        rows = slice(HEAD * (sl % 2), HEAD * (sl % 2) + HEAD)
                        score(sl, u.times(4, first + sl // 2), slot, rows, sl % 2, sl // 2, 1, False)
                    if sl in (3, 5, 7, 9):
                        i = (sl - 3) // 2
                        turn_map(i % 2, u.times(2, first + i // 2), pmap[:, 2 * (i % 2), :], i)
                    if sl == 11:
                        for b in range(2):
                            pe.wait_ge(pt_l[b], u.times(2, first + 2).n() + OPEN)
                        pe.wait_ge(bank_read[1], u.times(4, STAGES["qkv2"][1] + 3).round(2, 1))
                        attend(0, slot, u + UNITS)
                return work_of

            def mean_square(u):
                pe.wait_ge(sub_sq, u.n(1))
                pe.matmul(ob[1][:, :], ones[:, :], osq[:, :], start=True, stop=True).then_inc(sub_var, 1)

            def diff_part(iu, au):
                if au is None:
                    unit_steps_fed("qkv2", 4)
                    pe.wait_ge(lam_a, 1)
                    pe.matmul(tb[0][:, 0:1], ones[0:1, :], lam_row[2], start=True, stop=True).then_inc(lam_b, 1)
                    pe.wait_ge(lam_d, 1)
                elif iu is None:
                    def ready(k):
                        pe.wait_ge(sub_lo, k + 1 + OPEN)
                    weave(out_steps("out2", ready, range(DT - 1)), diff_slot(au), skip=5)
                    mean_square(au)
                    for _ in out_steps("out2", ready, [DT - 1]):
                        pass
                else:
                    weave(unit_steps("qkv2", iu), diff_slot(au))

            weave_units(pe.Fori, diff_part)
            stage("out2", 2, x=(OH, OL))
            stats(5, True)
            stage("gu2", FT // 2, normed(5))
            down("down2", 2)
            stats(6, True)
            pe.wait_ge(x_hi, 7 * DT)
            for n in range(2 * QT):
                u = Nth(STAGES["back"][1] + n)
                bank_free(u)
                for k in range(4):
                    mm = pe.transpose(bank[u.slot(2)][:, k * P:(k + 1) * P],
                                      xres[:, n % 2 * 4 + k, n // 2 * P:(n // 2 + 1) * P], ident[:, :])
                mm.then_inc(y_turned, 1)

        @block.scalar
        def _(act):
            own = Chain(act, av)

            def high(g, kt=DT):
                act.wait_ge(w_landed[g.slot(RAW)], g.round(RAW, 1) * 16)
                if not (isinstance(g.it, int) and g.base < SPLIT):
                    act.wait_ge(item_done, g.n(1 - SPLIT))
                act.activation(WH[:, g.slot(SPLIT), 0:kt, :], raw[:, g.slot(RAW), 0:kt, :], ACT.Copy).then_inc(w_hi, 1)

            def warm(func):
                act.activation(small[:, 90:91], small[:, 46:47], func)

            def root(m):
                act.wait_ge(var_ready, m + 1)
                act.activation(rstd, work[:, 1, :], ACT.Sqrt).then_inc(rstd_ready, 1)

            def norm_rms(m, src):
                root(m)
                for t in range(DT):
                    act.wait_ge(xn_ready, DT * m + t + 1)
                    act.activation(XH[:, t, :], src(t), ACT.Copy).then_inc(x_hi, 1)

            def norm_ln(m, g, b, split=True):
                root(m)
                for t in range(DT):
                    act.wait_ge(xn_ready, DT * m + t + 1)
                    y = act.activation(xres[:, t, :], tmp[t % 2], ACT.Identity, bias=b(t), scale=g(t))
                    if split:
                        own.link(y)
                        act.activation(XH[:, t, :], xres[:, t, :], ACT.Copy).then_inc(x_hi, 1)
                    else:
                        y.then_inc(x_hi, 1)

            def highs(name, times, per):
                with act.Fori(0, times) as it:
                    for j, kt in enumerate(loop_with_sizes(name, per)):
                        high(Nth(STAGES[name][0] + j + 2, it, per), kt)

            for t in range(DT):
                act.wait_ge(bank_read[t % 2], t // 2 + 1)
                if t >= 2:
                    act.wait_ge(sum_tiles, t - 1)
                act.activation(tmp[t % 2], xres[:, t, :], ACT.Square).then_inc(squared, 1)
                if t in (2, 5):
                    high(Nth(t // 4))
            warm(ACT.Sqrt)
            norm_rms(0, lambda t: tmp[t % 2])
            act.wait_ge(par_ok, 1)
            gates = 0
            for n, (kind, c) in enumerate(IN_ORDER):
                high(Nth(n + 2))
                u = Nth(STAGES["in"][1] + n)
                if kind == "gate":
                    act.wait_ge(item_done, n + 1)
                    if gates >= 2:
                        used = [i for i, x in enumerate(IN_ORDER) if x[0] == "value"][gates - 2]
                        act.wait_ge(bank_read[1], (DT + used) // 2 + 1)
                    act.activation(sig[:, gates % 2, :], bank[0][:, :], ACT.Sigmoid, bias=pcol("b_in", CT + c)).then_inc(bank_read[0], 1)
                    gates += 1
                elif kind == "pool":
                    act.wait_ge(item_done, n + 1)
                    act.wait_ge(consts, CONSTS)
                    act.activation(ppad[:, c, PAD:], bank[u.slot(2)][:, :], ACT.Identity,
                                   bias=pcol("b_in", 2 * CT + c)).then_inc(bank_read[u.slot(2)], 1)
                if n == 4:
                    act.wait_ge(taps_split, 2)
                    for j in range(TAPS):
                        act.activation(dg_h[:, j, :], ident[:, :], ACT.Copy,
                                       scale=tap_h[:, j:j + 1].bitcast(F32)).then_inc(diag_h, 1)
                if n == 10:
                    act.wait_ge(bank_read[1], (DT + in_item("value", PE_TILE)) // 2 + 1)
                    act.activation(u_h[:, :], upad[:, PE_TILE, :], ACT.Copy).then_inc(u_hi, 1)
            act.wait_ge(pe_conv, 1)
            act.activation(vconv[:, PE_TILE, :], ob[0][:, :], ACT.Identity, bias=pcol("b_dw", PE_TILE)).then_inc(pe_conv_out, 1)
            for i in range(CT):
                act.wait_ge(pool_mm, i + 1)
                if i >= 2:
                    act.wait_ge(pool_lo, i - 1)
                act.activation(mixp[:, i % 2, :], tb[i % 2][:, :], ACT.Copy, scale=pcol("s_pool", i)).then_inc(pool_out, 1)
                act.wait_ge(pool_out, i + 1)
                act.activation(XH[:, CT + i, :], mixp[:, i % 2, :], ACT.Copy).then_inc(pool_hi, 1)
            act.wait_ge(cv_var, 1)
            act.activation(rstd, work[:, 1, :], ACT.Sqrt).then_inc(cv_rstd, 1)
            for c in range(CT):
                act.wait_ge(cv_n, 2 + c)
                own.link(act.activation(vconv[:, c, :], vconv[:, c, :], ACT.Silu, bias=pcol("ln_b", c), scale=pcol("ln_g", c)))
                act.activation(XH[:, c, :], vconv[:, c, :], ACT.Copy).then_inc(cv_hi, 1)
            highs("out", 2, 4)
            norm_rms(1, lambda t: tmp[t % 2])

            def hidden_hi(it, j, layer, name):
                act.wait_ge(bank_read[1], Nth(STAGES[name][1] + 2 * j + 1, it, 4).round(2, 1))
                act.activation(HH[:, bass.ds(it * 2 + j, 1), :], hid[:, j:j + 1, :], ACT.Copy).then_inc(h_hi, 1)

            warm(ACT.Silu)
            with act.Fori(0, FT // 2) as it:
                for j in range(2):
                    g = Nth(STAGES["gu0"][0] + 2 * j, it, 4)
                    high(g + 2)
                    act.wait_ge(item_done, g.n(1))
                    act.wait_ge(bank_read[1], Nth(STAGES["gu0"][1] + 2 * j + 1, it, 4).round(2, -1))
                    act.activation(act_g[:, j, :], bank[0][:, :], ACT.Silu).then_inc(bank_read[0], 1)
                    high(g + 3)
                    hidden_hi(it, j, 0, "gu0")
            highs("down0", DT // 2, 8)
            norm_rms(2, lambda t: xres[:, t, :])
            act.wait_ge(gate_a, 1)
            act.activation(tmp[1][0:FOX_HEADS, :], tmp[1][0:FOX_HEADS, :], ACT.Exp).then_inc(gate_b, 1)
            act.wait_ge(gate_b, 1)
            act.activation(tmp[1][0:FOX_HEADS, :], tmp[1][0:FOX_HEADS, :], ACT.Ln, bias=1.0).then_inc(gate_b, 1)

            def exps(n, used):
                c, k = n % 2, (n // 2 + 1) * P
                act.wait_ge(mx[c], used.n(1))
                act.activation(pmap[:, n % 4, 0:k], sc[c][:, 0:k], ACT.Exp, bias=small[:, n % 4:n % 4 + 1],
                               accum_out=small[:, 4 + n % 4:5 + n % 4]).then_inc(ex[c], 1)

            def map_hi(b, used, head, i):
                act.wait_ge(t_done[b], used.n(1))
                act.activation(PTH[:, head, 0:i + 1, i * P:(i + 1) * P],
                               tb[b][:, 0:(i + 1) * P].rearrange("p (j q) -> p j q", q=P), ACT.Copy).then_inc(pt_h[b], 1)

            def value_hi(layer, u):
                act.wait_ge(v_turned, u.n(layer * UNITS + 1))
                act.activation(VH[:, u.slot(2), :], bank[1][:, :], ACT.Copy).then_inc(v_hi, 1)

            def value_out(name, iu):
                act.wait_ge(item_done, iu.times(4, STAGES[name][0] + 4).n())
                act.activation(vt[:, :], bank[0][:, :], ACT.Copy).then_inc(bank_read[0], 1)

            def unit_high(name, iu, j):
                high(iu.times(4, STAGES[name][0] + j + 2), (UNIT[2:] + UNIT[:2])[j])

            SLOT_OF_ITEM = (4, 8, 10, 12)

            def fox_part(iu, au):
                for sl in range(13):
                    if au is not None:
                        if sl == 2:
                            value_hi(0, au)
                        if sl < 8:
                            exps(sl, au.times(4, sl // 2))
                        if 2 <= sl < 10:
                            n = sl - 2
                            map_hi(n % 2, au.times(4, n // 2), n % 2, n // 2)
                        if sl >= 11:
                            e = sl - 11
                            r = slice(HEAD * e, HEAD * e + HEAD)
                            act.wait_ge(o_done[e], au.n(1))
                            act.activation(OH[r, at(au), :], ob[e][r, :].rearrange("p (a s) -> p a s", a=1), ACT.Copy).then_inc(o_hi, 1)
                    if iu is not None and sl in SLOT_OF_ITEM:
                        j = SLOT_OF_ITEM.index(sl)
                        if j < 2:
                            act.wait_ge(item_done, iu.times(4, STAGES["qkv1"][0] + j + 1).n())
                            act.activation(QKH[:, iu.slot(2), j, :], bank[j][:, :], ACT.Copy,
                                           scale=1.0 if j else HEAD ** -0.5).then_inc(qk_hi, 1)
                        if j == 3:
                            value_out("qkv1", iu)
                        unit_high("qkv1", iu, j)

            weave_units(act.Fori, fox_part)
            highs("out1", 2, 4)
            warm(ACT.Sqrt)
            norm_ln(3, lambda t: pcol("ln_attn_g_2", t), lambda t: pcol("ln_attn_b_2", t))

            def conv_hidden(name, layer):
                warm(ACT.Silu)
                with act.Fori(0, FT // 2) as it:
                    for j in range(2):
                        g = Nth(STAGES[name][0] + 2 * j, it, 4)
                        for side, dst in ((0, act_g), (1, hid)):
                            high(g + side + 2)
                            act.wait_ge(item_done, g.n(1 + side))
                            if side == 0:
                                act.wait_ge(hid_ready[j], Nth(FT * (layer - 1) + j, it, 2).round(2) + OPEN)
                            else:
                                act.wait_ge(h_lo[j], Nth(FT * layer + j, it, 2).round(2) + OPEN)
                            n = it * 2 + (j + FT * side)
                            act.activation(dst[:, j, :], bank[side][:, :], ACT.Identity, bias=ff_par(layer - 1, 3, n),
                                           scale=ff_par(layer - 1, 2, n)).then_inc(ff_lin[side], 1)
                        act.wait_ge(bank_read[0], Nth(STAGES[name][1] + 2 * j, it, 4).round(2, 1))
                        act.activation(act_g[:, j, :], act_g[:, j, :], ACT.Silu).then_inc(g_act, 1)
                        act.wait_ge(hid_ready[j], Nth(FT * (layer - 1) + j, it, 2).round(2, 1) + OPEN)
                        act.activation(HH[:, bass.ds(it * 2 + j, 1), :], hid[:, j:j + 1, :], ACT.Copy).then_inc(h_hi, 1)

            conv_hidden("gu1", 1)
            highs("down1", DT // 2, 8)
            warm(ACT.Sqrt)
            norm_ln(4, lambda t: pcol("ln_ffn_g_2", t), lambda t: pcol("ln_ffn_b_2", t))
            def sub_root(u):
                act.wait_ge(sub_var, u.n(1))
                act.activation(osq[:, :], ob[1][:, :], ACT.Ln, bias=small[:, 46:47], scale=1.0 / P).then_inc(sub_ln, 1)
                act.wait_ge(sub_ln, u.n(1))
                act.activation(osq[:, :], osq[:, :], ACT.Exp, scale=-0.5).then_inc(sub_rs, 1)

            def sub_high(u):
                act.wait_ge(sub_n, u.n(1))
                act.activation(OH[:, at(u), :], osb[:, :].rearrange("p (a s) -> p a s", a=1), ACT.Copy).then_inc(sub_hi, 1)

            def diff_part(iu, au):
                first = 4 * UNITS
                before = None if au is None or (isinstance(au.it, int) and au.base == 0) else au + -1
                for sl in range(13):
                    if au is not None:
                        if sl == 2:
                            value_hi(1, au)
                        if sl < 8:
                            exps(sl, au.times(4, first + sl // 2))
                        if sl == 3 and before is not None:
                            sub_root(before)
                        if sl == 5 and before is not None:
                            sub_high(before)
                        if sl in (3, 5, 7, 9):
                            i = (sl - 3) // 2
                            map_hi(i % 2, au.times(2, first + i // 2), 0, i)
                        if sl == 12:
                            act.wait_ge(o_done[0], au.n(UNITS + 1))
                            act.wait_ge(sub_lo, au.n() + OPEN)
                            act.activation(osb[:, :], ob[0][:, :], ACT.Copy).then_inc(o_read[0], 1)
                            act.wait_ge(o_read[0], au.n(UNITS + 1) + OPEN)
                            act.activation(osq[:, :], osb[:, :], ACT.Square).then_inc(sub_sq, 1)
                    if iu is not None:
                        if sl in (7, 11):
                            j = (sl - 7) // 4
                            act.wait_ge(roped, iu.times(2, j + 1).n())
                            act.activation(QKH[:, iu.slot(2), j, :], qk[:, :], ACT.Copy).then_inc(qk_hi, 1)
                        if sl == 12:
                            value_out("qkv2", iu)
                        if sl in (4, 8):
                            j = sl // 4 - 1
                            act.wait_ge(item_done, iu.times(4, STAGES["qkv2"][0] + j + 1).n())
                            for r in range(4):
                                o = r + 1 - 2 * (r % 2)
                                act.activation(rot[32 * r:32 * r + 32, :], bank[j][32 * o:32 * o + 32, :], ACT.Copy).then_inc(rot_ready, 1)
                        if sl in SLOT_OF_ITEM:
                            unit_high("qkv2", iu, SLOT_OF_ITEM.index(sl))
                if au is None:
                    act.wait_ge(lam_c, 1)
                    act.activation(lam_row[1], lam_row[0], ACT.Exp).then_inc(lam_c, 1)

            act.add_instruction(mybir.InstLoadActFuncSet(name=nc.get_next_instruction_name(), act_func_set_id=LN_EXP_SET,
                                                         engine=mybir.EngineType.Activation, ins=[], outs=[]))
            weave_units(act.Fori, diff_part)
            sub_root(Nth(UNITS - 1))
            sub_high(Nth(UNITS - 1))
            highs("out2", 2, 4)
            warm(ACT.Sqrt)
            norm_ln(5, lambda t: pcol("ln_attn_g_2", DT + t), lambda t: pcol("ln_attn_b_2", DT + t))
            conv_hidden("gu2", 2)
            highs("down2", DT // 2 - 1, 8)
            for j, kt in enumerate(loop_with_sizes("down2", 8)[:6]):
                high(Nth(STAGES["down2"][0] + 8 * (DT // 2 - 1) + j + 2), kt)
            warm(ACT.Sqrt)
            norm_ln(6, lambda t: pcol("ln_ffn_g_2", DT + t), lambda t: pcol("ln_ffn_b_2", DT + t), split=False)

        @block.vector
        def _(dve):
            own = Chain(dve, dv)

            def add_squares(x, count):
                own.link(dve.tensor_tensor(tmp[0], x, x, ALU.mult))
                dve.tensor_tensor(ssq, ssq, tmp[0], ALU.add).then_inc(*count)

            def clear_sums():
                own.did(dve.memset(ssum, 0.0))
                own.link(dve.memset(ssq, 0.0))

            own.did(dve.memset(small[:, 46:47], SUB_EPS))
            clear_sums()
            for t in range(DT + 1):
                if t < DT:
                    dve.wait_ge(turned_x, t + 1)
                    dve.tensor_copy(xres[:, t, :], bank[t % 2][:, :]).then_inc(bank_read[t % 2], 1)
                if t:
                    dve.wait_ge(squared, t)
                    if t > 1:
                        dve.wait_ge(sum_tiles, t - 1)
                    dve.tensor_tensor(ssq, ssq, tmp[(t - 1) % 2], ALU.add).then_inc(sum_tiles, 1)

            def rows_out(i):
                n = ROWS_OF[i]
                own.did(dve.tensor_copy(par[:, i * P:i * P + n], turned_rows(i)))

            dve.wait_ge(bank_read[0], DT // 2)
            dve.wait_ge(bank_read[1], DT // 2)
            dve.wait_ge(turned_par, 1)
            rows_out(0)
            own.sync()
            def moments(centred, var, width, eps):
                if centred:
                    own.link(dve.tensor_scalar(mean, sc[1][:, :], 1.0 / width, None, ALU.mult))
                    own.link(dve.tensor_tensor(tmp[0], mean, mean, ALU.mult))
                    own.link(dve.scalar_tensor_tensor(out=tmp[1], in0=sc[0][:, :], scalar=1.0 / width, in1=tmp[0],
                                                      op0=ALU.mult, op1=ALU.subtract))
                    own.link(dve.tensor_scalar(tmp[1], tmp[1], 0.0, eps, ALU.max, ALU.add))
                else:
                    own.link(dve.tensor_scalar(tmp[1], sc[0][:, :], 1.0 / width, eps, ALU.mult, ALU.add))
                dve.reciprocal(tmp[1], tmp[1]).then_inc(var, 1)
                clear_sums()

            def norm(m, scale, centred, in_place):
                dve.wait_ge(stats_done, m + 1)
                moments(centred, var_ready, D, LN_EPS if centred else RMS_EPS)
                dve.wait_ge(rstd_ready, m + 1)
                if centred:
                    own.link(dve.tensor_tensor(mean, mean, rstd, ALU.mult))
                for t in range(DT):
                    if t >= 2 and not in_place:
                        if m == 6:
                            dve.wait_ge(x_hi, DT * m + t - 1)
                        else:
                            dve.wait_ge(x_lo, DT * m + t - 1)
                    if centred:
                        own.link(dve.tensor_tensor(tmp[t % 2], xres[:, t, :], rstd, ALU.mult))
                        dve.tensor_tensor(tmp[t % 2], tmp[t % 2], mean, ALU.subtract).then_inc(xn_ready, 1)
                    else:
                        dst = xres[:, t, :] if in_place else tmp[t % 2]
                        dve.scalar_tensor_tensor(out=dst, in0=xres[:, t, :], scalar=pcol(scale, t), in1=rstd,
                                                 op0=ALU.mult, op1=ALU.mult).then_inc(xn_ready, 1)

            def counted(per):
                return lambda first, times: own.loop(times, per)

            norm(0, "g_mix", False, False)
            dve.wait_ge(turned_par, 2)
            for i in range(1, len(ROWS_OF)):
                rows_out(i)
            own.sync()
            dve.tensor_scalar(small[:, 47:48], pcol("b_subln_g_2", 0), 1.0 - LAMBDA_INIT, None, ALU.mult).then_inc(par_ok, 1)
            own.link(dve.tensor_copy(tap_h[:, :], par[:, P + PE_TILE:P + PE_TILE + TAPS * CT:CT]))
            dve.tensor_tensor(tap_l[:, :], par[:, P + PE_TILE:P + PE_TILE + TAPS * CT:CT], tap_h[:, :].bitcast(F32),
                              ALU.subtract).then_inc(taps_split, 2)
            dve.wait_ge(consts, CONSTS)
            dve.reciprocal(icnt[:, :], cnts[:, :]).then_inc(cv_n, 1)

            def gated(c):
                n = in_item("value", c)
                k = [x[1] for x in IN_ORDER if x[0] == "gate"].index(c)
                dve.wait_ge(item_done, n + 1)
                dve.wait_ge(bank_read[0], (DT + n - 1) // 2 + 1)
                dve.scalar_tensor_tensor(out=upad[:, c, TAPS - 1:], in0=bank[1][:, :], scalar=pcol("b_in", c),
                                         in1=sig[:, k % 2, :], op0=ALU.add, op1=ALU.mult).then_inc(bank_read[1], 1)
                dve.wait_ge(bank_read[1], (DT + n) // 2 + 1)

            def taps(c, a, b):
                if a == 0:
                    own.link(dve.tensor_scalar(vconv[:, c, :], upad[:, c, 0:S], tap(0, c), pcol("b_dw", c), ALU.mult, ALU.add))
                for j in range(max(a, 1), b):
                    own.link(dve.scalar_tensor_tensor(out=vconv[:, c, :], in0=upad[:, c, j:j + S], scalar=tap(j, c),
                                                      in1=vconv[:, c, :], op0=ALU.mult, op1=ALU.add))

            def add_conv(c, k):
                if k:
                    dve.wait_ge(cv_sum, k)
                own.did(dve.tensor_tensor(ssum, ssum, vconv[:, c, :], ALU.add))
                add_squares(vconv[:, c, :], (cv_sum, 1))

            gated(0)
            taps(0, 0, TAPS)
            add_conv(0, 0)
            gated(1)
            taps(1, 0, TAPS // 2)
            gated(PE_TILE)
            taps(1, TAPS // 2, TAPS)
            add_conv(1, 1)
            gated(2)
            taps(2, 0, TAPS)
            add_conv(2, 2)
            dve.wait_ge(pe_conv_out, 1)
            add_conv(PE_TILE, 3)
            dve.wait_ge(cv_stats, 1)
            moments(True, cv_var, C_CONV, LN_EPS)
            dve.wait_ge(cv_rstd, 1)
            own.link(dve.tensor_tensor(mean, mean, rstd, ALU.mult))
            for c in range(CT):
                own.link(dve.tensor_tensor(vconv[:, c, :], vconv[:, c, :], rstd, ALU.mult))
                dve.tensor_tensor(vconv[:, c, :], vconv[:, c, :], mean, ALU.subtract).then_inc(cv_n, 1)

            def residual(name, m, items_of_tile, factor, centred):
                per = (2 if centred else 1) * 2
                with own.loop(DT // 2, per) as it:
                    for j in range(2):
                        last = Nth(STAGES[name][0] + (j + 1) * items_of_tile - 1, it, 2 * items_of_tile)
                        u = Nth(STAGES[name][1] + j, it, 2)
                        r = xres[:, bass.ds(it * 2 + j, 1), :]
                        dve.wait_ge(item_done, last.n(1))
                        dve.scalar_tensor_tensor(out=r, in0=r, scalar=factor, in1=bank[j][:, :].rearrange("p (a s) -> p a s", a=1),
                                                 op0=ALU.mult, op1=ALU.add).then_inc(bank_read[j], 1)
                        dve.wait_ge(bank_read[j], u.round(2, 1))
                        dve.wait_ge(sum_tiles, Nth(DT * m + j, it, 2).n())
                        if centred:
                            own.did(dve.tensor_tensor(work[:, 2:3, :], work[:, 2:3, :], r, ALU.add))
                        own.link(dve.tensor_tensor(work[:, 0:1, :], r, r, ALU.mult))
                        dve.tensor_tensor(ssq, ssq, tmp[0], ALU.add).then_inc(sum_tiles, 1)

            residual("out", 1, 1, 1.0, False)
            norm(1, "g_ffn", False, False)
            with dve.Fori(0, FT // 2) as it:
                for j in range(2):
                    g, u = Nth(STAGES["gu0"][0] + 2 * j + 1, it, 4), Nth(STAGES["gu0"][1] + 2 * j, it, 4)
                    dve.wait_ge(item_done, g.n(1))
                    dve.wait_ge(bank_read[0], u.round(2, 1))
                    dve.wait_ge(h_lo[j], Nth(j, it, 2).round(2) + OPEN)
                    dve.tensor_tensor(hid[:, j, :], bank[1][:, :], act_g[:, j, :], ALU.mult).then_inc(bank_read[1], 1)
            residual("down0", 2, len(DOWN), 1.0, False)
            norm(2, "g_final", False, True)
            dve.wait_ge(gate_done, 1)
            z, e = tmp[0][0:FOX_HEADS, :], tmp[1][0:FOX_HEADS, :]
            own.link(dve.tensor_scalar(z, sc[0][0:FOX_HEADS, :], small[0:FOX_HEADS, 48:49], None, ALU.add))
            dve.scalar_tensor_tensor(out=e, in0=z, scalar=-1.0, in1=z, op0=ALU.mult, op1=ALU.min).then_inc(gate_a, 1)
            own.link(dve.tensor_scalar(z, z, 0.0, None, ALU.min))
            dve.wait_ge(gate_b, 2)
            own.link(dve.tensor_tensor(e, e, z, ALU.subtract))
            own.link(dve.memset(rstd[0:FOX_HEADS, :], 1.0))
            own.link(dve.tensor_tensor_scan(z, rstd[0:FOX_HEADS, :], e, 0.0, ALU.mult, ALU.add))
            dve.wait_ge(cc_zero, 1)
            for e in range(2):
                h, col = slice(64 * e, 64 * e + 64), 65 * e
                own.did(dve.tensor_tensor(hot[h, :], ident[h, col:col + FOX_HEADS:2],
                                          ident[h, col + 32:col + 32 + FOX_HEADS:2], ALU.add))
            high_c = PTH[0:FOX_HEADS, 0, 0, :]
            own.link(dve.tensor_copy(high_c, z))
            for r in range(0, P, 64):
                dve.tensor_copy(CC[r:r + FOX_HEADS, :], high_c.bitcast(F32)).then_inc(cc_ready, 1)
                dve.tensor_tensor(CC[r + 32:r + 32 + FOX_HEADS, :], z, high_c.bitcast(F32), ALU.subtract).then_inc(cc_ready, 1)
            dve.tensor_copy(onesr[:, :], ones[:, :]).then_inc(cc_ready, 1)
            dve.wait_ge(cc_ready, 5)

            def row_max(n, used):
                c = n % 2
                dve.wait_ge(s_done[c], used.n(1))
                dve.tensor_reduce(small[:, n % 4:n % 4 + 1], sc[c][:, 0:(n // 2 + 1) * P], AX_X, ALU.max, negate=True).then_inc(mx[c], 1)

            def map_lo(b, used, head, i):
                dve.wait_ge(pt_h[b], used.n(1))
                dve.tensor_tensor(PTL[:, head, 0:i + 1, i * P:(i + 1) * P],
                                  tb[b][:, 0:(i + 1) * P].rearrange("p (j q) -> p j q", q=P),
                                  PTH[:, head, 0:i + 1, i * P:(i + 1) * P].bitcast(F32), ALU.subtract).then_inc(pt_l[b], 1)

            def value_lo(layer, u):
                dve.wait_ge(v_hi, u.n(layer * UNITS + 1))
                dve.tensor_tensor(VL[:, u.slot(2), :], bank[1][:, :], VH[:, u.slot(2), :].bitcast(F32), ALU.subtract).then_inc(bank_read[1], 1)

            def bias_rows(u):
                dve.tensor_scalar(Cm[:, u.slot(2), :], CC[:, :], hot[:, at(u)], None, ALU.mult).then_inc(cm_ready, 1)

            def fox_part(iu, au):
                if au is None:
                    bias_rows(iu)
                for sl in range(13):
                    if au is not None:
                        if sl == 2:
                            value_lo(0, au)
                        if sl < 8:
                            row_max(sl, au.times(4, sl // 2))
                        if 1 <= sl < 9:
                            n = sl - 1
                            m = n % 4
                            dve.wait_ge(ex[n % 2], au.times(4, n // 2).n(1) + OPEN)
                            own.link(dve.reciprocal(small[:, 8 + m:9 + m], small[:, 4 + m:5 + m]))
                            k = (n // 2 + 1) * P
                            dve.tensor_scalar(pmap[:, m, 0:k], pmap[:, m, 0:k], small[:, 8 + m:9 + m], None, ALU.mult).then_inc(pn[n % 2], 1)
                        if 2 <= sl < 10:
                            n = sl - 2
                            map_lo(n % 2, au.times(4, n // 2), n % 2, n // 2)
                        if sl >= 11:
                            e = sl - 11
                            r = slice(HEAD * e, HEAD * e + HEAD)
                            dve.wait_ge(o_hi, au.times(2, e).n(1))
                            dve.tensor_tensor(OL[r, at(au), :], ob[e][r, :].rearrange("p (a s) -> p a s", a=1),
                                              OH[r, at(au), :].bitcast(F32), ALU.subtract).then_inc(o_read[e], 1)
                        if sl == 6 and iu is not None:
                            bias_rows(iu)
                    if iu is not None and sl in (4, 8):
                        j = sl // 4 - 1
                        dve.wait_ge(qk_hi, iu.times(2, j).n(1))
                        dve.scalar_tensor_tensor(out=QKL[:, iu.slot(2), j, :], in0=bank[j][:, :], scalar=1.0 if j else HEAD ** -0.5,
                                                 in1=QKH[:, iu.slot(2), j, :].bitcast(F32), op0=ALU.mult,
                                                 op1=ALU.subtract).then_inc(bank_read[j], 1)

            dve.wait_ge(cc_ready, 5)
            weave_units(counted(16), fox_part)
            clear_sums()
            residual("out1", 3, 1, ALPHA, True)
            norm(3, None, True, False)

            def conv_hidden(name, layer):
                with own.loop(FT // 2, 4) as it:
                    for j in range(2):
                        for side, dst in ((0, act_g), (1, hid)):
                            n = it * 2 + (j + FT * side)
                            h = Nth(FT * (layer - 1) + j, it, 2)
                            dve.wait_ge(ff_lin[side], h.n(1))
                            own.link(dve.scalar_tensor_tensor(
                                out=dst[:, j, 1:], in0=bank[side][:, 0:S - 1], scalar=ff_par(layer - 1, 1, n),
                                in1=dst[:, j, 1:], op0=ALU.mult, op1=ALU.add))
                            dve.scalar_tensor_tensor(
                                out=dst[:, j, 2:], in0=bank[side][:, 0:S - 2], scalar=ff_par(layer - 1, 0, n),
                                in1=dst[:, j, 2:], op0=ALU.mult, op1=ALU.add).then_inc(bank_read[side], 1)
                        dve.wait_ge(bank_read[1], Nth(STAGES[name][1] + 2 * j + 1, it, 4).round(2, 1))
                        dve.wait_ge(g_act, h.n(1))
                        dve.tensor_tensor(hid[:, j, :], hid[:, j, :], act_g[:, j, :], ALU.mult).then_inc(hid_ready[j], 1)

            conv_hidden("gu1", 1)
            residual("down1", 4, len(DOWN), ALPHA, True)
            norm(4, None, True, False)
            dve.wait_ge(rope_in, 32)
            def make_lambda():
                for k in range(2):
                    own.link(dve.tensor_tensor(lamr[:, 2 * k * HEAD:(2 * k + 1) * HEAD], lamr[:, 2 * k * HEAD:(2 * k + 1) * HEAD],
                                               lamr[:, (2 * k + 1) * HEAD:(2 * k + 2) * HEAD], ALU.mult))
                    ins = dve.tensor_reduce(lam_row[0][:, k:k + 1], lamr[:, 2 * k * HEAD:(2 * k + 1) * HEAD], AX_X, ALU.add)
                    if k == 0:
                        own.link(ins)
                    else:
                        ins.then_inc(lam_c, 1)
                dve.wait_ge(lam_c, 2)
                own.link(dve.tensor_tensor(lam_row[2], lam_row[1][:, 0:1], lam_row[1][:, 1:2], ALU.subtract))
                dve.tensor_scalar(lam_row[2], lam_row[2], LAMBDA_INIT, None, ALU.add).then_inc(lam_a, 1)
                dve.wait_ge(lam_b, 1)
                dve.tensor_copy(small[:, 49:50], tb[0][:, 0:1]).then_inc(lam_d, 1)
                dve.wait_ge(lam_d, 1)

            def head_scaled(u):
                dve.wait_ge(sub_rs, u.n(1))
                dve.scalar_tensor_tensor(out=osb[:, :], in0=osb[:, :], scalar=small[:, 47:48], in1=osq[:, :],
                                         op0=ALU.mult, op1=ALU.mult).then_inc(sub_n, 1)

            def diff_part(iu, au):
                first = 4 * UNITS
                for sl in range(13):
                    if au is not None:
                        if sl == 2:
                            value_lo(1, au)
                        if sl < 8:
                            row_max(sl, au.times(4, first + sl // 2))
                        if sl == 4 and not (isinstance(au.it, int) and au.base == 0):
                            head_scaled(au + -1)
                        if sl in (2, 4, 6, 8):
                            i = sl // 2 - 1
                            k, m = (i + 1) * P, 2 * (i % 2)
                            for c in range(2):
                                dve.wait_ge(ex[c], au.times(4, first + i).n(1) + OPEN)
                                own.did(dve.reciprocal(small[:, 8 + m + c:9 + m + c], small[:, 4 + m + c:5 + m + c]))
                            own.sync()
                            own.link(dve.tensor_tensor(small[:, 9 + m:10 + m], small[:, 9 + m:10 + m], small[:, 49:50], ALU.mult))
                            own.link(dve.tensor_scalar(pmap[:, m + 1, 0:k], pmap[:, m + 1, 0:k], small[:, 9 + m:10 + m], None, ALU.mult))
                            dve.scalar_tensor_tensor(out=pmap[:, m, 0:k], in0=pmap[:, m, 0:k], scalar=small[:, 8 + m:9 + m],
                                                     in1=pmap[:, m + 1, 0:k], op0=ALU.mult, op1=ALU.subtract).then_inc(pn[i % 2], 1)
                        if sl in (4, 6, 8, 10):
                            i = sl // 2 - 2
                            map_lo(i % 2, au.times(2, first + i // 2), 0, i)
                    if iu is not None and sl in (5, 9):
                        j = (sl - 5) // 4
                        scale = 1.0 if j else HEAD ** -0.5
                        dve.wait_ge(rot_ready, iu.times(8, 4 * j).n(4))
                        dve.wait_ge(qk_lo, iu.times(2, j).n() + OPEN)
                        dve.scalar_tensor_tensor(out=qk[:, :], in0=bank[j][:, :], scalar=scale, in1=rope[:, 0, :],
                                                 op0=ALU.mult, op1=ALU.mult).then_inc(bank_read[j], 1)
                        own.link(dve.scalar_tensor_tensor(out=rot[:, :], in0=rot[:, :], scalar=scale, in1=rope[:, 1, :],
                                                          op0=ALU.mult, op1=ALU.mult))
                        dve.wait_ge(bank_read[j], iu.times(4, STAGES["qkv2"][1] + j).round(2, 1))
                        dve.tensor_tensor(qk[:, :], qk[:, :], rot[:, :], ALU.add).then_inc(roped, 1)
                if au is None:
                    make_lambda()

            weave_units(counted(36), diff_part)
            head_scaled(Nth(UNITS - 1))
            dve.wait_ge(sub_n, UNITS)
            dve.wait_ge(sub_lo, UNITS + OPEN)
            clear_sums()
            residual("out2", 5, 1, ALPHA, True)
            norm(5, None, True, False)
            conv_hidden("gu2", 2)
            residual("down2", 6, len(DOWN), ALPHA, True)
            norm(6, None, True, False)
            for n in range(2 * QT):
                u = Nth(STAGES["back"][1] + n)
                dve.wait_ge(y_turned, n + 1)
                dve.tensor_copy(yout[:, n, :], bank[u.slot(2)][:, :]).then_inc(bank_read[u.slot(2)], 1)


TAP_LOADS = 1 + 8
CONSTS = 3 + 2 * CT + 2 + PAD + 1 + 3


def rope_tables():
    inv = (1.0 / (np.float32(10000.0) ** (np.arange(0, HEAD, 2, dtype=np.float32) / np.float32(HEAD)))).astype(np.float32)
    ang = (np.arange(S, dtype=np.float32)[None, :] * inv[:, None]).astype(np.float32)
    cos, sin = np.cos(ang).astype(np.float32), np.sin(ang).astype(np.float32)
    return np.stack([np.concatenate([cos, cos, cos, cos]), np.concatenate([-sin, sin, -sin, sin])])


NAMES = ["x", "g_mix", "w_in", "b_in", "w_dw", "b_dw", "ln_g", "ln_b", "w_pool", "s_pool", "w_out", "g_ffn",
         "w_gate", "w_up", "w_down", "g_final", "a_w_in_2", "a_b_f_2", "a_w_out_2", "kv_w_2", "b_w_q_2",
         "b_lambda_2", "b_subln_g_2", "b_w_out_2", "ffn_w_in_2", "ffn_conv_w_2", "ffn_conv_b_2",
         "ffn_w_out_2", "ln_attn_g_2", "ln_attn_b_2", "ln_ffn_g_2", "ln_ffn_b_2"]


def kernel(**inputs):
    import concourse.bacc as bacc
    from concourse.bass_utils import run_bass_kernel_spmd

    nc = bacc.Bacc("TRN2", target_bir_lowering=False, num_devices=1)
    arrays = {name: np.ascontiguousarray(inputs[name]) for name in NAMES}
    arrays["rope"] = rope_tables()
    dram = {name: nc.dram_tensor(f"in_{name}", a.shape, mybir.dt.from_np(a.dtype), kind="ExternalInput").ap()
            for name, a in arrays.items()}
    out = nc.dram_tensor("y", (1, S, D), F32, kind="ExternalOutput").ap()
    two_blocks(nc, dram, out)
    r = run_bass_kernel_spmd(nc, [{f"in_{name}": a for name, a in arrays.items()}], core_ids=[0])
    return r.results[0]["y"]
```

```python
from contextlib import ExitStack, contextmanager

import numpy as np
import concourse.bass as bass
from concourse import mybir

P = 128
S = 512
D = 1024
DT = D // P
QT = S // P
C_CONV = 512
CT = C_CONV // P
TAPS = 31
WINDOWS = (2, 4, 8, 16)
PAD = 16
D_FF = 2816
FT = D_FF // P
HEAD = 64
FOX_HEADS = D // HEAD
CHUNK = 64
RMS_EPS, LN_EPS, SUB_EPS = 1e-6, 1e-5, 1e-5
ALPHA = 4.0 ** 0.25
LAMBDA_INIT = 0.8 - 0.6 * float(np.exp(-0.3))
MASKED = -1.0e30
UNITS = DT
UNIT = (8, 8, 4, 4)
LN_EXP_SET = 6
DOWN = (6, 6, 5, 5)
assert sum(DOWN) == FT

F32 = mybir.dt.float32
F32R = mybir.dt.float32r
BF16 = mybir.dt.bfloat16
ALU = mybir.AluOpType
ACT = mybir.ActivationFunctionType
AX_X = mybir.AxisListType.X

OPEN = 1
RAW = 4
SPLIT = 2

STAGES = {}
_item, _turn = 0, DT
for _name, _n, _t in (("in", 12, 12), ("out", 8, 8), ("gu0", 2 * FT, 2 * FT), ("down0", 8 * len(DOWN), 8),
                      ("qkv1", 4 * UNITS, 4 * UNITS), ("out1", 8, 8), ("gu1", 2 * FT, 2 * FT),
                      ("down1", 8 * len(DOWN), 8), ("qkv2", 4 * UNITS, 4 * UNITS), ("out2", 8, 8),
                      ("gu2", 2 * FT, 2 * FT), ("down2", 8 * len(DOWN), 8)):
    STAGES[_name] = (_item, _turn)
    _item, _turn = _item + _n, _turn + _t
IN_ORDER = [("gate", 0), ("value", 0), ("pool", 0), ("pool", 1), ("gate", 1), ("value", 1),
            ("gate", 3), ("value", 3), ("gate", 2), ("value", 2), ("pool", 2), ("pool", 3)]
PE_TILE = 3
X_LOADS = 4
FOX_STEPS = (2,) * 12
DIFF_STEPS = (2, 2, 2, 2, 2, 2, 2, 2, 1, 3, 3, 1)
DIAG_CHUNK = 8
NORMS = ["x", "conv", "out", "down0", "out1", "down1", "out2", "down2"]
NORM = [0, 2, 3, 4, 5, 6, 7]
CENTRED = [NORMS.index(x) for x in ("conv", "out1", "down1", "out2", "down2")]
LAST_TURN = [STAGES[x][1] + DT if x in STAGES else None for x in NORMS]
SIZES = {"down0": 2 * DOWN, "down1": 2 * DOWN, "down2": 2 * DOWN}

ROWS0 = {}
_row = 0
for _name, _n in (("g_mix", 8), ("b_in", 12), ("b_dw", 4), ("ln_g", 4), ("ln_b", 4), ("s_pool", 4),
                  ("g_ffn", 8), ("g_final", 8), ("ln_attn_g_2", 16), ("ln_attn_b_2", 16),
                  ("ln_ffn_g_2", 16), ("ln_ffn_b_2", 16), ("b_subln_g_2", 1)):
    ROWS0[_name] = (_row, _n)
    _row += _n
ROWS_OF = [_row, TAPS * CT, 2 * 44, 2 * 44, 2 * 44, 2 * 44]


class Nth:

    def __init__(self, base, it=0, per=0):
        if isinstance(it, int):
            base, it, per = base + it * per, 0, 0
        self.base, self.it, self.per = base, it, per

    def __add__(self, k):
        return Nth(self.base + k, self.it, self.per)

    def times(self, m, k=0):
        return Nth(self.base * m + k, self.it, self.per * m)

    def n(self, k=0):
        return self.base + k if isinstance(self.it, int) else self.it * self.per + (self.base + k)

    def slot(self, size):
        assert self.per % size == 0
        return self.base % size

    def round(self, size, k=0):
        if isinstance(self.it, int):
            return self.base // size + k
        assert self.per % size == 0
        return self.it * (self.per // size) + (self.base // size + k)


class Chain:

    def __init__(self, eng, sem):
        self.eng, self.sem, self.count, self.it, self.per = eng, sem, 0, None, 0

    def did(self, ins):
        ins.then_inc(self.sem, 1)
        self.count += 1

    def sync(self, but=0):
        if self.it is None:
            self.eng.wait_ge(self.sem, self.count - but)
        else:
            self.eng.wait_ge(self.sem, self.it * self.per + self.count)

    def link(self, ins):
        self.did(ins)
        self.sync()

    @contextmanager
    def loop(self, times, per):
        start = self.count
        with self.eng.Fori(0, times) as it:
            self.it, self.per = it, per
            yield it
            assert self.count - start == per, (self.count - start, per)
        self.count, self.it = start + per * times, None


def two_blocks(nc, A, out):
    ctx = ExitStack()
    with ctx:
        def sb(name, shape, dt=F32, stack=None):
            return (stack or ctx).enter_context(nc.sbuf_tensor(name, shape, dt))

        def pb(name, dt=F32):
            return ctx.enter_context(nc.psum_tensor(name, [P, 512], dt))

        def sem(name):
            return ctx.enter_context(nc.semaphore(name))

        def sems(name, n):
            return [sem(f"{name}{i}") for i in range(n)]

        xres = sb("xres", [P, DT, S])
        XH = sb("XH", [P, DT, S], F32R)
        XL = sb("XL", [P, DT, S], F32R)
        raw = sb("raw", [P, RAW, DT, P])
        WH = sb("WH", [P, SPLIT, DT, P], F32R)
        WL = sb("WL", [P, SPLIT, DT, P], F32R)
        par = sb("par", [P, 6 * P])
        ident = sb("ident", [P, P])
        ones = sb("ones", [P, P])
        identb = sb("identb", [P, P], BF16)
        masks = sb("masks", [P, 2, P], BF16)
        work = sb("work", [P, 6, S])
        small = sb("small", [P, 96])
        tmp = [work[:, 0, :], work[:, 1, :]]
        ring = [work[:, i, :] for i in (0, 1, 4, 5)]
        ssum, ssq = work[:, 2, :], work[:, 3, :]
        odd_taps = work[:, 4, :]
        mean, square, var, rstd = (small[:, 4 * i + 16:4 * i + 20] for i in range(4))

        first = ExitStack()
        xin = sb("xin", [P, QT, D], stack=first)
        prow = sb("prow", [P, 6, P], stack=first)
        upad = sb("upad", [P, CT, TAPS - 1 + S], stack=first)
        sig = sb("sig", [P, 2, S], stack=first)
        vconv = sb("vconv", [P, CT, S], stack=first)
        ppad = sb("ppad", [P, CT, PAD + S], stack=first)
        psums = sb("psums", [P, 2, PAD + S], stack=first)
        ypool = sb("ypool", [P, CT, S], stack=first)
        wpool = sb("wpool", [P, CT, P], stack=first)
        mixp = sb("mixp", [P, 2, S], stack=first)
        tap_h = sb("tap_h", [P, TAPS], F32R, stack=first)
        tap_l = sb("tap_l", [P, TAPS], stack=first)
        dg_h = sb("dg_h", [P, TAPS, P], F32R, stack=first)
        dg_l = sb("dg_l", [P, TAPS, P], F32R, stack=first)
        u_h = sb("u_h", [P, TAPS - 1 + S], F32R, stack=first)
        u_l = sb("u_l", [P, TAPS - 1 + S], F32R, stack=first)
        cnts = sb("cnts", [P, PAD], stack=first)
        icnt = sb("icnt", [P, PAD], stack=first)
        first.close()
        ffn = ExitStack()
        HH = sb("HH", [P, FT, S], F32R, stack=ffn)
        HL = sb("HL", [P, FT, S], F32R, stack=ffn)
        act_g = sb("act_g", [P, 2, S], stack=ffn)
        hid = sb("hid", [P, 2, S], stack=ffn)
        ffn.close()
        att = ExitStack()
        QKH = sb("QKH", [P, 2, 2, S], F32R, stack=att)
        QKL = sb("QKL", [P, 2, 2, S], F32R, stack=att)
        VH = sb("VH", [P, 2, S], F32R, stack=att)
        VL = sb("VL", [P, 2, S], F32R, stack=att)
        PTH = sb("PTH", [P, 2, QT, S], F32R, stack=att)
        PTL = sb("PTL", [P, 2, QT, S], F32R, stack=att)
        OH = sb("OH", [P, DT, S], F32R, stack=att)
        OL = sb("OL", [P, DT, S], F32R, stack=att)
        pmap = sb("pmap", [P, 4, S], stack=att)
        Cm = sb("Cm", [P, 2, S], F32R, stack=att)
        wf = sb("wf", [P, DT, FOX_HEADS], stack=att)
        hot = sb("hot", [P, FOX_HEADS // 2], stack=att)
        onesr = sb("onesr", [P, P], F32R, stack=att)
        rope = sb("rope", [P, 2, S], stack=att)
        lamr = sb("lamr", [1, 4 * HEAD], stack=att)
        att.close()
        vt = work[:, 0, :]
        rot = work[:, 1, :]
        qk = work[:, 2, :]
        osb = work[:, 3, :]
        osq = work[:, 4, :]
        CC = work[:, 5, :]
        back = ExitStack()
        yout = sb("yout", [P, 2 * QT, S], stack=back)
        back.close()
        lam_row = [small[0:1, 40:42], small[0:1, 42:44], small[0:1, 44:45]]

        bank = [pb("bank0"), pb("bank1")]
        sc = [pb("score0"), pb("score1")]
        tb = [pb("turned0"), pb("turned1")]
        ob = [pb("attended0"), pb("attended1")]

        y_bank = tb + ob + bank + sc

        x_in = sems("x_in", X_LOADS)
        rows0_in = sem("rows0_in")
        par_in = sem("par_in")
        small_in = sem("small_in")
        wf_in = sem("wf_in")
        rope_in = sem("rope_in")
        w_landed = sems("w_landed", RAW)
        first_map = sem("first_map")
        w_hi = sem("w_hi")
        w_lo = sem("w_lo")
        item_done = sem("item_done")
        bank_read = sems("bank_read", 2)
        consts = sem("consts")
        turned_x = sem("turned_x")
        turned_par = sem("turned_par")
        par_ok = sem("par_ok")
        dv = sem("dv")
        av = sem("av")
        gv = sem("gv")
        sum_tiles = sem("sum_tiles")
        plain_sums = sem("plain_sums")
        last_squared = sem("last_squared")
        stats_done = sem("stats_done")
        var_ready = sem("var_ready")
        rstd_ready = sem("rstd_ready")
        shift_ready = sem("shift_ready")
        rstd_wide = sem("rstd_wide")
        mean_wide = sem("mean_wide")
        xn_ready = sem("xn_ready")
        x_hi = sem("x_hi")
        x_lo = sem("x_lo")
        cv_sum = sem("cv_sum")
        cv_n, cv_hi, cv_lo = sem("cv_n"), sem("cv_hi"), sem("cv_lo")
        squared = sem("squared")
        taps_split = sem("taps_split")
        diag_h, diag_l = sem("diag_h"), sem("diag_l")
        u_hi, u_lo = sem("u_hi"), sem("u_lo")
        pe_conv = sem("pe_conv")
        pe_conv_out = sem("pe_conv_out")
        ypool_ready, pool_mm = sem("ypool_ready"), sem("pool_mm")
        pool_out, pool_hi, pool_lo = sem("pool_out"), sem("pool_hi"), sem("pool_lo")
        h_hi = sem("h_hi")
        h_lo = sems("h_lo", 2)
        g_act = sem("g_act")
        ff_lin = sems("ff_lin", 2)
        gate_done = sem("gate_done")
        gate_a, gate_b = sem("gate_a"), sem("gate_b")
        cc_zero = sem("cc_zero")
        hid_ready = sems("hid_ready", 2)
        roped = sem("roped")
        rot_ready = sem("rot_ready")
        cc_ready = sem("cc_ready")
        cm_ready = sem("cm_ready")
        v_turned = sem("v_turned")
        v_hi = sem("v_hi")
        qk_hi = sem("qk_hi")
        qk_lo = sem("qk_lo")
        s_done = sems("s_done", 2)
        mx = sems("mx", 2)
        ex = sems("ex", 2)
        pn = sems("pn", 2)
        t_done = sems("t_done", 2)
        pt_h, pt_l = sems("pt_h", 2), sems("pt_l", 2)
        o_done = sems("o_done", 2)
        o_hi = sem("o_hi")
        o_read = sems("o_read", 2)
        lam_a, lam_b, lam_c, lam_d = (sem(f"lam_{x}") for x in "abcd")
        sub_sq, sub_var, sub_ln, sub_rs, sub_n, sub_hi, sub_lo = (
            sem(x) for x in ("sub_sq", "sub_var", "sub_ln", "sub_rs", "sub_n", "sub_hi", "sub_lo"))
        y_turned = sem("y_turned")
        y_copied = sems("y_copied", 2)
        y_out = sem("y_out")

        slots = [*h_lo, *hid_ready, *ex, *pt_l, *o_read, qk_lo, sub_lo]

        def pcol(name, t):
            return par[:, ROWS0[name][0] + t:ROWS0[name][0] + t + 1]

        def tap(j, c):
            return par[:, P + j * CT + c:P + j * CT + c + 1]

        def in_item(kind, c):
            return IN_ORDER.index((kind, c))

        def turned_rows(i):
            return ob[1][:, 0:ROWS_OF[0]] if i == 0 else tb[i // 4][:, i % 4 * P:i % 4 * P + ROWS_OF[i]]

        def ff_par(layer, what, n):
            return par[:, bass.ds(n + ((2 + 2 * layer + what // 2) * P + (what % 2) * 44), 1)]

        def cols(w):
            return w.rearrange("(k p) n -> p k n", p=P)

        w_in, w_out0 = cols(A["w_in"][0]), cols(A["w_out"][0])
        w_gate, w_up = cols(A["w_gate"][0]), cols(A["w_up"][0])
        a_in, a_out = cols(A["a_w_in_2"][0]), cols(A["a_w_out_2"][0])
        kv_w, b_q, b_out = cols(A["kv_w_2"]), cols(A["b_w_q_2"][0]), cols(A["b_w_out_2"][0])
        ff_in = [cols(A["ffn_w_in_2"][i]) for i in range(2)]
        downs = [cols(A["w_down"][0])] + [cols(A["ffn_w_out_2"][i]) for i in range(2)]

        def loop_with_sizes(name, per):
            own_sizes = SIZES.get(name, (DT,) * per)
            return [own_sizes[j + 2] if j + 2 < per else max(own_sizes[j + 2 - per], DT) for j in range(per)]

        def halves(kt):
            return slice(0, kt - kt // 2), slice(kt - kt // 2, kt)

        def at(u):
            return bass.ds(u.n(), 1)

        def weave_units(Fori, part):
            part(Nth(0), None)
            part(Nth(1), Nth(0))
            with Fori(0, (UNITS - 2) // 2) as it:
                for j in range(2):
                    part(Nth(2 + j, it, 2), Nth(1 + j, it, 2))
            part(None, Nth(UNITS - 1))

        block = ctx.enter_context(nc.Block())

        @block.sync
        def _(sp):
            def load(g, src, kt=DT):
                if not (isinstance(g.it, int) and g.base < RAW):
                    sp.wait_ge(w_lo, g.times(2).n(2 * (1 - RAW)))
                sp.dma_start(raw[:, g.slot(RAW), 0:kt, 0:src.shape[2]], src).then_inc(w_landed[g.slot(RAW)], 16)

            def stage(name, times, per, source):
                with sp.Fori(0, times) as it:
                    for j in range(per):
                        load(Nth(STAGES[name][0] + j, it, per), *source(it, j))

            xv = A["x"][0].rearrange("(q p) d -> p q d", p=P)
            for i in range(X_LOADS):
                c = slice(i * D // X_LOADS, (i + 1) * D // X_LOADS)
                sp.dma_start(xin[:, :, c], xv[:, :, c]).then_inc(x_in[i], 16)
            def load_in(n):
                kind, c = IN_ORDER[n]
                c += {"gate": CT, "value": 0, "pool": 2 * CT}[kind]
                load(Nth(n), w_in[:, :, c * P:(c + 1) * P])

            def rows(i, r, src, signal):
                n = src.shape[0]
                sp.dma_start(prow[r:r + n, i, :], src).then_inc(signal, 16)

            load_in(0)
            load_in(1)
            for name, (r, n) in ROWS0.items():
                src = A[name]
                if len(src.shape) == 1:
                    src = src.rearrange("(t p) -> t p", p=P)
                else:
                    src = src.rearrange("l (t p) -> (l t) p", p=P)
                rows(0, r, src, rows0_in)
            load_in(2)
            load_in(3)
            rows(1, 0, A["w_dw"][0].rearrange("j (c p) -> (j c) p", p=P), par_in)
            for layer in range(2):
                taps = A["ffn_conv_w_2"][layer].rearrange("j (c p) -> j c p", p=P)
                rows(2 + 2 * layer, 0, taps[0], par_in)
                rows(2 + 2 * layer, 44, taps[1], par_in)
                rows(3 + 2 * layer, 0, taps[2], par_in)
                rows(3 + 2 * layer, 44, A["ffn_conv_b_2"][layer].rearrange("(c p) -> c p", p=P), par_in)
            sp.dma_start(wpool[:, :, :], A["w_pool"][0].rearrange("i g h -> g i h")).then_inc(small_in, 16)
            for n in range(4, 12):
                load_in(n)

            def tiles(w, first=0):
                def source(it, j):
                    return (w[:, :, bass.ds(it * 4 * P + (first + j) * P, P)],)
                return source

            def pairs(wa, wb, first_b=0):
                def source(it, j):
                    return ((wa, wb)[j % 2][:, :, bass.ds(it * 2 * P + (j // 2 + (first_b if j % 2 else 0)) * P, P)],)
                return source

            def down(w):
                def source(it, j):
                    k0, kt = sum(DOWN[:j % 4]), DOWN[j % 4]
                    return (w[:, k0:k0 + kt, bass.ds(it * 2 * P + j // 4 * P, P)], kt)
                return source

            stage("out", 2, 4, tiles(w_out0))
            stage("gu0", FT // 2, 4, pairs(w_gate, w_up))
            stage("down0", DT // 2, 8, down(downs[0]))
            def units(name, wq, wk, wv):
                with sp.Fori(0, UNITS) as it:
                    for j in range(4):
                        g = Nth(STAGES[name][0] + j, it, 4)
                        if j < 2 and name == "qkv2":
                            src = (wq, wk)[j]
                            sp.wait_ge(w_lo, g.times(2).n(2 * (1 - RAW)))
                            sp.dma_start(raw[:, g.slot(RAW), :, 0:HEAD],
                                         src[:, :, bass.ds(it * HEAD, HEAD)]).then_inc(first_map, 16)
                            sp.wait_ge(first_map, it * 32 + 16 * (j + 1))
                            sp.dma_start(raw[:, g.slot(RAW), :, HEAD:P],
                                         src[:, :, bass.ds(it * HEAD + D // 2, HEAD)]).then_inc(w_landed[g.slot(RAW)], 16)
                        elif j < 2:
                            load(g, (wq, wk)[j][:, :, bass.ds(it * P, P)])
                        else:
                            load(g, wv[:, 4 * (j - 2):4 * (j - 1), bass.ds(it * P, P)], 4)

            units("qkv1", a_in[:, :, 0:D], a_in[:, :, D:2 * D], a_in[:, :, 2 * D:3 * D])
            stage("out1", 2, 4, tiles(a_out))
            stage("gu1", FT // 2, 4, pairs(ff_in[0], ff_in[0], FT))
            stage("down1", DT // 2, 8, down(downs[1]))
            units("qkv2", b_q, kv_w[:, :, 0:D], kv_w[:, :, D:2 * D])
            stage("out2", 2, 4, tiles(b_out))
            stage("gu2", FT // 2, 4, pairs(ff_in[1], ff_in[1], FT))
            stage("down2", DT // 2, 8, down(downs[2]))
            ov = out[0].rearrange("(q p) d -> p q d", p=P)
            for n in range(2 * QT):
                half, q = n // QT, n % QT
                sp.wait_ge(y_copied[n % 2], n // 2 + 1)
                sp.dma_start(ov[:, q, half * S:(half + 1) * S], yout[:, n, :]).then_inc(y_out, 16)
            sp.wait_ge(y_out, 16 * 2 * QT)

        @block.gpsimd
        def _(pool):
            own = Chain(pool, gv)

            def low(g, kt=DT):
                s = g.slot(SPLIT)
                for half in range(2):
                    ks = halves(kt)[half]
                    pool.wait_ge(w_hi, g.times(2).n(half + 1))
                    pool.tensor_tensor(WL[:, s, ks, :], raw[:, g.slot(RAW), ks, :], WH[:, s, ks, :].bitcast(F32),
                                       ALU.subtract).then_inc(w_lo, 1)

            pool.memset(ident[:, :], 0.0).then_inc(consts, 1)
            pool.memset(ones[:, :], 1.0).then_inc(consts, 1)
            pool.wait_ge(consts, 1)
            pool.affine_select(out=ident[:, :], in_=ident[:, :], compare_op=ALU.not_equal, fill=1.0,
                               base=0, pattern=[[-1, P]], channel_multiplier=1).then_inc(consts, 1)
            for c in range(CT):
                pool.memset(ppad[:, c, 0:PAD], 0.0).then_inc(consts, 1)
                pool.memset(upad[:, c, 0:TAPS - 1], 0.0).then_inc(consts, 1)
            for c in range(2):
                pool.memset(psums[:, c, 0:PAD], 0.0).then_inc(consts, 1)
            for c in range(PAD):
                pool.memset(cnts[:, c:c + 1], float(c + 1)).then_inc(consts, 1)
            pool.memset(masks[:, :, :], 0.0).then_inc(consts, 1)
            done = 3 + 2 * CT + 2 + PAD + 1
            pool.wait_ge(consts, done)
            pool.affine_select(out=masks[:, 0, :], in_=masks[:, 0, :], compare_op=ALU.is_ge, fill=MASKED,
                               base=0, pattern=[[-1, P]], channel_multiplier=1).then_inc(consts, 1)
            pool.memset(masks[0:CHUNK, 1, CHUNK:P], MASKED).then_inc(consts, 1)
            pool.tensor_copy(identb[:, :], ident[:, :]).then_inc(consts, 1)
            for n, q in enumerate(slots):
                pool.memset(small[:, 64 + n:65 + n], 0.0).then_inc(q, OPEN)

            def lows_of_x(m, src):
                for t in range(DT):
                    pool.wait_ge(x_hi, DT * m + t + 1)
                    pool.tensor_tensor(XL[:, t, :], src(t), XH[:, t, :].bitcast(F32),
                                       ALU.subtract).then_inc(x_lo, 1)

            low(Nth(0))
            low(Nth(1))
            lows_of_x(0, lambda t: ring[t % 4])

            def pooled(i):
                w = WINDOWS[i]
                n = in_item("pool", i)
                pool.wait_ge(bank_read[n % 2], (DT + n) // 2 + 1)
                src, d, side = ppad[:, i, :], 1, 0
                while d < w:
                    dst = psums[:, side, :]
                    own.link(pool.tensor_tensor(dst[:, PAD:], src[:, PAD:], src[:, PAD - d:PAD + S - d], ALU.add))
                    src, d, side = dst, 2 * d, 1 - side
                own.did(pool.tensor_tensor(ypool[:, i, 0:w], src[:, PAD:PAD + w], icnt[:, 0:w], ALU.mult))
                own.link(pool.tensor_scalar(ypool[:, i, w:], src[:, PAD + w:], 1.0 / w, None, ALU.mult))
                pool.tensor_tensor(ypool[:, i, :], ypool[:, i, :], ppad[:, i, PAD:], ALU.subtract).then_inc(ypool_ready, 1)

            for n in range(12):
                low(Nth(n + 2))
                if n == 2:
                    pool.wait_ge(taps_split, 2)
                if 2 <= n < 6:
                    for a in [(n - 2) * DIAG_CHUNK]:
                        k = min(DIAG_CHUNK, TAPS - a)
                        pool.tensor_tensor(dg_l[:, a:a + k, :], ident[:, :].unsqueeze(1).broadcast_to([P, k, P]),
                                           tap_l[:, a:a + k].unsqueeze(2).broadcast_to([P, k, P]), ALU.mult).then_inc(diag_l, 1)
                if n == 5:
                    pool.wait_ge(cv_n, 1)
                if n == 6:
                    pooled(0)
                if n == 8:
                    pooled(1)
                if n == 10:
                    pool.wait_ge(u_hi, 1)
                    pool.tensor_tensor(u_l[:, :], upad[:, PE_TILE, :], u_h[:, :].bitcast(F32), ALU.subtract).then_inc(u_lo, 1)
            pooled(2)
            pooled(3)
            for i in range(CT):
                pool.wait_ge(pool_hi, i + 1)
                pool.tensor_tensor(XL[:, CT + i, :], mixp[:, i % 2, :], XH[:, CT + i, :].bitcast(F32),
                                   ALU.subtract).then_inc(pool_lo, 1)
            for c in range(CT):
                pool.wait_ge(cv_hi, c + 1)
                pool.tensor_tensor(XL[:, c, :], vconv[:, c, :], XH[:, c, :].bitcast(F32),
                                   ALU.subtract).then_inc(cv_lo, 1)

            def lows(name, times, per):
                with pool.Fori(0, times) as it:
                    for j, kt in enumerate(loop_with_sizes(name, per)):
                        low(Nth(STAGES[name][0] + j + 2, it, per), kt)

            def lows_of_hidden(name, layer):
                with pool.Fori(0, FT // 2) as it:
                    for j in range(2):
                        low(Nth(STAGES[name][0] + 2 * j + 2, it, 4))
                        low(Nth(STAGES[name][0] + 2 * j + 3, it, 4))
                        h = Nth(FT * layer + j, it, 2)
                        pool.wait_ge(h_hi, h.n(1))
                        pool.tensor_tensor(HL[:, bass.ds(it * 2 + j, 1), :], hid[:, j:j + 1, :],
                                           HH[:, bass.ds(it * 2 + j, 1), :].bitcast(F32), ALU.subtract).then_inc(h_lo[j], 1)

            lows("out", 2, 4)
            lows_of_x(1, lambda t: ring[t % 4])
            lows_of_hidden("gu0", 0)
            lows("down0", DT // 2, 8)
            lows_of_x(2, lambda t: xres[:, t, :])
            pool.memset(CC[:, :], 0.0).then_inc(cc_zero, 1)

            with pool.Fori(0, UNITS) as it:
                for j in range(4):
                    low(Nth(STAGES["qkv1"][0] + j + 2, it, 4), (UNIT[2:] + UNIT[:2])[j])
            lows("out1", 2, 4)
            lows_of_x(3, lambda t: xres[:, t, :])
            lows_of_hidden("gu1", 1)
            lows("down1", DT // 2, 8)
            lows_of_x(4, lambda t: xres[:, t, :])

            def sub_low(u):
                pool.wait_ge(sub_hi, u.n(1))
                pool.tensor_tensor(OL[:, at(u), :], osb[:, :].rearrange("p (a s) -> p a s", a=1),
                                   OH[:, at(u), :].bitcast(F32), ALU.subtract).then_inc(sub_lo, 1)

            def unit_lows(iu, au):
                for j in range(4):
                    if iu is not None:
                        low(iu.times(4, STAGES["qkv2"][0] + j + 2), (UNIT[2:] + UNIT[:2])[j])
                    if j == 0 and au is not None and not (isinstance(au.it, int) and au.base == 0):
                        sub_low(au + -1)
                    if j < 2 and iu is not None:
                        pool.wait_ge(qk_hi, iu.times(2, 2 * UNITS + j).n(1))
                        pool.tensor_tensor(QKL[:, iu.slot(2), j, :], qk[:, :], QKH[:, iu.slot(2), j, :].bitcast(F32),
                                           ALU.subtract).then_inc(qk_lo, 1)

            weave_units(pool.Fori, unit_lows)
            sub_low(Nth(UNITS - 1))
            lows("out2", 2, 4)
            lows_of_x(5, lambda t: xres[:, t, :])
            lows_of_hidden("gu2", 2)
            lows("down2", DT // 2 - 1, 8)
            for j, kt in enumerate(loop_with_sizes("down2", 8)[:6]):
                low(Nth(STAGES["down2"][0] + 8 * (DT // 2 - 1) + j + 2), kt)

        @block.tensor
        def _(pe):
            def product(out_, wh, wl, xh, xl, start, stop):
                pe.matmul(out_, wh, xl, start=start, stop=False)
                pe.matmul(out_, wh, xh, start=False, stop=False)
                return pe.matmul(out_, wl, xh, start=False, stop=stop)

            def step(g, b, hi, lo, k0, k, kt, start, stop):
                if k == 0:
                    pe.wait_ge(w_lo, g.times(2).n(1))
                if k == kt - kt // 2:
                    pe.wait_ge(w_lo, g.times(2).n(2))
                s = g.slot(SPLIT)
                mm = product(bank[b][:, :], WH[:, s, k, :], WL[:, s, k, :], hi[:, k0 + k, :], lo[:, k0 + k, :],
                             start and k == 0, stop and k == kt - 1)
                if k == kt - 1:
                    mm.then_inc(item_done, 1)

            def item(g, b, hi, lo, k0, kt, start, stop):
                for k in range(kt):
                    step(g, b, hi, lo, k0, k, kt, start, stop)

            def bank_free(u):
                pe.wait_ge(bank_read[u.slot(2)], u.round(2))

            def two_items(name, ready, order=tuple(range(DT))):
                g, u = STAGES[name]
                for k in order:
                    ready(k)
                    for j in range(2):
                        if k == order[0]:
                            bank_free(Nth(u + j))
                            pe.wait_ge(w_lo, 2 * (g + j + 1))
                        s = (g + j) % SPLIT
                        mm = product(bank[(u + j) % 2][:, :], WH[:, s, k, :], WL[:, s, k, :], XH[:, k, :], XL[:, k, :],
                                     k == order[0], k == order[-1])
                        if k == order[-1]:
                            mm.then_inc(item_done, 1)

            def whole(name, j, it=0, per=4, x=(XH, XL)):
                u = Nth(STAGES[name][1] + j, it, per)
                bank_free(u)
                item(Nth(STAGES[name][0] + j, it, per), u.slot(2), *x, 0, DT, True, True)

            def stage(name, times, ready=None, x=(XH, XL), order=tuple(range(DT))):
                if ready:
                    two_items(name, ready, order)
                for j in range(2, 4):
                    whole(name, j, x=x)
                with pe.Fori(1, times) as it:
                    for j in range(4):
                        whole(name, j, it, x=x)

            def normed(m):
                return lambda k: pe.wait_ge(x_lo, DT * m + k + 1)

            def down(name, layer):
                early = sum(DOWN[:3])
                for p, q in enumerate(h_lo):
                    pe.wait_ge(q, layer * FT // 2 + (early + 1 - p) // 2 + OPEN)
                with pe.Fori(0, DT // 2) as it:
                    for j in range(8):
                        u = Nth(STAGES[name][1] + j // 4, it, 2)
                        if j % 4 == 0:
                            bank_free(u)
                        if j == 3:
                            for q in h_lo:
                                pe.wait_ge(q, (layer + 1) * FT // 2 + OPEN)
                        item(Nth(STAGES[name][0] + j, it, 8), u.slot(2), HH, HL, sum(DOWN[:j % 4]), DOWN[j % 4],
                             j % 4 == 0, j % 4 == 3)

            def stats(n, ready):
                def over_channels(first, x):
                    for q in range(QT):
                        mm = pe.matmul(sc[0][:, first + q:first + q + 1], x[:, q * P:(q + 1) * P], ones[:, 0:1],
                                       start=True, stop=True)
                    return mm

                if n in CENTRED:
                    pe.wait_ge(plain_sums, CENTRED.index(n) + 1)
                    over_channels(QT, ssum)
                ready()
                over_channels(0, ssq).then_inc(stats_done, 1)

                def widen(to, numbers):
                    for q in range(QT):
                        mm = pe.transpose(to[:, q * P:(q + 1) * P], numbers[:, q:q + 1].broadcast_to([P, P]), ident[:, :])
                    return mm

                pe.wait_ge(rstd_ready, n + 1)
                widen(sc[0], rstd).then_inc(rstd_wide, 1)
                if n in CENTRED:
                    pe.wait_ge(shift_ready, CENTRED.index(n) + 1)
                    widen(sc[1], mean).then_inc(mean_wide, 1)

            def norm_stats(m):
                stats(NORM[m], lambda: pe.wait_ge(sum_tiles, DT * (m + 1)))

            pe.wait_ge(consts, 3)
            for t in range(DT):
                pe.wait_ge(x_in[t * X_LOADS // DT], 16)
                if t >= 2:
                    pe.wait_ge(bank_read[t % 2], t // 2)
                for q in range(QT):
                    mm = pe.transpose(bank[t % 2][:, q * P:(q + 1) * P], xin[:, q, t * P:(t + 1) * P], ident[:, :])
                mm.then_inc(turned_x, 1)
            def turn_rows(i):
                n = ROWS_OF[i]
                return pe.transpose(turned_rows(i), prow[0:n, i, :], ident[0:n, 0:n])

            pe.wait_ge(rows0_in, 16 * len(ROWS0))
            turn_rows(0).then_inc(turned_par, 1)
            norm_stats(0)
            pe.wait_ge(par_in, 16 * TAP_LOADS)
            for i in range(1, len(ROWS_OF)):
                mm = turn_rows(i)
            mm.then_inc(turned_par, 1)
            two_items("in", normed(0))
            for n in range(2, 12):
                whole("in", n)
            pe.wait_ge(u_lo, 1)
            pe.wait_ge(diag_h, TAPS)
            pe.wait_ge(diag_l, -(-TAPS // DIAG_CHUNK))
            for j in range(TAPS):
                mm = product(ob[0][:, :], dg_h[:, j, :], dg_l[:, j, :], u_h[:, j:j + S], u_l[:, j:j + S], j == 0, j == TAPS - 1)
            mm.then_inc(pe_conv, 1)
            pe.wait_ge(small_in, 16)
            pe.wait_ge(par_ok, 1)
            for i in range(CT):
                pe.wait_ge(ypool_ready, i + 1)
                if i >= 2:
                    pe.wait_ge(pool_out, i - 1)
                pe.matmul(tb[i % 2][:, :], wpool[:, i, :], ypool[:, i, :], start=True, stop=True).then_inc(pool_mm, 1)
            stats(NORMS.index("conv"), lambda: pe.wait_ge(cv_sum, CT))
            pe.wait_ge(pool_lo, CT)
            stage("out", 2, lambda k: pe.wait_ge(cv_lo, k + 1) if k < CT else None,
                  order=(*range(CT, DT), *range(CT)))
            norm_stats(1)
            stage("gu0", FT // 2, normed(1))
            down("down0", 0)
            norm_stats(2)
            pe.wait_ge(wf_in, 32)
            for k in range(DT):
                pe.wait_ge(xn_ready, 2 * DT + k + 1)
                mm = pe.matmul(ob[0][0:FOX_HEADS, :], wf[:, k, :], xres[:, k, :], start=(k == 0), stop=(k == DT - 1))
            mm.then_inc(gate_done, 1)

            def unit_steps(name, u):
                turn0 = STAGES[name][1]
                item0 = STAGES[name][0]
                for tile in range(3):
                    for k in range(DT):
                        part, kk = (tile, k) if tile < 2 else (2 + k // 4, k % 4)
                        if k == 0:
                            bank_free(u.times(4, turn0 + tile))
                        step(u.times(4, item0 + part), tile % 2, XH, XL, k - kk, kk, UNIT[part],
                             part < 3, part != 2)
                        yield

            def unit_steps_fed(name, m):
                two_items(name, normed(m))
                turn0, item0 = STAGES[name][1], STAGES[name][0]
                bank_free(Nth(turn0 + 2))
                for k in range(DT):
                    step(Nth(item0 + 2 + k // 4), 0, XH, XL, k - k % 4, k % 4, 4, k < 4, k >= 4)

            def turn_v(name, u):
                pe.wait_ge(bank_read[0], u.times(4, STAGES[name][1] + 2).round(2, 1))
                bank_free(u.times(4, STAGES[name][1] + 3))
                for q in range(QT):
                    mm = pe.transpose(bank[1][:, q * P:(q + 1) * P], vt[:, q * P:(q + 1) * P], ident[:, :])
                mm.then_inc(v_turned, 1)

            def score(n, used, slot, rows, i, mask, bias):
                c = n % 2
                q, k = slice(i * P, (i + 1) * P), slice(0, (i + 1) * P)
                pe.wait_ge(ex[c], used.n() + OPEN)
                pe.matmul(sc[c][:, k], QKH[rows, slot, 0, q], QKL[rows, slot, 1, k], start=True, stop=False)
                pe.matmul(sc[c][:, k], QKH[rows, slot, 0, q], QKH[rows, slot, 1, k], start=False, stop=False)
                pe.matmul(sc[c][:, k], QKL[rows, slot, 0, q], QKH[rows, slot, 1, k], start=False, stop=False)
                if bias:
                    pe.matmul(sc[c][:, k], onesr[rows, :], Cm[rows, slot, k], start=False, stop=False)
                pe.matmul(sc[c][:, q], identb[:, :], masks[:, mask, :], start=False, stop=True).then_inc(s_done[c], 1)

            def turn_map(b, used, src, i):
                pe.wait_ge(pn[b], used.n(1))
                pe.wait_ge(pt_l[b], used.n() + OPEN)
                for j in range(i + 1):
                    mm = pe.transpose(tb[b][:, j * P:(j + 1) * P], src[:, j * P:(j + 1) * P], ident[:, :])
                mm.then_inc(t_done[b], 1)

            def attend(e, slot, turn):
                pe.wait_ge(o_read[e], turn.n() + OPEN)
                for j in range(QT):
                    mm = product(ob[e][:, j * P:], VH[:, slot, j * P:(j + 1) * P], VL[:, slot, j * P:(j + 1) * P],
                                 PTH[:, e, j, j * P:], PTL[:, e, j, j * P:], j == 0, j == QT - 1)
                mm.then_inc(o_done[e], 1)

            def weave(steps, slot_work, counts):
                for sl, count in enumerate(counts):
                    slot_work(sl)
                    for _ in range(count):
                        next(steps, None)
                for _ in steps:
                    pass

            def out_steps(name, ready, ks):
                g, u = STAGES[name]
                for k in ks:
                    ready(k)
                    for j in range(2):
                        if k == 0:
                            bank_free(Nth(u + j))
                        step(Nth(g + j), (u + j) % 2, OH, OL, 0, k, DT, True, True)
                        yield

            def fox_slot(u):
                slot = u.slot(2)

                def work_of(sl):
                    if sl == 1:
                        turn_v("qkv1", u)
                    if sl < 8:
                        if sl == 0:
                            pe.wait_ge(cm_ready, u.n(1))
                            pe.wait_ge(bank_read[0], u.times(4, STAGES["qkv1"][1]).round(2, 1))
                            pe.wait_ge(bank_read[1], u.times(4, STAGES["qkv1"][1] + 1).round(2, 1))
                        rows = slice(HEAD * (sl % 2), HEAD * (sl % 2) + HEAD)
                        score(sl, u.times(4, sl // 2), slot, rows, sl // 2, 0, True)
                    if 2 <= sl < 10:
                        n = sl - 2
                        turn_map(n % 2, u.times(4, n // 2), pmap[:, n % 4, :], n // 2)
                    if sl >= 10:
                        e = sl - 10
                        pe.wait_ge(pt_l[e], u.times(4, 4).n() + OPEN)
                        pe.wait_ge(bank_read[1], u.times(4, STAGES["qkv1"][1] + 3).round(2, 1))
                        attend(e, slot, u)
                return work_of

            def fox_part(iu, au):
                if au is None:
                    unit_steps_fed("qkv1", 2)
                elif iu is None:
                    def ready(k):
                        for e in range(2):
                            pe.wait_ge(o_read[e], k + 1 + OPEN)
                    weave(out_steps("out1", ready, range(DT - 1)), fox_slot(au), (0,) * 3 + (2,) * 9)
                    for _ in out_steps("out1", ready, [DT - 1]):
                        pass
                else:
                    weave(unit_steps("qkv1", iu), fox_slot(au), FOX_STEPS)

            pe.wait_ge(consts, CONSTS)
            weave_units(pe.Fori, fox_part)
            stage("out1", 2, x=(OH, OL))
            norm_stats(3)
            stage("gu1", FT // 2, normed(3))
            down("down1", 1)
            norm_stats(4)

            def diff_slot(u):
                slot = u.slot(2)
                first = 4 * UNITS

                def work_of(sl):
                    if sl == 1:
                        turn_v("qkv2", u)
                    if sl == 2 and not (isinstance(u.it, int) and u.base == 0):
                        mean_square(u + -1)
                    if sl < 8:
                        if sl == 0:
                            pe.wait_ge(qk_lo, u.times(2, 2).n() + OPEN)
                        rows = slice(HEAD * (sl % 2), HEAD * (sl % 2) + HEAD)
                        score(sl, u.times(4, first + sl // 2), slot, rows, sl // 2, 1, False)
                    if sl in (3, 5, 7, 9):
                        i = (sl - 3) // 2
                        turn_map(i % 2, u.times(2, first + i // 2), pmap[:, 2 * (i % 2), :], i)
                    if sl == 11:
                        for b in range(2):
                            pe.wait_ge(pt_l[b], u.times(2, first + 2).n() + OPEN)
                        pe.wait_ge(bank_read[1], u.times(4, STAGES["qkv2"][1] + 3).round(2, 1))
                        attend(0, slot, u + UNITS)
                return work_of

            def mean_square(u):
                pe.wait_ge(sub_sq, u.n(1))
                pe.matmul(ob[1][:, :], ones[:, :], osq[:, :], start=True, stop=True).then_inc(sub_var, 1)

            def diff_part(iu, au):
                if au is None:
                    unit_steps_fed("qkv2", 4)
                    pe.wait_ge(lam_a, 1)
                    pe.matmul(tb[0][:, 0:1], ones[0:1, :], lam_row[2], start=True, stop=True).then_inc(lam_b, 1)
                    pe.wait_ge(lam_d, 1)
                elif iu is None:
                    def ready(k):
                        pe.wait_ge(sub_lo, k + 1 + OPEN)
                    weave(out_steps("out2", ready, range(DT - 1)), diff_slot(au), (0,) * 5 + (2,) * 7)
                    mean_square(au)
                    for _ in out_steps("out2", ready, [DT - 1]):
                        pass
                else:
                    weave(unit_steps("qkv2", iu), diff_slot(au), DIFF_STEPS)

            weave_units(pe.Fori, diff_part)
            stage("out2", 2, x=(OH, OL))
            norm_stats(5)
            stage("gu2", FT // 2, normed(5))
            down("down2", 2)
            norm_stats(6)
            for n in range(2 * QT):
                half, q = n // QT, n % QT
                pe.wait_ge(x_hi, DT * 6 + QT * (half + 1))
                for k in range(4):
                    mm = pe.transpose(y_bank[n][:, k * P:(k + 1) * P], xres[:, 4 * half + k, q * P:(q + 1) * P], ident[:, :])
                mm.then_inc(y_turned, 1)

        @block.scalar
        def _(act):
            own = Chain(act, av)

            def high(g, kt=DT):
                act.wait_ge(w_landed[g.slot(RAW)], g.round(RAW, 1) * 16)
                if not (isinstance(g.it, int) and g.base < SPLIT):
                    act.wait_ge(item_done, g.n(1 - SPLIT))
                for ks in halves(kt):
                    act.activation(WH[:, g.slot(SPLIT), ks, :], raw[:, g.slot(RAW), ks, :], ACT.Copy).then_inc(w_hi, 1)

            def warm(func):
                act.activation(small[:, 90:91], small[:, 46:47], func)

            def root(n):
                if n >= 2:
                    act.wait_ge(bank_read[1], (LAST_TURN[n] + 1) // 2)
                    act.activation(tmp[1], xres[:, DT - 1, :], ACT.Square).then_inc(last_squared, 1)
                act.wait_ge(var_ready, n + 1)
                act.activation(rstd, var, ACT.Sqrt).then_inc(rstd_ready, 1)

            def norm_rms(m, src):
                root(NORM[m])
                for t in range(DT):
                    act.wait_ge(xn_ready, DT * m + t + 1)
                    act.activation(XH[:, t, :], src(t), ACT.Copy).then_inc(x_hi, 1)

            def norm_ln(m, g, b, split=True):
                root(NORM[m])
                for t in range(DT):
                    act.wait_ge(xn_ready, DT * m + t + 1)
                    if split:
                        act.activation(XH[:, t, :], ring[t % 4], ACT.Identity, bias=b(t), scale=g(t))
                    act.activation(xres[:, t, :], ring[t % 4], ACT.Identity, bias=b(t), scale=g(t)).then_inc(x_hi, 1)

            def highs(name, times, per):
                with act.Fori(0, times) as it:
                    for j, kt in enumerate(loop_with_sizes(name, per)):
                        high(Nth(STAGES[name][0] + j + 2, it, per), kt)

            for t in range(DT):
                act.wait_ge(bank_read[t % 2], t // 2 + 1)
                if t >= 2:
                    act.wait_ge(sum_tiles, t - 1)
                act.activation(tmp[t % 2], xres[:, t, :], ACT.Square).then_inc(squared, 1)
                if t in (2, 5):
                    high(Nth(t // 4))
            warm(ACT.Sqrt)
            norm_rms(0, lambda t: ring[t % 4])
            act.wait_ge(par_ok, 1)
            gates = 0
            for n, (kind, c) in enumerate(IN_ORDER):
                high(Nth(n + 2))
                u = Nth(STAGES["in"][1] + n)
                if kind == "gate":
                    act.wait_ge(item_done, n + 1)
                    if gates >= 2:
                        used = [i for i, x in enumerate(IN_ORDER) if x[0] == "value"][gates - 2]
                        act.wait_ge(bank_read[1], (DT + used) // 2 + 1)
                    act.activation(sig[:, gates % 2, :], bank[0][:, :], ACT.Sigmoid, bias=pcol("b_in", CT + c)).then_inc(bank_read[0], 1)
                    gates += 1
                elif kind == "pool":
                    act.wait_ge(item_done, n + 1)
                    act.wait_ge(consts, CONSTS)
                    act.activation(ppad[:, c, PAD:], bank[u.slot(2)][:, :], ACT.Identity,
                                   bias=pcol("b_in", 2 * CT + c)).then_inc(bank_read[u.slot(2)], 1)
                if 3 <= n < 7:
                    act.wait_ge(taps_split, 2)
                    for j in range((n - 3) * DIAG_CHUNK, min((n - 2) * DIAG_CHUNK, TAPS)):
                        act.activation(dg_h[:, j, :], ident[:, :], ACT.Copy,
                                       scale=tap_h[:, j:j + 1].bitcast(F32)).then_inc(diag_h, 1)
                if n == 10:
                    act.wait_ge(bank_read[1], (DT + in_item("value", PE_TILE)) // 2 + 1)
                    act.activation(u_h[:, :], upad[:, PE_TILE, :], ACT.Copy).then_inc(u_hi, 1)
            act.wait_ge(pe_conv, 1)
            act.activation(vconv[:, PE_TILE, :], ob[0][:, :], ACT.Identity, bias=pcol("b_dw", PE_TILE)).then_inc(pe_conv_out, 1)
            for i in range(CT):
                act.wait_ge(pool_mm, i + 1)
                if i >= 2:
                    act.wait_ge(pool_lo, i - 1)
                act.activation(mixp[:, i % 2, :], tb[i % 2][:, :], ACT.Copy, scale=pcol("s_pool", i)).then_inc(pool_out, 1)
                act.wait_ge(pool_out, i + 1)
                act.activation(XH[:, CT + i, :], mixp[:, i % 2, :], ACT.Copy).then_inc(pool_hi, 1)
            warm(ACT.Sqrt)
            root(NORMS.index("conv"))
            for c in range(CT):
                act.wait_ge(cv_n, 2 + c)
                own.link(act.activation(vconv[:, c, :], vconv[:, c, :], ACT.Silu, bias=pcol("ln_b", c), scale=pcol("ln_g", c)))
                act.activation(XH[:, c, :], vconv[:, c, :], ACT.Copy).then_inc(cv_hi, 1)
            highs("out", 2, 4)
            norm_rms(1, lambda t: ring[t % 4])

            def hidden_hi(it, j, name):
                act.wait_ge(bank_read[1], Nth(STAGES[name][1] + 2 * j + 1, it, 4).round(2, 1))
                act.activation(HH[:, bass.ds(it * 2 + j, 1), :], hid[:, j:j + 1, :], ACT.Copy).then_inc(h_hi, 1)

            warm(ACT.Silu)
            with act.Fori(0, FT // 2) as it:
                for j in range(2):
                    g = Nth(STAGES["gu0"][0] + 2 * j, it, 4)
                    high(g + 2)
                    act.wait_ge(item_done, g.n(1))
                    act.wait_ge(bank_read[1], Nth(STAGES["gu0"][1] + 2 * j + 1, it, 4).round(2, -1))
                    act.activation(act_g[:, j, :], bank[0][:, :], ACT.Silu).then_inc(bank_read[0], 1)
                    high(g + 3)
                    hidden_hi(it, j, "gu0")
            highs("down0", DT // 2, 8)
            act.wait_ge(item_done, STAGES["qkv1"][0])
            act.dma_start(wf[:, :, :], a_in[:, :, 3 * D:3 * D + FOX_HEADS]).then_inc(wf_in, 16)
            act.dma_start(small[0:FOX_HEADS, 48:49], A["a_b_f_2"].rearrange("o h -> h o")).then_inc(wf_in, 16)
            norm_rms(2, lambda t: xres[:, t, :])
            act.wait_ge(gate_a, 1)
            act.activation(tmp[1][0:FOX_HEADS, :], tmp[1][0:FOX_HEADS, :], ACT.Exp).then_inc(gate_b, 1)
            act.wait_ge(gate_b, 1)
            act.activation(tmp[1][0:FOX_HEADS, :], tmp[1][0:FOX_HEADS, :], ACT.Ln, bias=1.0).then_inc(gate_b, 1)

            def exps(n, used):
                c, k = n % 2, (n // 2 + 1) * P
                act.wait_ge(mx[c], used.n(1))
                act.activation(pmap[:, n % 4, 0:k], sc[c][:, 0:k], ACT.Exp, bias=small[:, n % 4:n % 4 + 1],
                               accum_out=small[:, 4 + n % 4:5 + n % 4]).then_inc(ex[c], 1)

            def map_hi(b, used, head, i):
                act.wait_ge(t_done[b], used.n(1))
                act.activation(PTH[:, head, 0:i + 1, i * P:(i + 1) * P],
                               tb[b][:, 0:(i + 1) * P].rearrange("p (j q) -> p j q", q=P), ACT.Copy).then_inc(pt_h[b], 1)

            def value_hi(layer, u):
                act.wait_ge(v_turned, u.n(layer * UNITS + 1))
                act.activation(VH[:, u.slot(2), :], bank[1][:, :], ACT.Copy).then_inc(v_hi, 1)

            def value_out(name, iu):
                act.wait_ge(item_done, iu.times(4, STAGES[name][0] + 4).n())
                act.activation(vt[:, :], bank[0][:, :], ACT.Copy).then_inc(bank_read[0], 1)

            def unit_high(name, iu, j):
                high(iu.times(4, STAGES[name][0] + j + 2), (UNIT[2:] + UNIT[:2])[j])

            SLOT_OF_ITEM = (4, 8, 10, 12)

            def fox_part(iu, au):
                for sl in range(13):
                    if au is not None:
                        if sl == 2:
                            value_hi(0, au)
                        if sl < 8:
                            exps(sl, au.times(4, sl // 2))
                        if 2 <= sl < 10:
                            n = sl - 2
                            map_hi(n % 2, au.times(4, n // 2), n % 2, n // 2)
                        if sl >= 11:
                            e = sl - 11
                            r = slice(HEAD * e, HEAD * e + HEAD)
                            act.wait_ge(o_done[e], au.n(1))
                            act.activation(OH[r, at(au), :], ob[e][r, :].rearrange("p (a s) -> p a s", a=1), ACT.Copy).then_inc(o_hi, 1)
                    if iu is not None and sl in SLOT_OF_ITEM:
                        j = SLOT_OF_ITEM.index(sl)
                        if j < 2:
                            act.wait_ge(item_done, iu.times(4, STAGES["qkv1"][0] + j + 1).n())
                            act.activation(QKH[:, iu.slot(2), j, :], bank[j][:, :], ACT.Copy,
                                           scale=1.0 if j else HEAD ** -0.5).then_inc(qk_hi, 1)
                        if j == 3:
                            value_out("qkv1", iu)
                        unit_high("qkv1", iu, j)

            weave_units(act.Fori, fox_part)
            highs("out1", 2, 4)
            warm(ACT.Sqrt)
            norm_ln(3, lambda t: pcol("ln_attn_g_2", t), lambda t: pcol("ln_attn_b_2", t))

            def conv_hidden(name, layer):
                warm(ACT.Silu)
                with act.Fori(0, FT // 2) as it:
                    for j in range(2):
                        g = Nth(STAGES[name][0] + 2 * j, it, 4)
                        for side, dst in ((0, act_g), (1, hid)):
                            act.wait_ge(item_done, g.n(1 + side))
                            if side == 0:
                                act.wait_ge(hid_ready[j], Nth(FT * (layer - 1) + j, it, 2).round(2) + OPEN)
                            else:
                                act.wait_ge(h_lo[j], Nth(FT * layer + j, it, 2).round(2) + OPEN)
                            n = it * 2 + (j + FT * side)
                            act.activation(dst[:, j, :], bank[side][:, :], ACT.Identity, bias=ff_par(layer - 1, 3, n),
                                           scale=ff_par(layer - 1, 2, n)).then_inc(ff_lin[side], 1)
                            high(g + side + 2)
                        act.wait_ge(bank_read[0], Nth(STAGES[name][1] + 2 * j, it, 4).round(2, 1))
                        act.activation(act_g[:, j, :], act_g[:, j, :], ACT.Silu).then_inc(g_act, 1)
                        act.wait_ge(hid_ready[j], Nth(FT * (layer - 1) + j, it, 2).round(2, 1) + OPEN)
                        act.activation(HH[:, bass.ds(it * 2 + j, 1), :], hid[:, j:j + 1, :], ACT.Copy).then_inc(h_hi, 1)

            conv_hidden("gu1", 1)
            highs("down1", DT // 2, 8)
            warm(ACT.Sqrt)
            act.wait_ge(item_done, STAGES["qkv2"][0])
            act.dma_start(rope[:, :, :], A["rope"].rearrange("a p s -> p a s")).then_inc(rope_in, 16)
            act.dma_start(lamr[:, :], A["b_lambda_2"].rearrange("o a d -> o (a d)")).then_inc(rope_in, 16)
            norm_ln(4, lambda t: pcol("ln_ffn_g_2", t), lambda t: pcol("ln_ffn_b_2", t))
            def sub_root(u):
                act.wait_ge(sub_var, u.n(1))
                act.activation(osq[:, :], ob[1][:, :], ACT.Ln, bias=small[:, 46:47], scale=1.0 / P).then_inc(sub_ln, 1)
                act.wait_ge(sub_ln, u.n(1))
                act.activation(osq[:, :], osq[:, :], ACT.Exp, scale=-0.5).then_inc(sub_rs, 1)

            def sub_high(u):
                act.wait_ge(sub_n, u.n(1))
                act.activation(OH[:, at(u), :], osb[:, :].rearrange("p (a s) -> p a s", a=1), ACT.Copy).then_inc(sub_hi, 1)

            def diff_part(iu, au):
                first = 4 * UNITS
                before = None if au is None or (isinstance(au.it, int) and au.base == 0) else au + -1
                for sl in range(13):
                    if au is not None:
                        if sl == 2:
                            value_hi(1, au)
                        if sl < 8:
                            exps(sl, au.times(4, first + sl // 2))
                        if sl == 3 and before is not None:
                            sub_root(before)
                        if sl == 5 and before is not None:
                            sub_high(before)
                        if sl in (3, 5, 7, 9):
                            i = (sl - 3) // 2
                            map_hi(i % 2, au.times(2, first + i // 2), 0, i)
                        if sl == 12:
                            act.wait_ge(o_done[0], au.n(UNITS + 1))
                            act.wait_ge(sub_lo, au.n() + OPEN)
                            act.activation(osb[:, :], ob[0][:, :], ACT.Copy).then_inc(o_read[0], 1)
                            if iu is not None:
                                value_out("qkv2", iu)
                            act.wait_ge(o_read[0], au.n(UNITS + 1) + OPEN)
                            act.activation(osq[:, :], osb[:, :], ACT.Square).then_inc(sub_sq, 1)
                    if iu is not None:
                        if sl in (7, 11):
                            j = (sl - 7) // 4
                            act.wait_ge(roped, iu.times(2, j + 1).n())
                            act.activation(QKH[:, iu.slot(2), j, :], qk[:, :], ACT.Copy).then_inc(qk_hi, 1)
                        if sl == 12 and au is None:
                            value_out("qkv2", iu)
                        if sl in (4, 8):
                            j = sl // 4 - 1
                            act.wait_ge(item_done, iu.times(4, STAGES["qkv2"][0] + j + 1).n())
                            for r in range(4):
                                o = r + 1 - 2 * (r % 2)
                                act.activation(rot[32 * r:32 * r + 32, :], bank[j][32 * o:32 * o + 32, :], ACT.Copy).then_inc(rot_ready, 1)
                        if sl in SLOT_OF_ITEM:
                            unit_high("qkv2", iu, SLOT_OF_ITEM.index(sl))
                if au is None:
                    act.wait_ge(lam_c, 1)
                    act.activation(lam_row[1], lam_row[0], ACT.Exp).then_inc(lam_c, 1)

            act.add_instruction(mybir.InstLoadActFuncSet(name=nc.get_next_instruction_name(), act_func_set_id=LN_EXP_SET,
                                                         engine=mybir.EngineType.Activation, ins=[], outs=[]))
            weave_units(act.Fori, diff_part)
            sub_root(Nth(UNITS - 1))
            sub_high(Nth(UNITS - 1))
            highs("out2", 2, 4)
            warm(ACT.Sqrt)
            norm_ln(5, lambda t: pcol("ln_attn_g_2", DT + t), lambda t: pcol("ln_attn_b_2", DT + t))
            conv_hidden("gu2", 2)
            highs("down2", DT // 2 - 1, 8)
            for j, kt in enumerate(loop_with_sizes("down2", 8)[:6]):
                high(Nth(STAGES["down2"][0] + 8 * (DT // 2 - 1) + j + 2), kt)
            warm(ACT.Sqrt)
            norm_ln(6, lambda t: pcol("ln_ffn_g_2", DT + t), lambda t: pcol("ln_ffn_b_2", DT + t), split=False)
            for n in range(0, 2 * QT, 2):
                act.wait_ge(y_turned, n + 1)
                act.activation(yout[:, n, :], y_bank[n][:, :], ACT.Copy).then_inc(y_copied[0], 1)

        @block.vector
        def _(dve):
            own = Chain(dve, dv)

            def add_squares(x, count):
                own.link(dve.tensor_tensor(tmp[0], x, x, ALU.mult))
                dve.tensor_tensor(ssq, ssq, tmp[0], ALU.add).then_inc(*count)

            def clear_sums():
                own.did(dve.memset(ssum, 0.0))
                own.link(dve.memset(ssq, 0.0))

            own.did(dve.memset(small[:, 46:47], SUB_EPS))
            clear_sums()
            for t in range(DT + 1):
                if t < DT:
                    dve.wait_ge(turned_x, t + 1)
                    dve.tensor_copy(xres[:, t, :], bank[t % 2][:, :]).then_inc(bank_read[t % 2], 1)
                if t:
                    dve.wait_ge(squared, t)
                    if t > 1:
                        dve.wait_ge(sum_tiles, t - 1)
                    dve.tensor_tensor(ssq, ssq, tmp[(t - 1) % 2], ALU.add).then_inc(sum_tiles, 1)

            def rows_out(i):
                n = ROWS_OF[i]
                own.did(dve.tensor_copy(par[:, i * P:i * P + n], turned_rows(i)))

            dve.wait_ge(bank_read[0], DT // 2)
            dve.wait_ge(bank_read[1], DT // 2)
            dve.wait_ge(turned_par, 1)
            rows_out(0)
            own.sync()
            def moments(n, width, eps):
                centred = n in CENTRED
                dve.wait_ge(stats_done, n + 1)
                if centred:
                    own.link(dve.tensor_scalar(mean, sc[0][:, QT:2 * QT], 1.0 / width, None, ALU.mult))
                    own.link(dve.tensor_tensor(square, mean, mean, ALU.mult))
                    own.link(dve.scalar_tensor_tensor(out=var, in0=sc[0][:, 0:QT], scalar=1.0 / width, in1=square,
                                                      op0=ALU.mult, op1=ALU.subtract))
                    own.link(dve.tensor_scalar(var, var, 0.0, eps, ALU.max, ALU.add))
                else:
                    own.link(dve.tensor_scalar(var, sc[0][:, 0:QT], 1.0 / width, eps, ALU.mult, ALU.add))
                dve.reciprocal(var, var).then_inc(var_ready, 1)
                dve.wait_ge(rstd_ready, n + 1)

                if centred:
                    dve.tensor_tensor(mean, mean, rstd, ALU.mult).then_inc(shift_ready, 1)
                dve.wait_ge(rstd_wide, n + 1)

            def centre(n, t, x, dst):
                own.link(dve.tensor_tensor(dst, x, sc[0][:, :], ALU.mult))
                if t == 0:
                    dve.wait_ge(mean_wide, CENTRED.index(n) + 1)
                return dve.tensor_tensor(dst, dst, sc[1][:, :], ALU.subtract)

            def norm(m, scale, centred, in_place):
                moments(NORM[m], D, LN_EPS if centred else RMS_EPS)
                for t in range(DT):
                    if t >= 4 and not in_place:
                        if centred:
                            dve.wait_ge(x_hi, DT * m + t - 3)
                        else:
                            dve.wait_ge(x_lo, DT * m + t - 3)
                    if centred:
                        centre(NORM[m], t, xres[:, t, :], ring[t % 4]).then_inc(xn_ready, 1)
                    else:
                        dst = xres[:, t, :] if in_place else ring[t % 4]
                        dve.scalar_tensor_tensor(out=dst, in0=xres[:, t, :], scalar=pcol(scale, t), in1=sc[0][:, :],
                                                 op0=ALU.mult, op1=ALU.mult).then_inc(xn_ready, 1)
                clear_sums()

            def counted(per):
                return lambda first, times: own.loop(times, per)

            norm(0, "g_mix", False, False)
            dve.wait_ge(turned_par, 2)
            for i in range(1, len(ROWS_OF)):
                rows_out(i)
            own.sync()
            dve.tensor_scalar(small[:, 47:48], pcol("b_subln_g_2", 0), 1.0 - LAMBDA_INIT, None, ALU.mult).then_inc(par_ok, 1)
            own.link(dve.tensor_copy(tap_h[:, :], par[:, P + PE_TILE:P + PE_TILE + TAPS * CT:CT]))
            dve.tensor_tensor(tap_l[:, :], par[:, P + PE_TILE:P + PE_TILE + TAPS * CT:CT], tap_h[:, :].bitcast(F32),
                              ALU.subtract).then_inc(taps_split, 2)
            dve.wait_ge(consts, CONSTS)
            dve.reciprocal(icnt[:, :], cnts[:, :]).then_inc(cv_n, 1)

            def gated(c):
                n = in_item("value", c)
                k = [x[1] for x in IN_ORDER if x[0] == "gate"].index(c)
                dve.wait_ge(item_done, n + 1)
                dve.wait_ge(bank_read[0], (DT + n - 1) // 2 + 1)
                dve.scalar_tensor_tensor(out=upad[:, c, TAPS - 1:], in0=bank[1][:, :], scalar=pcol("b_in", c),
                                         in1=sig[:, k % 2, :], op0=ALU.add, op1=ALU.mult).then_inc(bank_read[1], 1)
                dve.wait_ge(bank_read[1], (DT + n) // 2 + 1)

            def taps(c, a, b):
                for j in range(a, b):
                    part = odd_taps if j % 2 else vconv[:, c, :]
                    if j == 0:
                        ins = dve.tensor_scalar(part, upad[:, c, 0:S], tap(0, c), pcol("b_dw", c), ALU.mult, ALU.add)
                    elif j == 1:
                        ins = dve.tensor_scalar(part, upad[:, c, 1:1 + S], tap(1, c), None, ALU.mult)
                    else:
                        ins = dve.scalar_tensor_tensor(out=part, in0=upad[:, c, j:j + S], scalar=tap(j, c),
                                                       in1=part, op0=ALU.mult, op1=ALU.add)
                    own.did(ins)
                    if j:
                        own.sync(but=1)
                if b == TAPS:
                    own.sync()
                    own.link(dve.tensor_tensor(vconv[:, c, :], vconv[:, c, :], odd_taps, ALU.add))

            def add_conv(c, k):
                if k:
                    dve.wait_ge(cv_sum, k)
                add = dve.tensor_tensor(ssum, ssum, vconv[:, c, :], ALU.add)
                if k == CT - 1:
                    add.then_inc(plain_sums, 1)
                else:
                    own.did(add)
                add_squares(vconv[:, c, :], (cv_sum, 1))

            gated(0)
            taps(0, 0, 29)
            gated(1)
            taps(0, 29, TAPS)
            add_conv(0, 0)
            taps(1, 0, 8)
            gated(PE_TILE)
            taps(1, 8, 22)
            gated(2)
            taps(1, 22, TAPS)
            add_conv(1, 1)
            taps(2, 0, TAPS)
            add_conv(2, 2)
            dve.wait_ge(pe_conv_out, 1)
            add_conv(PE_TILE, 3)
            moments(NORMS.index("conv"), C_CONV, LN_EPS)
            for c in range(CT):
                centre(NORMS.index("conv"), c, vconv[:, c, :], vconv[:, c, :]).then_inc(cv_n, 1)
            clear_sums()

            def residual(name, m, items_of_tile, factor, centred):
                def tile(it, j, final=False):
                    last = Nth(STAGES[name][0] + (j + 1) * items_of_tile - 1, it, 2 * items_of_tile)
                    u = Nth(STAGES[name][1] + j, it, 2)
                    r = xres[:, bass.ds(it * 2 + j, 1), :]
                    dve.wait_ge(item_done, last.n(1))
                    dve.scalar_tensor_tensor(out=r, in0=r, scalar=factor, in1=bank[j][:, :].rearrange("p (a s) -> p a s", a=1),
                                             op0=ALU.mult, op1=ALU.add).then_inc(bank_read[j], 1)
                    dve.wait_ge(bank_read[j], u.round(2, 1))
                    dve.wait_ge(sum_tiles, Nth(DT * m + j, it, 2).n())
                    if final:
                        if centred:
                            dve.tensor_tensor(ssum, ssum, xres[:, DT - 1, :], ALU.add).then_inc(plain_sums, 1)
                        dve.wait_ge(last_squared, m)
                        dve.tensor_tensor(ssq, ssq, tmp[1], ALU.add).then_inc(sum_tiles, 1)
                        return
                    if centred:
                        own.did(dve.tensor_tensor(work[:, 2:3, :], work[:, 2:3, :], r, ALU.add))
                    own.link(dve.tensor_tensor(work[:, 0:1, :], r, r, ALU.mult))
                    dve.tensor_tensor(ssq, ssq, tmp[0], ALU.add).then_inc(sum_tiles, 1)

                with own.loop(DT // 2 - 1, (2 if centred else 1) * 2) as it:
                    for j in range(2):
                        tile(it, j)
                tile(DT // 2 - 1, 0)
                tile(DT // 2 - 1, 1, True)

            residual("out", 1, 1, 1.0, False)
            norm(1, "g_ffn", False, False)
            with dve.Fori(0, FT // 2) as it:
                for j in range(2):
                    g, u = Nth(STAGES["gu0"][0] + 2 * j + 1, it, 4), Nth(STAGES["gu0"][1] + 2 * j, it, 4)
                    dve.wait_ge(item_done, g.n(1))
                    dve.wait_ge(bank_read[0], u.round(2, 1))
                    dve.wait_ge(h_lo[j], Nth(j, it, 2).round(2) + OPEN)
                    dve.tensor_tensor(hid[:, j, :], bank[1][:, :], act_g[:, j, :], ALU.mult).then_inc(bank_read[1], 1)
            residual("down0", 2, len(DOWN), 1.0, False)
            norm(2, "g_final", False, True)
            dve.wait_ge(gate_done, 1)
            z, e = tmp[0][0:FOX_HEADS, :], tmp[1][0:FOX_HEADS, :]
            own.link(dve.tensor_scalar(z, ob[0][0:FOX_HEADS, :], small[0:FOX_HEADS, 48:49], None, ALU.add))
            dve.scalar_tensor_tensor(out=e, in0=z, scalar=-1.0, in1=z, op0=ALU.mult, op1=ALU.min).then_inc(gate_a, 1)
            own.link(dve.tensor_scalar(z, z, 0.0, None, ALU.min))
            dve.wait_ge(gate_b, 2)
            own.link(dve.tensor_tensor(e, e, z, ALU.subtract))
            own.link(dve.memset(osq[0:FOX_HEADS, :], 1.0))
            own.link(dve.tensor_tensor_scan(z, osq[0:FOX_HEADS, :], e, 0.0, ALU.mult, ALU.add))
            dve.wait_ge(cc_zero, 1)
            for e in range(2):
                h, col = slice(64 * e, 64 * e + 64), 65 * e
                own.did(dve.tensor_tensor(hot[h, :], ident[h, col:col + FOX_HEADS:2],
                                          ident[h, col + 32:col + 32 + FOX_HEADS:2], ALU.add))
            high_c = PTH[0:FOX_HEADS, 0, 0, :]
            own.link(dve.tensor_copy(high_c, z))
            for r in range(0, P, 64):
                dve.tensor_copy(CC[r:r + FOX_HEADS, :], high_c.bitcast(F32)).then_inc(cc_ready, 1)
                dve.tensor_tensor(CC[r + 32:r + 32 + FOX_HEADS, :], z, high_c.bitcast(F32), ALU.subtract).then_inc(cc_ready, 1)
            dve.tensor_copy(onesr[:, :], ones[:, :]).then_inc(cc_ready, 1)
            dve.wait_ge(cc_ready, 5)

            def row_max(n, used):
                c = n % 2
                dve.wait_ge(s_done[c], used.n(1))
                dve.tensor_reduce(small[:, n % 4:n % 4 + 1], sc[c][:, 0:(n // 2 + 1) * P], AX_X, ALU.max, negate=True).then_inc(mx[c], 1)

            def map_lo(b, used, head, i):
                dve.wait_ge(pt_h[b], used.n(1))
                dve.tensor_tensor(PTL[:, head, 0:i + 1, i * P:(i + 1) * P],
                                  tb[b][:, 0:(i + 1) * P].rearrange("p (j q) -> p j q", q=P),
                                  PTH[:, head, 0:i + 1, i * P:(i + 1) * P].bitcast(F32), ALU.subtract).then_inc(pt_l[b], 1)

            def value_lo(layer, u):
                dve.wait_ge(v_hi, u.n(layer * UNITS + 1))
                dve.tensor_tensor(VL[:, u.slot(2), :], bank[1][:, :], VH[:, u.slot(2), :].bitcast(F32), ALU.subtract).then_inc(bank_read[1], 1)

            def bias_rows(u):
                dve.tensor_scalar(Cm[:, u.slot(2), :], CC[:, :], hot[:, at(u)], None, ALU.mult).then_inc(cm_ready, 1)

            def fox_part(iu, au):
                if au is None:
                    bias_rows(iu)
                for sl in range(13):
                    if au is not None:
                        if sl == 2:
                            value_lo(0, au)
                        if sl < 8:
                            row_max(sl, au.times(4, sl // 2))
                        if 1 <= sl < 9:
                            n = sl - 1
                            m = n % 4
                            dve.wait_ge(ex[n % 2], au.times(4, n // 2).n(1) + OPEN)
                            own.link(dve.reciprocal(small[:, 8 + m:9 + m], small[:, 4 + m:5 + m]))
                            k = (n // 2 + 1) * P
                            dve.tensor_scalar(pmap[:, m, 0:k], pmap[:, m, 0:k], small[:, 8 + m:9 + m], None, ALU.mult).then_inc(pn[n % 2], 1)
                        if 2 <= sl < 10:
                            n = sl - 2
                            map_lo(n % 2, au.times(4, n // 2), n % 2, n // 2)
                        if sl >= 11:
                            e = sl - 11
                            r = slice(HEAD * e, HEAD * e + HEAD)
                            dve.wait_ge(o_hi, au.times(2, e).n(1))
                            dve.tensor_tensor(OL[r, at(au), :], ob[e][r, :].rearrange("p (a s) -> p a s", a=1),
                                              OH[r, at(au), :].bitcast(F32), ALU.subtract).then_inc(o_read[e], 1)
                        if sl == 6 and iu is not None:
                            bias_rows(iu)
                    if iu is not None and sl in (4, 8):
                        j = sl // 4 - 1
                        dve.wait_ge(qk_hi, iu.times(2, j).n(1))
                        dve.scalar_tensor_tensor(out=QKL[:, iu.slot(2), j, :], in0=bank[j][:, :], scalar=1.0 if j else HEAD ** -0.5,
                                                 in1=QKH[:, iu.slot(2), j, :].bitcast(F32), op0=ALU.mult,
                                                 op1=ALU.subtract).then_inc(bank_read[j], 1)

            dve.wait_ge(cc_ready, 5)
            weave_units(counted(16), fox_part)
            clear_sums()
            residual("out1", 3, 1, ALPHA, True)
            norm(3, None, True, False)

            def conv_hidden(name, layer):
                with own.loop(FT // 2, 4) as it:
                    for j in range(2):
                        for side, dst in ((0, act_g), (1, hid)):
                            n = it * 2 + (j + FT * side)
                            h = Nth(FT * (layer - 1) + j, it, 2)
                            dve.wait_ge(ff_lin[side], h.n(1))
                            own.link(dve.scalar_tensor_tensor(
                                out=dst[:, j, 1:], in0=bank[side][:, 0:S - 1], scalar=ff_par(layer - 1, 1, n),
                                in1=dst[:, j, 1:], op0=ALU.mult, op1=ALU.add))
                            dve.scalar_tensor_tensor(
                                out=dst[:, j, 2:], in0=bank[side][:, 0:S - 2], scalar=ff_par(layer - 1, 0, n),
                                in1=dst[:, j, 2:], op0=ALU.mult, op1=ALU.add).then_inc(bank_read[side], 1)
                        dve.wait_ge(bank_read[1], Nth(STAGES[name][1] + 2 * j + 1, it, 4).round(2, 1))
                        dve.wait_ge(g_act, h.n(1))
                        dve.tensor_tensor(hid[:, j, :], hid[:, j, :], act_g[:, j, :], ALU.mult).then_inc(hid_ready[j], 1)

            conv_hidden("gu1", 1)
            residual("down1", 4, len(DOWN), ALPHA, True)
            norm(4, None, True, False)
            dve.wait_ge(rope_in, 32)

            def make_lambda():
                for k in range(2):
                    own.link(dve.tensor_tensor(lamr[:, 2 * k * HEAD:(2 * k + 1) * HEAD], lamr[:, 2 * k * HEAD:(2 * k + 1) * HEAD],
                                               lamr[:, (2 * k + 1) * HEAD:(2 * k + 2) * HEAD], ALU.mult))
                    ins = dve.tensor_reduce(lam_row[0][:, k:k + 1], lamr[:, 2 * k * HEAD:(2 * k + 1) * HEAD], AX_X, ALU.add)
                    if k == 0:
                        own.link(ins)
                    else:
                        ins.then_inc(lam_c, 1)
                dve.wait_ge(lam_c, 2)
                own.link(dve.tensor_tensor(lam_row[2], lam_row[1][:, 0:1], lam_row[1][:, 1:2], ALU.subtract))
                dve.tensor_scalar(lam_row[2], lam_row[2], LAMBDA_INIT, None, ALU.add).then_inc(lam_a, 1)
                dve.wait_ge(lam_b, 1)
                dve.tensor_copy(small[:, 49:50], tb[0][:, 0:1]).then_inc(lam_d, 1)
                dve.wait_ge(lam_d, 1)

            def head_scaled(u):
                dve.wait_ge(sub_rs, u.n(1))
                dve.scalar_tensor_tensor(out=osb[:, :], in0=osb[:, :], scalar=small[:, 47:48], in1=osq[:, :],
                                         op0=ALU.mult, op1=ALU.mult).then_inc(sub_n, 1)

            def diff_part(iu, au):
                first = 4 * UNITS
                for sl in range(13):
                    if au is not None:
                        if sl == 2:
                            value_lo(1, au)
                        if sl < 8:
                            row_max(sl, au.times(4, first + sl // 2))
                        if sl == 4 and not (isinstance(au.it, int) and au.base == 0):
                            head_scaled(au + -1)
                        if sl in (2, 4, 6, 8):
                            i = sl // 2 - 1
                            k, m = (i + 1) * P, 2 * (i % 2)
                            for c in range(2):
                                dve.wait_ge(ex[c], au.times(4, first + i).n(1) + OPEN)
                                own.did(dve.reciprocal(small[:, 8 + m + c:9 + m + c], small[:, 4 + m + c:5 + m + c]))
                            own.sync()
                            own.link(dve.tensor_tensor(small[:, 9 + m:10 + m], small[:, 9 + m:10 + m], small[:, 49:50], ALU.mult))
                            own.link(dve.tensor_scalar(pmap[:, m + 1, 0:k], pmap[:, m + 1, 0:k], small[:, 9 + m:10 + m], None, ALU.mult))
                            dve.scalar_tensor_tensor(out=pmap[:, m, 0:k], in0=pmap[:, m, 0:k], scalar=small[:, 8 + m:9 + m],
                                                     in1=pmap[:, m + 1, 0:k], op0=ALU.mult, op1=ALU.subtract).then_inc(pn[i % 2], 1)
                        if sl in (4, 6, 8, 10):
                            i = sl // 2 - 2
                            map_lo(i % 2, au.times(2, first + i // 2), 0, i)
                    if iu is not None and sl in (5, 9):
                        j = (sl - 5) // 4
                        scale = 1.0 if j else HEAD ** -0.5
                        dve.wait_ge(rot_ready, iu.times(8, 4 * j).n(4))
                        dve.wait_ge(qk_lo, iu.times(2, j).n() + OPEN)
                        dve.scalar_tensor_tensor(out=qk[:, :], in0=bank[j][:, :], scalar=scale, in1=rope[:, 0, :],
                                                 op0=ALU.mult, op1=ALU.mult).then_inc(bank_read[j], 1)
                        own.link(dve.scalar_tensor_tensor(out=rot[:, :], in0=rot[:, :], scalar=scale, in1=rope[:, 1, :],
                                                          op0=ALU.mult, op1=ALU.mult))
                        dve.wait_ge(bank_read[j], iu.times(4, STAGES["qkv2"][1] + j).round(2, 1))
                        dve.tensor_tensor(qk[:, :], qk[:, :], rot[:, :], ALU.add).then_inc(roped, 1)
                if au is None:
                    make_lambda()

            weave_units(counted(36), diff_part)
            head_scaled(Nth(UNITS - 1))
            dve.wait_ge(sub_n, UNITS)
            dve.wait_ge(sub_lo, UNITS + OPEN)
            clear_sums()
            residual("out2", 5, 1, ALPHA, True)
            norm(5, None, True, False)
            conv_hidden("gu2", 2)
            residual("down2", 6, len(DOWN), ALPHA, True)
            norm(6, None, True, False)
            for n in range(1, 2 * QT, 2):
                dve.wait_ge(y_turned, n + 1)
                dve.tensor_copy(yout[:, n, :], y_bank[n][:, :]).then_inc(y_copied[1], 1)


TAP_LOADS = 1 + 8
CONSTS = 3 + 2 * CT + 2 + PAD + 1 + 3


def rope_tables():
    inv = (1.0 / (np.float32(10000.0) ** (np.arange(0, HEAD, 2, dtype=np.float32) / np.float32(HEAD)))).astype(np.float32)
    ang = (np.arange(S, dtype=np.float32)[None, :] * inv[:, None]).astype(np.float32)
    cos, sin = np.cos(ang).astype(np.float32), np.sin(ang).astype(np.float32)
    return np.stack([np.concatenate([cos, cos, cos, cos]), np.concatenate([-sin, sin, -sin, sin])])


NAMES = ["x", "g_mix", "w_in", "b_in", "w_dw", "b_dw", "ln_g", "ln_b", "w_pool", "s_pool", "w_out", "g_ffn",
         "w_gate", "w_up", "w_down", "g_final", "a_w_in_2", "a_b_f_2", "a_w_out_2", "kv_w_2", "b_w_q_2",
         "b_lambda_2", "b_subln_g_2", "b_w_out_2", "ffn_w_in_2", "ffn_conv_w_2", "ffn_conv_b_2",
         "ffn_w_out_2", "ln_attn_g_2", "ln_attn_b_2", "ln_ffn_g_2", "ln_ffn_b_2"]


def kernel(**inputs):
    import concourse.bacc as bacc
    from concourse.bass_utils import run_bass_kernel_spmd

    nc = bacc.Bacc("TRN2", target_bir_lowering=False, num_devices=1)
    arrays = {name: np.ascontiguousarray(inputs[name]) for name in NAMES}
    arrays["rope"] = rope_tables()
    dram = {name: nc.dram_tensor(f"in_{name}", a.shape, mybir.dt.from_np(a.dtype), kind="ExternalInput").ap()
            for name, a in arrays.items()}
    out = nc.dram_tensor("y", (1, S, D), F32, kind="ExternalOutput").ap()
    two_blocks(nc, dram, out)
    r = run_bass_kernel_spmd(nc, [{f"in_{name}": a for name, a in arrays.items()}], core_ids=[0])
    return r.results[0]["y"]
```
